# Optimizing a Trainium2 kernel written in Bass

```python
import math
import jax, jax.numpy as jnp
from jax import lax
import numpy as np

D_MODEL = 1024
BATCH = 1
SEQ = 1024
DEPTH = 1
DEC_BATCH = 8
DEC_SEQ = 8
PAST_LEN = 8192
PAGE_SIZE = 128

D_MIX = D_MODEL
GLA_WIDTH = D_MIX // 2
RG_WIDTH = D_MIX - GLA_WIDTH
N_GLA_HEADS = 4
GLA_DV = GLA_WIDTH // N_GLA_HEADS
GLA_DK = GLA_DV // 2
GLA_QK = N_GLA_HEADS * GLA_DK
GATE_RANK = 16
GATE_TAU = 16.0
GLA_CHUNK = 64
RG_BLOCKS = 8
RG_BLOCK_W = RG_WIDTH // RG_BLOCKS
RG_C = 8.0
CONV_W = 4
D_FF = -(-8 * D_MODEL // (3 * 256)) * 256
DN_ALPHA = (2.0 * DEPTH) ** 0.25
DN_BETA = (8.0 * DEPTH) ** -0.25
LN_EPS = 1e-5
RMS_EPS = 1e-6
IN_SIZES = (GLA_QK, GLA_QK, GLA_WIDTH, GLA_WIDTH, GATE_RANK, RG_WIDTH, RG_WIDTH)
D_IN = sum(IN_SIZES)
IN_SPLITS = tuple(int(s) for s in np.cumsum(IN_SIZES)[:-1])

kernel_name = "hymba_gla_rglru_deepnorm_step"

def layer_norm(x, g, b):
    xf = x.astype(jnp.float32)
    mu = jnp.mean(xf, axis=-1, keepdims=True)
    var = jnp.mean(jnp.square(xf - mu), axis=-1, keepdims=True)
    return ((xf - mu) * lax.rsqrt(var + LN_EPS) * g.astype(jnp.float32) + b.astype(jnp.float32)).astype(x.dtype)

def gla_chunked(q, k, v, log_a, s0):
    B, T, H, _ = q.shape
    pad = (-T) % GLA_CHUNK
    widths = ((0, 0), (0, pad), (0, 0), (0, 0))
    q, k, v, log_a = [jnp.pad(t.astype(jnp.float32), widths) for t in (q, k, v, log_a)]
    n = (T + pad) // GLA_CHUNK

    def blocks(t):
        return t.reshape(B, n, GLA_CHUNK, H, t.shape[-1]).transpose(1, 0, 3, 2, 4)

    q, k, v, log_a = blocks(q), blocks(k), blocks(v), blocks(log_a)
    b = jnp.cumsum(log_a, axis=3)
    b_last = b[:, :, :, -1:, :]
    q_e = q * jnp.exp(b)
    k_e = k * jnp.exp(-b)
    k_end = k * jnp.exp(b_last - b)
    causal = jnp.tril(jnp.ones((GLA_CHUNK, GLA_CHUNK), dtype=bool))
    scores = jnp.where(causal, jnp.einsum('nbhcd,nbhsd->nbhcs', q_e, k_e), 0.0)
    o_intra = jnp.einsum('nbhcs,nbhsv->nbhcv', scores, v)
    kv = jnp.einsum('nbhsd,nbhsv->nbhdv', k_end, v)
    decay = jnp.exp(b_last[:, :, :, 0, :])

    def step(s, inp):
        dec, upd = inp
        return dec[..., None] * s + upd, s

    s_final, s_start = lax.scan(step, s0.astype(jnp.float32), (decay, kv))
    o = o_intra + jnp.einsum('nbhcd,nbhdv->nbhcv', q_e, s_start)
    o = o.transpose(1, 0, 3, 2, 4).reshape(B, n * GLA_CHUNK, H, GLA_DV)[:, :T]
    return o, s_final

def causal_conv(x, buf, w, b):
    T = x.shape[1]
    xp = jnp.concatenate([buf.astype(x.dtype), x], axis=1)
    y = b
    for j in range(CONV_W):
        y = y + xp[:, j:j + T] * w[j]
    return y, xp[:, -(CONV_W - 1):]

def rg_lru(xc, h0, w_a, b_a, w_x, b_x, lam):
    B, T, _ = xc.shape
    xb = xc.reshape(B, T, RG_BLOCKS, RG_BLOCK_W)
    r = jax.nn.sigmoid(jnp.einsum('btnc,ncd->btnd', xb, w_a).reshape(B, T, RG_WIDTH) + b_a)
    i = jax.nn.sigmoid(jnp.einsum('btnc,ncd->btnd', xb, w_x).reshape(B, T, RG_WIDTH) + b_x)
    log_a = (-RG_C * jax.nn.softplus(-lam) * r).astype(jnp.float32)
    a = jnp.exp(log_a)
    u = jnp.sqrt(jnp.maximum(-jnp.expm1(2.0 * log_a), 0.0)) * (i * xc).astype(jnp.float32)

    def step(h, inp):
        a_t, u_t = inp
        h = a_t * h + u_t
        return h, h

    h_last, hs = lax.scan(step, h0.astype(jnp.float32), (jnp.swapaxes(a, 0, 1), jnp.swapaxes(u, 0, 1)))
    return jnp.swapaxes(hs, 0, 1).astype(xc.dtype), h_last

def mixer(u, s_gla, h_rg, conv_buf, w_in, gla_w_gate, gla_b_gate, gla_norm_g,
          rg_conv_w, rg_conv_b, rg_w_a, rg_b_a, rg_w_x, rg_b_x, rg_lambda, w_out):
    B, T, _ = u.shape
    proj = u @ w_in
    q, k, v, g_gla, z_lr, x_rg, g_rg = jnp.split(proj, IN_SPLITS, axis=-1)
    q = q.reshape(B, T, N_GLA_HEADS, GLA_DK) * (GLA_DK ** -0.5)
    k = k.reshape(B, T, N_GLA_HEADS, GLA_DK)
    v = v.reshape(B, T, N_GLA_HEADS, GLA_DV)
    log_a = jax.nn.log_sigmoid((z_lr @ gla_w_gate + gla_b_gate).astype(jnp.float32)) / GATE_TAU
    log_a = log_a.reshape(B, T, N_GLA_HEADS, GLA_DK)
    o, s_new = gla_chunked(q, k, v, log_a, s_gla)
    o = o * lax.rsqrt(jnp.mean(jnp.square(o), axis=-1, keepdims=True) + RMS_EPS) * gla_norm_g.astype(jnp.float32)
    y_gla = o.reshape(B, T, GLA_WIDTH).astype(u.dtype) * jax.nn.silu(g_gla)
    xc, buf_new = causal_conv(x_rg, conv_buf, rg_conv_w, rg_conv_b)
    hs, h_new = rg_lru(xc, h_rg, rg_w_a, rg_b_a, rg_w_x, rg_b_x, rg_lambda)
    y_rg = hs * jax.nn.gelu(g_rg)
    y = jnp.concatenate([y_gla, y_rg], axis=-1) @ w_out
    return y, s_new, h_new, buf_new

def swiglu(u, w_gate, w_up, w_down):
    return (jax.nn.silu(u @ w_gate) * (u @ w_up)) @ w_down

def trunk(x, s_gla, h_rg, conv_buf, w_in, gla_w_gate, gla_b_gate, gla_norm_g,
          rg_conv_w, rg_conv_b, rg_w_a, rg_b_a, rg_w_x, rg_b_x, rg_lambda, w_out,
          ln1_g, ln1_b, ffn_w_gate, ffn_w_up, ffn_w_down, ln2_g, ln2_b):
    new_gla, new_rg, new_conv = [], [], []
    for l in range(DEPTH):
        mix, s_n, h_n, b_n = mixer(x, s_gla[l], h_rg[l], conv_buf[l], w_in[l], gla_w_gate[l], gla_b_gate[l],
                                   gla_norm_g[l], rg_conv_w[l], rg_conv_b[l], rg_w_a[l], rg_b_a[l],
                                   rg_w_x[l], rg_b_x[l], rg_lambda[l], w_out[l])
        x = layer_norm(DN_ALPHA * x + mix, ln1_g[l], ln1_b[l])
        x = layer_norm(DN_ALPHA * x + swiglu(x, ffn_w_gate[l], ffn_w_up[l], ffn_w_down[l]), ln2_g[l], ln2_b[l])
        new_gla.append(s_n.astype(x.dtype))
        new_rg.append(h_n.astype(x.dtype))
        new_conv.append(b_n.astype(x.dtype))
    return x, jnp.stack(new_gla), jnp.stack(new_rg), jnp.stack(new_conv)

def setup_inputs(seed: int = 0) -> dict:
    key = jax.random.key(seed)
    ks = jax.random.split(key, 32)
    f32 = jnp.float32
    nrm = lambda k, shape, s: jax.random.normal(k, shape, f32) * s
    col_scale = jnp.concatenate([jnp.full((s,), DN_BETA if idx in (2, 5) else 1.0, f32)
                                 for idx, s in enumerate(IN_SIZES)])
    u_lam = jax.random.uniform(ks[14], (DEPTH, RG_WIDTH), f32, 0.9, 0.999)
    root = u_lam ** (1.0 / RG_C)
    rg_lambda = jnp.log(root) - jnp.log1p(-root)
    return {
        "x_prompt": nrm(ks[0], (BATCH, SEQ, D_MODEL), 1.0),
        "x_sample": nrm(ks[1], (DEC_BATCH, DEC_SEQ, D_MODEL), 1.0),
        "state_gla": nrm(ks[2], (DEPTH, DEC_BATCH, N_GLA_HEADS, GLA_DK, GLA_DV), 0.3),
        "state_rglru": nrm(ks[3], (DEPTH, DEC_BATCH, RG_WIDTH), 0.5),
        "state_conv": nrm(ks[4], (DEPTH, DEC_BATCH, CONV_W - 1, RG_WIDTH), 1.0),
        "w_in": nrm(ks[5], (DEPTH, D_MODEL, D_IN), D_MODEL ** -0.5) * col_scale,
        "gla_w_gate": nrm(ks[6], (DEPTH, GATE_RANK, GLA_QK), GATE_RANK ** -0.5),
        "gla_b_gate": 2.0 + nrm(ks[7], (DEPTH, GLA_QK), 0.1),
        "gla_norm_g": 1.0 + nrm(ks[8], (DEPTH, GLA_DV), 0.02),
        "rg_conv_w": nrm(ks[9], (DEPTH, CONV_W, RG_WIDTH), CONV_W ** -0.5),
        "rg_conv_b": nrm(ks[10], (DEPTH, RG_WIDTH), 0.01),
        "rg_w_a": nrm(ks[11], (DEPTH, RG_BLOCKS, RG_BLOCK_W, RG_BLOCK_W), RG_BLOCK_W ** -0.5),
        "rg_b_a": nrm(ks[12], (DEPTH, RG_WIDTH), 0.01),
        "rg_w_x": nrm(ks[13], (DEPTH, RG_BLOCKS, RG_BLOCK_W, RG_BLOCK_W), RG_BLOCK_W ** -0.5),
        "rg_b_x": nrm(ks[15], (DEPTH, RG_WIDTH), 0.01),
        "rg_lambda": rg_lambda,
        "w_out": nrm(ks[16], (DEPTH, D_MIX, D_MODEL), D_MIX ** -0.5 * DN_BETA),
        "ln1_g": 1.0 + nrm(ks[17], (DEPTH, D_MODEL), 0.02),
        "ln1_b": nrm(ks[18], (DEPTH, D_MODEL), 0.01),
        "ffn_w_gate": nrm(ks[19], (DEPTH, D_MODEL, D_FF), D_MODEL ** -0.5),
        "ffn_w_up": nrm(ks[20], (DEPTH, D_MODEL, D_FF), D_MODEL ** -0.5 * DN_BETA),
        "ffn_w_down": nrm(ks[21], (DEPTH, D_FF, D_MODEL), D_FF ** -0.5 * DN_BETA),
        "ln2_g": 1.0 + nrm(ks[22], (DEPTH, D_MODEL), 0.02),
        "ln2_b": nrm(ks[23], (DEPTH, D_MODEL), 0.01),
    }

def reference(x_prompt, x_sample, state_gla, state_rglru, state_conv, w_in, gla_w_gate, gla_b_gate,
              gla_norm_g, rg_conv_w, rg_conv_b, rg_w_a, rg_b_a, rg_w_x, rg_b_x, rg_lambda, w_out,
              ln1_g, ln1_b, ffn_w_gate, ffn_w_up, ffn_w_down, ln2_g, ln2_b):
    weights = (w_in, gla_w_gate, gla_b_gate, gla_norm_g, rg_conv_w, rg_conv_b, rg_w_a, rg_b_a,
               rg_w_x, rg_b_x, rg_lambda, w_out, ln1_g, ln1_b, ffn_w_gate, ffn_w_up, ffn_w_down,
               ln2_g, ln2_b)
    B = x_prompt.shape[0]
    dt = x_prompt.dtype
    zero_gla = jnp.zeros((DEPTH, B, N_GLA_HEADS, GLA_DK, GLA_DV), dt)
    zero_rg = jnp.zeros((DEPTH, B, RG_WIDTH), dt)
    zero_conv = jnp.zeros((DEPTH, B, CONV_W - 1, RG_WIDTH), dt)
    y_prompt, gla_p, rg_p, conv_p = trunk(x_prompt, zero_gla, zero_rg, zero_conv, *weights)
    y_sample, gla_s, rg_s, conv_s = trunk(x_sample, state_gla, state_rglru, state_conv, *weights)
    return (y_prompt, y_sample, gla_p, rg_p, conv_p, gla_s, rg_s, conv_s)


_drawn_inputs = setup_inputs


def setup_inputs(seed=0):
    import zlib

    import numpy as np

    out = dict(_drawn_inputs(seed))
    spreads = {}
    factors = {'gla_norm_g': 22.736,
     'rg_b_a': 22.276,
     'rg_b_x': 8.0,
     'ln1_g': 2.83,
     'ln1_b': 5.724,
     'ln2_g': 7.944,
     'ln2_b': 16.433}
    for name, (base, spread) in spreads.items():
        noise = np.random.default_rng([zlib.crc32(name.encode()), seed]).standard_normal(out[name].shape)
        drawn = base * np.exp(spread * noise) if base else spread * noise
        out[name] = __import__('jax').numpy.asarray(drawn.astype(out[name].dtype))
    for name, factor in factors.items():
        out[name] = (out[name] * factor).astype(out[name].dtype)
    return out
```

```python
from contextlib import ExitStack

import concourse.bass as bass
from concourse import mybir

F32 = mybir.dt.float32
F32R = mybir.dt.float32r
ACT = mybir.ActivationFunctionType
ALU = mybir.AluOpType

P = 128
D = 1024
KC = D // P
TP = 1024
NB, LS = 8, 8
TS = NB * LS
T = TP + TS
NT = -(-T // P)
CH = [(0, 364), (364, 362), (726, 362)]
CW = CH[0][1]
F = 2816
NF = F // P
NG = NF // 2
DK, DV, CHUNK = 64, 128, 64
STEPS = TP // P
RANK = 16
COL_Q, COL_G, COL_Z, COL_XR, COL_GR = 0, 1024, 1536, 1552, 2064
ALPHA = 2.0 ** 0.25
LN_EPS, RMS_EPS = 1e-5, 1e-6

N_Z, N_XR, N_QKV, N_GR, N_G, N_WO, N_FFN = 0, 1, 5, 13, 17, 21, 29


def tokens(i):
    return i * P, min(P, T - i * P)


def chunk_of(i):
    t0, w = tokens(i)
    return max(k for k, (c0, _) in enumerate(CH) if c0 < t0 + w)


def out_bank(n):
    return n % 8 if n < NT else (0, 1, 2, 7)[(n - NT) % 4]


class Steps:

    def __init__(self, eng, sem):
        self.eng, self.sem, self.base, self.k = eng, sem, 0, 0

    def __call__(self, ins):
        ins.then_inc(self.sem, 1)
        self.k += 1
        self.eng.wait_ge(self.sem, self.base + self.k)

    def enter(self, i, per):
        self.saved, self.per = self.base + self.k, per
        self.base, self.k = i * per + self.saved, 0

    def leave(self, n):
        assert self.k == self.per, (self.k, self.per)
        self.base, self.k = self.saved + n * self.per, 0


def build(nc, x_prompt, x_sample, state_gla, state_rglru, state_conv, w_in, gla_w_gate, gla_b_gate,
          gla_norm_g, rg_conv_w, rg_conv_b, rg_w_a, rg_b_a, rg_w_x, rg_b_x, rg_lambda, w_out,
          ln1_g, ln1_b, ffn_w_gate, ffn_w_up, ffn_w_down, ln2_g, ln2_b,
          y_prompt, y_sample, gla_p, rg_p, conv_p, gla_s, rg_s, conv_s):
    ctx = ExitStack()
    with ctx:
        def at(name, shape, offset, dt=F32):
            return nc.alloc_sbuf_tensor_at(name, shape, dt, offset=BASE + offset)

        def sem(name):
            return ctx.enter_context(nc.semaphore(name))

        BASE = 16512
        TB = T * 4
        R_HIGH, R_LOW = 0, 8 * TB
        R_OHS = 16 * TB
        R_X = R_OHS + NT * 4096
        R_G = R_X + 32768
        R_RING = R_G + 45056
        R_RAW = R_RING + 4 * TB
        R_CONST = R_RAW + 8192

        act_h = at("act_h", [P, KC, T], R_HIGH, F32R)
        act_l = at("act_l", [P, KC, T], R_LOW, F32R)
        qk = at("qk", [P, 4, T], R_OHS)
        xr = at("xr", [P, 4, T], R_OHS + 4 * TB)
        rows = at("rows", [P, NT, D], R_OHS)
        v = at("v", [P, 4, T], R_X)
        soft = at("soft", [P, 2, T], R_X)
        z = at("z", [RANK, T], R_X + 2 * TB)
        cum = at("cum", [P, 2, T], R_X + 4 * TB)
        m01 = at("m01", [P, T], R_X + 6 * TB)
        gw = at("gw", [P, 2, P], R_X + 7 * TB)
        x_in = at("x_in", [P, NT, D], R_G)
        xc, t1, t2, tn = (at(n, [P, T], R_G + j * TB) for j, n in enumerate(("xc", "t1", "t2", "tn")))
        gw4 = at("gw4", [P, 4, 2, P], R_G + 4 * TB)
        g_at = [R_G]

        def gla(name, shape, bufs=1):
            size = 4
            for s in shape[1:]:
                size *= s
            out = []
            for b in range(bufs):
                out.append(at(f"{name}{b}", shape, g_at[0]))
                g_at[0] += -(-size // 32) * 32
            return out

        eb, enb, een = gla("eb", [P, 2, P])[0], gla("enb", [P, 2, P])[0], gla("een", [P, 2, P])[0]
        qe = gla("qe", [P, 2, 2, P], 2)
        qi = gla("qi", [P, 2, 2, CHUNK], 2)
        ke = gla("ke", [P, 2, P], 2)
        ka = gla("ka", [P, 2, CHUNK], 2)
        k2 = gla("k2", [P, 2, P], 2)
        k2t = gla("k2t", [P, 2 * P], 2)
        vt = gla("vt", [P, 4 * DV], 2)
        sc = gla("sc", [P, 4, P], 2)
        s_p = gla("s_p", [P, 2, DV])[0]
        s_s = gla("s_s", [P, 2, NB, DV])[0]
        vb = gla("vb", [P, NB, DV])[0]
        gx = gla("gx", [P, CW], 2)
        gt = gla("gt", [P, CW], 2)
        assert g_at[0] <= R_RING
        sq = at("sq", [P, T], R_G + 32768)
        rs = at("rs", [P, T], R_G + 32768 + TB)
        sg = [at(f"sg{b}", [P, CW], R_G + 32768 + 2 * TB + b * 1472) for b in range(2)]
        wh = [at(f"wh{b}", [P, KC, P], R_RING + b * 8192, F32R) for b in range(2)]
        wl = [at(f"wl{b}", [P, KC, P], R_RING + b * 8192 + 4096, F32R) for b in range(2)]
        raw = [at(f"raw{b}", [P, 1024], R_RAW + b * 4096) for b in range(2)]
        wo_h = [at(f"wo_h{b}", [P, KC, 512], r, F32R) for b, r in enumerate((R_G, R_X))]
        wo_l = [at(f"wo_l{b}", [P, KC, 512], r + 16384, F32R) for b, r in enumerate((R_G, R_X))]
        ln1 = at("ln1", [P, 2, D], R_G + 32768)
        gu_h = [[at(f"gu_h{m}{b}", [P, KC, P], R_G + m * 16384 + b * 8192, F32R) for b in range(2)] for m in range(2)]
        gu_l = [[at(f"gu_l{m}{b}", [P, KC, P], R_G + m * 16384 + b * 8192 + 4096, F32R) for b in range(2)]
                for m in range(2)]
        wd_h = [at(f"wd_h{b}", [P, D], R_X + b * 8192, F32R) for b in range(2)]
        wd_l = [at(f"wd_l{b}", [P, D], R_X + b * 8192 + 4096, F32R) for b in range(2)]
        ln2 = at("ln2", [P, 2, D], R_X + 16384)
        sl = [at(f"sl{b}", [P, CW], R_X + 24576 + b * 1472) for b in range(2)]
        hf = [at(f"hf{b}", [P, CW], R_X + 24576 + (2 + b) * 1472) for b in range(2)]
        hid_h = [at(f"hid_h{b}", [P, T], R_RING + b * TB, F32R) for b in range(2)]
        hid_l = [at(f"hid_l{b}", [P, T], R_RING + (2 + b) * TB, F32R) for b in range(2)]
        c_at = [R_CONST]

        def const(name, shape):
            size = 4
            for s in shape[1:]:
                size *= s
            out = at(name, shape, c_at[0])
            c_at[0] += -(-size // 32) * 32
            return out

        ident = const("ident", [P, P])
        causal = const("causal", [P, P])
        smask = const("smask", [TS, TS])
        ones = const("ones", [P, P])
        bmask = const("bmask", [TS, NB])
        par = const("par", [P, 35])
        cw = par[:, 0:16].rearrange("p (j c) -> p j c", j=4)
        cb, ba, bx, lam = (par[:, 16 + 4 * j:20 + 4 * j] for j in range(4))
        bg, gn = par[:, 32:34], par[:, 34:35]
        pk = const("pk", [P, 4, 4])
        hba, hbx, kp, kn = (pk[:, :, j] for j in range(4))
        cur = const("cur", [P, 4])
        e0, e1, e2, e3 = (const(n, [P, 4]) for n in ("e0", "e1", "e2", "e3"))
        eps = const("eps", [P, 1])
        res = const("res", [P, NG])
        dec = [const(f"dec{b}", [P, 2, NB]) for b in range(2)]
        dec2 = const("dec2", [P, 2])
        stats = [const(f"stats{b}", [P, 2, 6]) for b in range(2)]
        mv = [const(f"mv{b}", [P, 4]) for b in range(2)]
        wgate = at("wgate", [RANK, 2, P], R_X + 7 * TB + 1024)
        assert c_at[0] <= 229344 - BASE, c_at[0] - (229344 - BASE)
        st_in = at("st_in", [P, 4, 32], R_OHS + 8 * TB)
        st_out = at("st_out", [P, 4, 36], R_OHS + 8 * TB + 512)
        st_rows = at("st_rows", [36, 512], R_X)

        par_rows = at("par_rows", [35, P], R_X + 2048)
        ps = [ctx.enter_context(nc.psum_tensor(f"ps{b}", [P, 512], F32)) for b in range(8)]

        x_loaded = [sem(f"x_loaded{i}") for i in range(NT)]
        raw_loaded = [sem("raw_loaded0"), sem("raw_loaded1")]
        params_loaded, gw_loaded, state_loaded = sem("params_loaded"), sem("gw_loaded"), sem("state_loaded")
        gla_state_loaded, ln1_loaded, ln2_loaded = sem("gla_state_loaded"), sem("ln1_loaded"), sem("ln2_loaded")
        out_stored, states_stored = sem("out_stored"), sem("states_stored")
        consts_made, gw_zeroed = sem("consts_made"), sem("gw_zeroed")
        turned, turned_high, turned_low = sem("turned"), sem("turned_high"), sem("turned_low")
        w_high, w_low = sem("w_high"), sem("w_low")
        in_done, in_read = sem("in_done"), sem("in_read")
        zg_done, zg_read, soft_ready, cum_ready = sem("zg_done"), sem("zg_read"), sem("soft_ready"), sem("cum_ready")
        states_turned, states_read = sem("states_turned"), sem("states_read")
        states_back, states_rows = sem("states_back"), sem("states_rows")
        dve_step, act_step, pool_step = sem("dve_step"), sem("act_step"), sem("pool_step")
        lam_abs, lam_ready = sem("lam_abs"), sem("lam_ready")
        conv_ready, gates_done, gates_read = sem("conv_ready"), sem("gates_done"), sem("gates_read")
        decay_ready, room_ready, root_ready, h_ready = sem("decay_ready"), sem("room_ready"), sem("root_ready"), sem("h_ready")
        d_ready, exp_ready, prep_ready = sem("d_ready"), sem("exp_ready"), sem("prep_ready")
        a_done, b_done, tok_ready, sc_ready, o_ready = (sem(n) for n in ("a_done", "b_done", "tok_ready", "sc_ready", "o_ready"))
        vb_ready, kv_done, kv_read = sem("vb_ready"), sem("kv_done"), sem("kv_read")
        gx_ready, poly_ready, tanh_ready, gelu_done = (sem(n) for n in ("gx_ready", "poly_ready", "tanh_ready", "gelu_done"))
        sq_ready, ms_done, rs_ready, o_normed, sg_ready, yg_ready = (
            sem(n) for n in ("sq_ready", "ms_done", "rs_ready", "o_normed", "sg_ready", "yg_ready"))
        y_high, y_low, y_low2 = sem("y_high"), sem("y_low"), sem("y_low2")
        op_done, op_read = sem("op_done"), sem("op_read")
        var_ready, std_ready, ln_z, ln_done = sem("var_ready"), sem("std_ready"), sem("ln_z"), sem("ln_done")
        gate_done, up_done, silu_ready, hid_ready, hid_high, hid_low = (
            sem(n) for n in ("gate_done", "up_done", "silu_ready", "hid_ready", "hid_high", "hid_low"))
        down_done, down_read = sem("down_done"), sem("down_read")

        w_in_v = w_in.rearrange("l (c p) n -> p (l c) n", p=P)
        w_out_v = w_out.rearrange("l (c p) n -> p (l c) n", p=P)
        w_gu_v = [w.rearrange("l (c p) n -> p (l c) n", p=P) for w in (ffn_w_gate, ffn_w_up)]
        w_dn_v = ffn_w_down.rearrange("l f n -> (l f) n")
        xp_v = x_prompt.rearrange("b t d -> (b t) d")
        xs_v = x_sample.rearrange("b t d -> (b t) d")
        yp_v = y_prompt.rearrange("b t d -> (b t) d")
        ys_v = y_sample.rearrange("b t d -> (b t) d")

        def raw3(n, c=KC):
            return raw[n % 2][:, :].rearrange("p (c n) -> p c n", c=c)

        block = ctx.enter_context(nc.Block())

        @block.sync
        def _(sp):
            def x_rows(i):
                return xp_v[i * P:(i + 1) * P, :] if i < NT - 1 else xs_v

            def piece(n, slot, src, dst=None):
                if not isinstance(n, int) or n >= 2:
                    sp.wait_ge(w_low, n - 1)
                sp.dma_start(raw3(slot) if dst is None else dst, src).then_inc(raw_loaded[slot % 2], 16)

            def w_in_tile(col):
                return w_in_v[:, :, bass.ds(col, P)]

            sp.dma_start(x_in[:, 0, :], x_rows(0)).then_inc(x_loaded[0], 16)
            piece(0, 0, w_in_v[:, :, COL_Z:COL_Z + RANK], raw[0][:, 0:KC * RANK].rearrange("p (c n) -> p c n", c=KC))
            for i in range(1, 4):
                sp.dma_start(x_in[:, i, :], x_rows(i)).then_inc(x_loaded[i], 16)
            piece(1, 1, w_in_tile(COL_XR))
            for i in range(4, NT):
                w = tokens(i)[1]
                sp.dma_start(x_in[0:w, i, :], x_rows(i)).then_inc(x_loaded[i], 16)
            for n in range(2, 5):
                piece(n, n, w_in_tile(COL_XR + (n - 1) * P))
            sp.wait_ge(gw_zeroed, 1)
            for c in range(4):
                for m, w in enumerate((rg_w_a, rg_w_x)):
                    for q in range(2):
                        sp.dma_start(gw4[q * 64:q * 64 + 64, c, m, q * 64:q * 64 + 64],
                                     w[0, 2 * c + q]).then_inc(gw_loaded, 16)
            for p in range(2):
                sp.dma_start(s_s[:, p, :, :], state_gla[0, :, 2 * p:2 * p + 2].rearrange("b q d v -> (q d) b v")
                             ).then_inc(gla_state_loaded, 16)
            with sp.Fori(0, 4) as i:
                for j in range(2):
                    piece(i * 2 + (N_QKV + j), N_QKV + j, w_in_tile(i * 256 + (COL_Q + j * P)))
            for j in range(4):
                piece(N_GR + j, N_GR + j, w_in_tile(COL_GR + j * P))
            for j in range(2):
                piece(N_G + j, N_G + j, w_in_tile(COL_G + j * P))
            sp.wait_ge(states_rows, 1)
            sp.dma_start(conv_p[0, 0], st_rows[0:3, :]).then_inc(states_stored, 16)
            sp.dma_start(conv_s.rearrange("l b w c -> (l b w) c"), st_rows[3:27, :]).then_inc(states_stored, 16)
            sp.dma_start(rg_p[0], st_rows[27:28, :]).then_inc(states_stored, 16)
            sp.dma_start(rg_s[0], st_rows[28:36, :]).then_inc(states_stored, 16)
            for j in range(2, 4):
                piece(N_G + j, N_G + j, w_in_tile(COL_G + j * P))
            sp.wait_ge(kv_read, STEPS + 2)
            sp.dma_start(gla_p[0, 0].rearrange("(p q) d v -> (q d) p v", q=2), s_p[:, :, :]).then_inc(states_stored, 16)
            for p in range(2):
                sp.dma_start(gla_s[0, :, 2 * p:2 * p + 2].rearrange("b q d v -> (q d) b v"),
                             s_s[:, p, :, :]).then_inc(states_stored, 16)
            for m in range(8):
                q = m % 4
                piece(N_WO + m, N_WO + m, w_out_v[:, 2 * q:2 * q + 2, (m // 4) * 512:(m // 4) * 512 + 512],
                      raw3(N_WO + m, 2))
            sp.wait_ge(y_low, NT)
            sp.wait_ge(y_low2, NT)
            for i in range(NT):
                w = tokens(i)[1]
                sp.dma_start(rows[0:w, i, :], x_rows(i)).then_inc(x_loaded[i], 16)
            for j, w in enumerate((ln1_g, ln1_b)):
                sp.dma_start(ln1[:, j, :], w[0:1, :].broadcast_to([P, D])).then_inc(ln1_loaded, 16)

            def ffn_pieces(g):
                for j in range(2):
                    for m in range(2):
                        k = 3 * j + m
                        piece(g * 6 + (N_FFN + k), N_FFN + k, w_gu_v[m][:, :, bass.ds(g * 256 + j * P, P)])
                    k = 3 * j + 2
                    piece(g * 6 + (N_FFN + k), N_FFN + k, w_dn_v[bass.ds(g * 256 + j * P, P), :],
                          raw[(N_FFN + k) % 2][:, :])

            ffn_pieces(0)
            for j, w in enumerate((ln2_g, ln2_b)):
                sp.dma_start(ln2[:, j, :], w[0:1, :].broadcast_to([P, D])).then_inc(ln2_loaded, 16)
            with sp.Fori(1, NG) as g:
                ffn_pieces(g)
            for i in range(NT):
                sp.wait_ge(ln_done, NT + i + 1)
                w = tokens(i)[1]
                dst = yp_v[i * P:(i + 1) * P, :] if i < NT - 1 else ys_v
                sp.dma_start(dst, rows[0:w, i, :]).then_inc(out_stored, 16)
            sp.wait_ge(out_stored, 16 * NT)
            sp.wait_ge(states_stored, 16 * 7)

        @block.gpsimd
        def _(pool):
            step = Steps(pool, pool_step)
            pool.dma_start(par_rows[0:16, :], rg_conv_w.rearrange("l j (c p) -> (l j c) p", p=P)).then_inc(params_loaded, 16)
            for r, src in ((16, rg_conv_b), (20, rg_b_a), (24, rg_b_x), (28, rg_lambda), (32, gla_b_gate), (34, gla_norm_g)):
                n = src.shape[1] // P
                pool.dma_start(par_rows[r:r + n, :], src.rearrange("l (c p) -> (l c) p", p=P)).then_inc(params_loaded, 16)
            pool.dma_start(wgate[:, :, :], gla_w_gate[0].rearrange("r (a n) -> r a n", a=2)).then_inc(params_loaded, 16)
            pool.dma_start(st_rows[0:24, :], state_conv[0].rearrange("b w c -> (b w) c")).then_inc(state_loaded, 16)
            pool.dma_start(st_rows[24:32, :], state_rglru[0]).then_inc(state_loaded, 16)
            step(pool.memset(ident[:, :], 1.0))
            step(pool.affine_select(out=ident[:, :], in_=ident[:, :], compare_op=ALU.is_equal, fill=0.0, base=0,
                                    pattern=[[-1, P]], channel_multiplier=1))
            step(pool.memset(causal[:, :], 1.0))
            step(pool.affine_select(out=causal[:, :], in_=causal[:, :], compare_op=ALU.is_ge, fill=0.0, base=0,
                                    pattern=[[1, P]], channel_multiplier=-1))
            step(pool.affine_select(out=smask[:, :].rearrange("p (b c) -> p b c", b=NB),
                                    in_=causal[0:TS, 0:TS].rearrange("p (b c) -> p b c", b=NB),
                                    compare_op=ALU.is_ge, fill=0.0, base=0,
                                    pattern=[[-LS, NB], [0, LS]], channel_multiplier=1))
            step(pool.memset(bmask[:, :], 1.0))
            step(pool.affine_select(out=bmask[:, :], in_=bmask[:, :], compare_op=ALU.is_ge, fill=0.0, base=0,
                                    pattern=[[-LS, NB]], channel_multiplier=1))
            step(pool.affine_select(out=bmask[:, :], in_=bmask[:, :], compare_op=ALU.is_ge, fill=0.0, base=LS - 1,
                                    pattern=[[LS, NB]], channel_multiplier=-1))
            pool.memset(ones[:, :], 1.0 / DV)
            pool.memset(eps[:, :], RMS_EPS)
            step(pool.memset(m01[:, :], 1.0))
            pool.memset(m01[:, 0:TP:CHUNK], 0.0)
            pool.memset(m01[:, TP:T:LS], 0.0)
            step(pool.memset(res[:, :], 1.0))
            step(pool.memset(res[:, 0:1], ALPHA))
            pool.memset(dec2[:, :], 0.0).then_inc(consts_made, 1)

            def low(n, slot, dst, src):
                pool.wait_ge(w_high, n + 1)
                pool.tensor_tensor(dst[0], src, dst[1].bitcast(F32), ALU.subtract).then_inc(w_low, 1)

            def ring_low(n, slot):
                low(n, slot, (wl[slot % 2][:, :, :], wh[slot % 2][:, :, :]), raw3(slot))

            low(0, 0, (wl[0][:, :, 0:RANK], wh[0][:, :, 0:RANK]),
                raw[0][:, 0:KC * RANK].rearrange("p (c n) -> p c n", c=KC))
            with pool.Fori(0, 6) as i:
                for j in range(2):
                    ring_low(i * 2 + (N_XR + j), N_XR + j)

            def gelu_poly(m):
                w = CH[m % 3][1]
                pool.wait_ge(gx_ready, m + 1)
                if m >= 2:
                    pool.wait_ge(gelu_done, m - 1)
                a, b = gx[m % 2][:, 0:w], gt[m % 2][:, 0:w]
                step(pool.tensor_tensor(b, a, a, ALU.mult))
                step(pool.tensor_scalar(b, b, 0.044715, 1.0, ALU.mult, ALU.add))
                pool.tensor_tensor(b, b, a, ALU.mult).then_inc(poly_ready, 1)

            for m in range(12):
                if m % 3 == 0:
                    ring_low(N_GR + m // 3, N_GR + m // 3)
                gelu_poly(m)
            for j in range(4):
                ring_low(N_G + j, N_G + j)
            for m in range(8):
                q, b = m % 4, m // 4
                low(N_WO + m, N_WO + m, (wo_l[b][:, 2 * q:2 * q + 2, :], wo_h[b][:, 2 * q:2 * q + 2, :]),
                    raw3(N_WO + m, 2))
            for i in range(NT):
                t0, w = tokens(i)
                pool.wait_ge(y_high, 2 * i + 2)
                pool.tensor_tensor(act_l[:, 4:8, t0:t0 + w], xr[:, :, t0:t0 + w],
                                   act_h[:, 4:8, t0:t0 + w].bitcast(F32), ALU.subtract).then_inc(y_low2, 1)

            def affine(i, ln, base):
                w = tokens(i)[1]
                pool.wait_ge(ln_z, base + i + 1)
                pool.tensor_tensor(rows[0:w, i, :], rows[0:w, i, :], ln[0:w, 1, :], ALU.add).then_inc(ln_done, 1)

            pool.wait_ge(ln1_loaded, 32)
            for i in range(NT):
                affine(i, ln1, 0)

            def ffn_lows(g):
                for j in range(2):
                    for m in range(2):
                        k = 3 * j + m
                        low(g * 6 + (N_FFN + k), N_FFN + k, (gu_l[m][j][:, :, :], gu_h[m][j][:, :, :]), raw3(N_FFN + k))
                    k = 3 * j + 2
                    low(g * 6 + (N_FFN + k), N_FFN + k, (wd_l[j][:, :], wd_h[j][:, :]), raw[(N_FFN + k) % 2][:, :])

            with pool.Fori(0, NG) as g:
                ffn_lows(g)
            pool.wait_ge(ln2_loaded, 32)
            for i in range(NT):
                affine(i, ln2, NT)

        @block.scalar
        def _(act):
            step = Steps(act, act_step)

            def turn_high(n):
                i, g = n // 2, n % 2
                t0, w = tokens(i % NT)
                act.wait_ge(turned, n + 1)
                act.activation(act_h[:, 4 * g:4 * g + 4, t0:t0 + w],
                               ps[3 + n % 4][:, :].rearrange("p (c t) -> p c t", c=4)[:, :, 0:w],
                               ACT.Copy).then_inc(turned_high, 1)

            def high(n, slot, dst, src, uses):
                act.wait_ge(raw_loaded[slot % 2], uses)
                act.activation(dst, src, ACT.Copy).then_inc(w_high, 1)

            def loads(n, slot):
                return (n - slot % 2) * 8 + 16

            def ring_high(n, slot, wait=True):
                if wait:
                    act.wait_ge(in_done, n * 3 - 3)
                high(n, slot, wh[slot % 2][:, :, :], raw3(slot), loads(n, slot))

            def read(n, k, out, fn=ACT.Copy, also=None):
                c0, cn = CH[k]
                act.wait_ge(in_done, n * 3 + (k + 1))
                ins = act.activation(out, ps[k][:, 0:cn], fn)
                ins.then_inc(in_read, 1)
                return ins

            high(0, 0, wh[0][:, :, 0:RANK], raw[0][:, 0:KC * RANK].rearrange("p (c n) -> p c n", c=KC), 16)
            high(1, 1, wh[1][:, :, :], raw3(1), 16)
            for n in range(2 * NT):
                turn_high(n)
            for k, (c0, cn) in enumerate(CH):
                act.wait_ge(in_done, k + 1)
                act.activation(z[:, c0:c0 + cn], ps[k][0:RANK, 0:cn], ACT.Copy).then_inc(in_read, 1)
            ring_high(2, 2)
            act.wait_ge(states_read, 1)
            act.activation(e0[:, :], lam[:, :], ACT.Abs).then_inc(lam_abs, 1)
            for u in range(6):
                p, k = u // 3, u % 3
                c0, cn = CH[k]
                act.wait_ge(zg_done, u + 1)
                act.activation(cum[:, p, c0:c0 + cn], ps[3 + u % 5][:, 0:cn], ACT.Identity,
                               bias=bg[:, p:p + 1]).then_inc(zg_read, 1)
            act.wait_ge(zg_read, 6)
            step(act.activation(soft[:, :, :], cum[:, :, :], ACT.Abs))
            act.wait_ge(lam_abs, 1)
            act.activation(e0[:, :], e0[:, :], ACT.Exp, scale=-1.0).then_inc(lam_ready, 1)
            step(act.activation(soft[:, :, :], soft[:, :, :], ACT.Exp, scale=-1.0))
            act.activation(soft[:, :, :], soft[:, :, :], ACT.Ln, bias=1.0).then_inc(soft_ready, 1)
            with act.Fori(0, 2) as i:
                for j in range(2):
                    for k, (c0, cn) in enumerate(CH):
                        read(i * 2 + (N_XR + j), k, xr[:, bass.ds(i * 2 + j, 1), c0:c0 + cn])
                    ring_high(i * 2 + (N_XR + j + 2), N_XR + j + 2)

            def rg_tanh(i, k):
                c0, cn = CH[k]
                act.wait_ge(gates_done, i * 3 + (k + 1))
                act.activation(t1[:, c0:c0 + cn], ps[3][:, 0:cn], ACT.Tanh, bias=cur[:, 0:1], scale=0.5)
                act.activation(t2[:, c0:c0 + cn], ps[4][:, 0:cn], ACT.Tanh, bias=cur[:, 1:2],
                               scale=0.5).then_inc(gates_read, 1)

            def qkv_body(i, n0, dst, last):
                ch = i + (n0 - N_QKV) // 2
                n = i * 2 + n0

                def tile(j, k):
                    c0, cn = CH[k]
                    read(n + j, k, dst[:, bass.ds(i * 2 + j, 1), c0:c0 + cn])

                tile(0, 0)
                tile(0, 1)
                rg_tanh(ch, 0)
                tile(0, 2)
                ring_high(n + 2, n0 + 2)
                rg_tanh(ch, 1)
                tile(1, 0)
                rg_tanh(ch, 2)
                act.wait_ge(gates_read, ch * 3 + 3)
                step(act.activation(tn[:, :], t1[:, :], ACT.Tanh, bias=cur[:, 2:3], scale=cur[:, 2:3]))
                act.activation(t1[:, :], t1[:, :], ACT.Exp, bias=cur[:, 3:4],
                               scale=cur[:, 3:4]).then_inc(decay_ready, 1)
                tile(1, 1)
                act.wait_ge(room_ready, ch + 1)
                act.activation(tn[:, :], tn[:, :], ACT.Sqrt, scale=-1.0).then_inc(root_ready, 1)
                tile(1, 2)
                ring_high(n + 3, n0 + 3)

            for n0, dst in ((N_QKV, qk), (N_QKV + 4, v)):
                with act.Fori(0, 2) as i:
                    step.enter(i, 1)
                    qkv_body(i, n0, dst, False)
                    step.leave(2)

            def exps(s):
                w = tokens(s)[1]
                t0 = tokens(s)[0]
                act.wait_ge(d_ready, s + 1)
                act.activation(een[:, :, 0:w], een[:, :, 0:w], ACT.Exp, scale=1 / 16)
                act.activation(enb[:, :, 0:w], cum[:, :, t0:t0 + w], ACT.Exp, scale=-1 / 16)
                act.activation(eb[:, :, 0:w], cum[:, :, t0:t0 + w], ACT.Exp, scale=1 / 16).then_inc(exp_ready, 1)

            def to_tokens(s):
                w = tokens(s)[1]
                act.wait_ge(a_done, s + 1)
                act.activation(k2t[s % 2][0:w, :], ps[4][0:w, 0:2 * P], ACT.Copy)
                act.activation(vt[s % 2][0:w, :], ps[5][0:w, :], ACT.Copy).then_inc(tok_ready, 1)

            def gelu_tanh(m):
                w = CH[m % 3][1]
                act.wait_ge(poly_ready, m + 1)
                act.activation(gt[m % 2][:, 0:w], gt[m % 2][:, 0:w], ACT.Tanh,
                               scale=0.7978845608028654).then_inc(tanh_ready, 1)

            exps(0)
            for m in range(12):
                n, k = N_GR + m // 3, m % 3
                if m + 1 <= STEPS:
                    exps(m + 1)
                if m >= 2:
                    act.wait_ge(gelu_done, m - 1)
                act.wait_ge(in_done, n * 3 + k + 1)
                act.activation(gx[m % 2][:, 0:CH[k][1]], ps[k][:, 0:CH[k][1]], ACT.Copy).then_inc(gx_ready, 1)
                if k == 2:
                    ring_high(n + 2, n + 2)
                if m <= STEPS:
                    to_tokens(m)
                if m >= 1:
                    gelu_tanh(m - 1)
            gelu_tanh(11)
            act.wait_ge(states_back, 1)
            act.activation(st_rows[:, :], ps[4][0:36, :], ACT.Copy).then_inc(states_rows, 1)

            def wo_high(m):
                q, b = m % 4, m // 4
                n = N_WO + m
                high(n, n, wo_h[b][:, 2 * q:2 * q + 2, :], raw3(n, 2), loads(n, n))

            act.wait_ge(states_stored, 16 * 7)
            act.wait_ge(o_ready, STEPS + 1)
            act.wait_ge(gelu_done, 12)
            act.activation(sq[:, :], qk[:, 0, :], ACT.Square).then_inc(sq_ready, 1)
            for h in range(4):
                n = N_G + h
                if h:
                    act.wait_ge(o_normed, h)
                for k, (c0, cn) in enumerate(CH):
                    act.wait_ge(ms_done, 3 * h + k + 1)
                    ins = act.activation(rs[:, c0:c0 + cn], ps[3 + k][:, 0:cn], ACT.Ln, bias=eps[:, 0:1])
                step(ins)
                act.activation(rs[:, :], rs[:, :], ACT.Exp, scale=-0.5).then_inc(rs_ready, 1)
                if h < 3:
                    act.activation(sq[:, :], qk[:, h + 1, :], ACT.Square).then_inc(sq_ready, 1)
                for k, (c0, cn) in enumerate(CH):
                    u = 3 * h + k
                    if u >= 2:
                        act.wait_ge(yg_ready, u - 1)
                    act.wait_ge(in_done, n * 3 + k + 1)
                    act.activation(sg[u % 2][:, 0:cn], ps[k][:, 0:cn], ACT.Silu).then_inc(sg_ready, 1)
                if h < 2:
                    ring_high(n + 2, n + 2)
                else:
                    for m in range(4 * (h - 2), 4 * (h - 2) + 4):
                        wo_high(m)
            act.wait_ge(yg_ready, 12)
            for i in range(NT):
                t0, w = tokens(i)
                act.activation(act_h[:, 0:4, t0:t0 + w], qk[:, :, t0:t0 + w], ACT.Copy).then_inc(y_high, 1)
                act.activation(act_h[:, 4:8, t0:t0 + w], xr[:, :, t0:t0 + w], ACT.Copy).then_inc(y_high, 1)

            def root(i, base):
                w = tokens(i)[1]
                act.wait_ge(var_ready, base + i + 1)
                act.activation(mv[i % 2][0:w, 1:2], mv[i % 2][0:w, 1:2], ACT.Sqrt).then_inc(std_ready, 1)

            def ffn_highs(g, j):
                for m in range(2):
                    k = 3 * j + m
                    n = g * 6 + (N_FFN + k)
                    high(n, N_FFN + k, gu_h[m][j][:, :, :], raw3(N_FFN + k), loads(n, N_FFN + k))
                return 3 * j + 2

            def down_high(g, j):
                k = 3 * j + 2
                n = g * 6 + (N_FFN + k)
                high(n, N_FFN + k, wd_h[j][:, :], raw[(N_FFN + k) % 2][:, :], loads(n, N_FFN + k))

            act.wait_ge(op_done, NT)
            for i in range(NT):
                root(i, 0)
                if i == 5:
                    ffn_highs(0, 0)
                if i >= 1:
                    for n in (2 * (i - 1), 2 * (i - 1) + 1):
                        turn_high(2 * NT + n)
            for n in (2 * NT - 2, 2 * NT - 1):
                turn_high(2 * NT + n)
            act.wait_ge(op_done, 2 * NT)
            down_high(0, 0)
            ffn_highs(0, 1)
            down_high(0, 1)

            def unit(g, u):
                j, k = u // 3, u % 3
                c0, cn = CH[k]
                act.wait_ge(gate_done, g * 6 + (u + 1))
                act.activation(sl[u % 2][:, 0:cn], ps[u % 2][:, 0:cn], ACT.Silu).then_inc(silu_ready, 1)

            def unit_high(g, u):
                j, k = u // 3, u % 3
                c0, cn = CH[k]
                act.wait_ge(hid_ready, g * 6 + (u + 1))
                act.activation(hid_h[j][:, c0:c0 + cn], hf[u % 2][:, 0:cn], ACT.Copy).then_inc(hid_high, 1)

            def ffn(g, more):
                for u in range(6):
                    unit(g, u)
                    if u:
                        unit_high(g, u - 1)
                    if more and u == 3:
                        act.wait_ge(up_done, g * 6 + 3)
                        ffn_highs(g + 1, 0)
                unit_high(g, 5)
                if more:
                    act.wait_ge(down_done, g * (2 * NT) + 2 * NT)
                    down_high(g + 1, 0)
                    act.wait_ge(up_done, g * 6 + 6)
                    ffn_highs(g + 1, 1)
                    down_high(g + 1, 1)

            with act.Fori(0, NG - 1) as g:
                ffn(g, True)
            ffn(NG - 1, False)
            for i in range(NT):
                root(i, NT)

        @block.vector
        def _(dve):
            step = Steps(dve, dve_step)

            def turn_low(n):
                i, g = n // 2, n % 2
                t0, w = tokens(i % NT)
                dve.wait_ge(turned_high, n + 1)
                dve.tensor_tensor(act_l[:, 4 * g:4 * g + 4, t0:t0 + w],
                                  ps[3 + n % 4][:, :].rearrange("p (c t) -> p c t", c=4)[:, :, 0:w],
                                  act_h[:, 4 * g:4 * g + 4, t0:t0 + w].bitcast(F32),
                                  ALU.subtract).then_inc(turned_low, 1)

            for n in range(2 * NT):
                turn_low(n)
            dve.memset(gw4[:, :, :, :], 0.0).then_inc(gw_zeroed, 1)
            dve.wait_ge(states_turned, 1)
            dve.tensor_copy(par[:, :], ps[7][:, P:P + 35])
            dve.tensor_copy(st_in[:, :, :], ps[7][:, 0:128].rearrange("p (c n) -> p c n", c=4)).then_inc(states_read, 1)
            dve.wait_ge(lam_ready, 1)
            step(dve.tensor_scalar(e1[:, :], e0[:, :], 2.0, None, ALU.add))
            step(dve.reciprocal(e1[:, :], e1[:, :]))
            step(dve.tensor_tensor(e1[:, :], e0[:, :], e1[:, :], ALU.mult))
            step(dve.tensor_tensor(e2[:, :], e1[:, :], e1[:, :], ALU.mult))
            step(dve.tensor_scalar(e3[:, :], e2[:, :], 1 / 17, None, ALU.mult))
            for q in range(15, 1, -2):
                step(dve.scalar_tensor_tensor(out=e3[:, :], in0=e3[:, :], scalar=1.0 / q, in1=e2[:, :],
                                              op0=ALU.add, op1=ALU.mult))
            step(dve.scalar_tensor_tensor(out=e3[:, :], in0=e3[:, :], scalar=1.0, in1=e1[:, :],
                                          op0=ALU.add, op1=ALU.mult))
            step(dve.tensor_scalar(e2[:, :], lam[:, :], -1.0, 0.0, ALU.mult, ALU.max))
            step(dve.scalar_tensor_tensor(out=e3[:, :], in0=e3[:, :], scalar=2.0, in1=e2[:, :],
                                          op0=ALU.mult, op1=ALU.add))
            dve.tensor_scalar(kp, e3[:, :], 2.0, None, ALU.mult)
            dve.tensor_scalar(kn, e3[:, :], -4.0, None, ALU.mult)
            dve.tensor_scalar(hba, ba[:, :], 0.5, None, ALU.mult)
            step(dve.tensor_scalar(hbx, bx[:, :], 0.5, None, ALU.mult))
            dve.wait_ge(soft_ready, 1)
            dve.wait_ge(consts_made, 1)
            step(dve.scalar_tensor_tensor(out=cum[:, :, :], in0=cum[:, :, :], scalar=0.0, in1=soft[:, :, :],
                                          op0=ALU.min, op1=ALU.subtract))
            for p in range(2):
                ins = dve.tensor_tensor_scan(cum[:, p, :], m01[:, :], cum[:, p, :], 0.0, ALU.mult, ALU.add)
            ins.then_inc(cum_ready, 1)

            dve.wait_ge(in_read, 3 * N_QKV)
            dve.wait_ge(gw_loaded, 16 * 16)

            def sample(tile, a, b):
                return tile.rearrange("p (b t) -> p b t", b=NB)[:, :, a:b]

            def rg_body(ch):
                one = bass.ds(ch, 1)
                x_t = xr[:, one, :].rearrange("p o t -> p (o t)")
                dve.tensor_copy(gw[:, :, :], gw4[:, one, :, :].rearrange("p o m n -> p (o m) n"))
                dve.tensor_copy(cur[:, :], pk[:, one, :].rearrange("p o k -> p (o k)"))
                step(dve.tensor_scalar(xc[:, :], x_t, cw[:, 3, one], cb[:, one], ALU.mult, ALU.add))
                for d in range(1, 4):
                    tap = cw[:, 3 - d, one]
                    dve.scalar_tensor_tensor(out=xc[:, d:TP], in0=x_t[:, 0:TP - d], scalar=tap, in1=xc[:, d:TP],
                                             op0=ALU.mult, op1=ALU.add)
                    s_x = x_t[:, TP:T]
                    s_c = xc[:, TP:T]
                    dve.scalar_tensor_tensor(out=sample(s_c, d, LS), in0=sample(s_x, 0, LS - d), scalar=tap,
                                             in1=sample(s_c, d, LS), op0=ALU.mult, op1=ALU.add)
                    hist = st_in[:, one, 0:24].rearrange("p o (b w) -> p (o b) w", w=3)[:, :, 3 - d:3]
                    ins = dve.scalar_tensor_tensor(out=sample(s_c, 0, d), in0=hist, scalar=tap,
                                                   in1=sample(s_c, 0, d), op0=ALU.mult, op1=ALU.add)
                    if d < 3:
                        step(ins)
                ins.then_inc(conv_ready, 1)
                dve.tensor_copy(st_out[:, one, 0:3], xr[:, one, TP - 3:TP])
                dve.tensor_copy(st_out[:, one, 3:27].rearrange("p o (b w) -> p (o b) w", w=3), sample(x_t[:, TP:T], LS - 3, LS))
                dve.wait_ge(decay_ready, ch + 1)
                step(dve.scalar_tensor_tensor(out=tn[:, :], in0=t1[:, :], scalar=1.0, in1=tn[:, :],
                                              op0=ALU.add, op1=ALU.mult))
                dve.tensor_scalar(t1[:, :], tn[:, :], -1.0, 1.0, ALU.mult, ALU.add)
                step(dve.scalar_tensor_tensor(out=tn[:, :], in0=tn[:, :], scalar=2.0, in1=tn[:, :],
                                              op0=ALU.subtract, op1=ALU.mult))
                dve.tensor_scalar(tn[:, :], tn[:, :], 0.0, None, ALU.min).then_inc(room_ready, 1)
                step(dve.scalar_tensor_tensor(out=t2[:, :], in0=t2[:, :], scalar=1.0, in1=xc[:, :],
                                              op0=ALU.add, op1=ALU.mult))
                dve.wait_ge(root_ready, ch + 1)
                step(dve.scalar_tensor_tensor(out=t2[:, :], in0=t2[:, :], scalar=0.5, in1=tn[:, :],
                                              op0=ALU.mult, op1=ALU.mult))
                first_a, first_u = sample(t1[:, TP:T], 0, 1), sample(t2[:, TP:T], 0, 1)
                h0 = st_in[:, one, 24:32].rearrange("p o (b w) -> p (o b) w", w=1)
                tmp = tn[:, 0:NB].rearrange("p (b w) -> p b w", w=1)
                step(dve.tensor_tensor(tmp, first_a, h0, ALU.mult))
                dve.tensor_tensor(first_u, first_u, tmp, ALU.add)
                step(dve.memset(first_a, 0.0))
                step(dve.tensor_tensor_scan(x_t, t1[:, :], t2[:, :], 0.0, ALU.mult, ALU.add))
                dve.tensor_copy(st_out[:, one, 27:28], xr[:, one, TP - 1:TP])
                dve.tensor_copy(st_out[:, one, 28:36].rearrange("p o (b w) -> p (o b) w", w=1),
                                sample(x_t[:, TP:T], LS - 1, LS)).then_inc(h_ready, 1)

            with dve.Fori(0, 4) as i:
                step.enter(i, 10)
                rg_body(i)
                step.leave(4)

            dve.wait_ge(h_ready, 4)
            for b in range(2):
                dve.memset(qe[b][:, :, :, :], 0.0)
                dve.memset(qi[b][:, :, :, :], 0.0)
                dve.memset(sc[b][:, :, :], 0.0)
            step(dve.memset(s_p[:, :, :], 0.0))

            def spread(s):
                t0, w = tokens(s)
                c = CHUNK if s < STEPS else LS
                b = cum[:, :, t0:t0 + w].rearrange("p a (n c) -> p a n c", c=c)
                dve.tensor_tensor(een[:, :, 0:w].rearrange("p a (n c) -> p a n c", c=c),
                                  b[:, :, :, c - 1:c].broadcast_to([P, 2, w // c, c]), b,
                                  ALU.subtract).then_inc(d_ready, 1)

            def prep(s):
                t0, w = tokens(s)
                b = s % 2
                c = CHUNK if s < STEPS else LS
                if s >= 2:
                    dve.wait_ge(b_done, s - 1)
                dve.wait_ge(exp_ready, s + 1)
                for q in range(2):
                    r = slice(64 * q, 64 * q + 64)
                    dve.scalar_tensor_tensor(out=qe[b][r, :, q, 0:w], in0=qk[r, 0:2, t0:t0 + w], scalar=DK ** -0.5,
                                             in1=eb[r, :, 0:w], op0=ALU.mult, op1=ALU.mult)
                dve.tensor_tensor(ke[b][:, :, 0:w], qk[:, 2:4, t0:t0 + w], enb[:, :, 0:w], ALU.mult)
                dve.tensor_copy(dec[b][:, :, 0:w // c], eb[:, :, c - 1:w:c])
                if s < STEPS:
                    dve.tensor_tensor(ka[b][:, :, :], qk[:, 2:4, t0:t0 + 64], een[:, :, 0:64], ALU.mult)
                    step(dve.tensor_tensor(k2[b][:, :, 64:128], qk[:, 2:4, t0 + 64:t0 + 128], een[:, :, 64:128], ALU.mult))
                    for q in range(2):
                        r = slice(64 * q, 64 * q + 64)
                        dve.tensor_tensor(qi[b][r, :, q, :], qe[b][r, :, q, 64:128],
                                          dec[b][r, :, 0:1].broadcast_to([64, 2, 64]), ALU.mult)
                    dve.tensor_tensor(k2[b][:, :, 0:64], ka[b][:, :, :],
                                      dec[b][:, :, 1:2].broadcast_to([P, 2, 64]), ALU.mult).then_inc(prep_ready, 1)
                else:
                    dve.tensor_tensor(k2[b][:, :, 0:w], qk[:, 2:4, t0:t0 + w], een[:, :, 0:w],
                                      ALU.mult).then_inc(prep_ready, 1)

            def mask(s):
                b = s % 2
                dve.wait_ge(a_done, s + 1)
                if s < STEPS:
                    p3 = ps[3][:, :].rearrange("p (h c) -> p h c", h=4)
                    dve.tensor_tensor(sc[b][0:64, :, :], p3[0:64, :, :],
                                      causal[0:64, :].rearrange("p (o c) -> p o c", o=1).broadcast_to([64, 4, P]), ALU.mult)
                    dve.tensor_tensor(sc[b][64:128, :, 64:128], p3[64:128, :, 64:128],
                                      causal[64:128, 64:128].rearrange("p (o c) -> p o c", o=1).broadcast_to([64, 4, 64]),
                                      ALU.mult).then_inc(sc_ready, 1)
                else:
                    dve.tensor_tensor(sc[b][0:TS, :, 0:TS], ps[3][0:TS, :].rearrange("p (h c) -> p h c", h=4)[:, :, 0:TS],
                                      smask[:, :].rearrange("p (o c) -> p o c", o=1).broadcast_to([TS, 4, TS]),
                                      ALU.mult).then_inc(sc_ready, 1)

            def take(s):
                t0, w = tokens(s)
                b = s % 2
                if s < STEPS:
                    step(dve.tensor_tensor(dec2[:, :], dec[b][:, :, 0], dec[b][:, :, 1], ALU.mult))
                dve.wait_ge(b_done, s + 1)
                dve.tensor_copy(qk[:, :, t0:t0 + w], ps[6][:, :].rearrange("p (h c) -> p h c", h=4)[:, :, 0:w]
                                ).then_inc(o_ready, 1)
                if s < STEPS:
                    for p in range(2):
                        ins = dve.scalar_tensor_tensor(out=s_p[:, p, :], in0=s_p[:, p, :], scalar=dec2[:, p:p + 1],
                                                       in1=ps[7][:, p * DV:p * DV + DV], op0=ALU.mult, op1=ALU.add)
                    ins.then_inc(kv_read, 1)

            def gelu(m):
                c, (c0, cn) = m // 3, CH[m % 3]
                a, b = gx[m % 2][:, 0:cn], gt[m % 2][:, 0:cn]
                dve.wait_ge(tanh_ready, m + 1)
                step(dve.scalar_tensor_tensor(out=b, in0=b, scalar=1.0, in1=a, op0=ALU.add, op1=ALU.mult))
                dve.scalar_tensor_tensor(out=xr[:, c, c0:c0 + cn], in0=b, scalar=0.5, in1=xr[:, c, c0:c0 + cn],
                                         op0=ALU.mult, op1=ALU.mult).then_inc(gelu_done, 1)

            def spread_v(h):
                dve.tensor_tensor(vb[0:TS, :, :],
                                  vt[STEPS % 2][0:TS, h * DV:(h + 1) * DV].rearrange("p (o v) -> p o v", o=1).broadcast_to([TS, NB, DV]),
                                  bmask[:, :].rearrange("p (b o) -> p b o", o=1).broadcast_to([TS, NB, DV]),
                                  ALU.mult).then_inc(vb_ready, 1)

            spread(0)
            prep(0)
            for m in range(12):
                if m + 1 <= STEPS:
                    if m:
                        dve.wait_ge(prep_ready, m + 1)
                    spread(m + 1)
                if m <= STEPS:
                    mask(m)
                if 1 <= m <= STEPS + 1:
                    take(m - 1)
                if m + 1 <= STEPS:
                    prep(m + 1)
                if m >= 2:
                    gelu(m - 2)
                if m == 9:
                    for h in range(4):
                        if h:
                            dve.wait_ge(kv_done, h)
                        spread_v(h)
                        if h % 2:
                            p = h // 2
                            dve.wait_ge(kv_done, h + 1)
                            for q in range(NB):
                                ins = dve.scalar_tensor_tensor(
                                    out=s_s[:, p, q, :], in0=s_s[:, p, q, :], scalar=dec[STEPS % 2][:, p, q:q + 1],
                                    in1=ps[3 if q < 4 else 7][:, (q % 4) * DV:(q % 4 + 1) * DV], op0=ALU.mult, op1=ALU.add)
                            ins.then_inc(kv_read, 1)
            gelu(10)
            gelu(11)

            for h in range(4):
                dve.wait_ge(rs_ready, h + 1)
                dve.scalar_tensor_tensor(out=qk[:, h, :], in0=qk[:, h, :], scalar=gn[:, 0:1], in1=rs[:, :],
                                         op0=ALU.mult, op1=ALU.mult).then_inc(o_normed, 1)
                dve.wait_ge(o_normed, h + 1)
                for k, (c0, cn) in enumerate(CH):
                    u = 3 * h + k
                    dve.wait_ge(sg_ready, u + 1)
                    dve.tensor_tensor(qk[:, h, c0:c0 + cn], qk[:, h, c0:c0 + cn], sg[u % 2][:, 0:cn],
                                      ALU.mult).then_inc(yg_ready, 1)
            for i in range(NT):
                t0, w = tokens(i)
                dve.wait_ge(y_high, 2 * i + 1)
                dve.tensor_tensor(act_l[:, 0:4, t0:t0 + w], qk[:, :, t0:t0 + w],
                                  act_h[:, 0:4, t0:t0 + w].bitcast(F32), ALU.subtract).then_inc(y_low, 1)

            def out_read(i, half):
                w = tokens(i)[1]
                n = half * NT + i
                dve.wait_ge(x_loaded[i], 32)
                dve.wait_ge(op_done, n + 1)
                r = rows[0:w, i, half * 512:half * 512 + 512]
                ins = dve.scalar_tensor_tensor(out=r, in0=r, scalar=ALPHA, in1=ps[out_bank(n)][0:w, :],
                                               op0=ALU.mult, op1=ALU.add)
                ins.then_inc(op_read, 1)

            def norm_a(i):
                w = tokens(i)[1]
                st, m = stats[i % 2], mv[i % 2]
                for half in range(2):
                    ins = dve.bn_stats(st[0:w, half, :], rows[0:w, i, half * 512:half * 512 + 512])
                step(ins)
                step(dve.bn_aggr(m[0:w, 0:2], st[0:w, :, :]))
                step(dve.tensor_scalar(m[0:w, 1:2], m[0:w, 1:2], LN_EPS, None, ALU.add))
                dve.reciprocal(m[0:w, 1:2], m[0:w, 1:2]).then_inc(var_ready, 1)

            def norm_b(i, base, ln):
                w = tokens(i)[1]
                m = mv[i % 2]
                dve.wait_ge(std_ready, base + i + 1)
                r = rows[0:w, i, :]
                step(dve.tensor_scalar(r, r, m[0:w, 0:1], m[0:w, 1:2], ALU.subtract, ALU.mult))
                dve.tensor_tensor(r, r, ln[0:w, 0, :], ALU.mult).then_inc(ln_z, 1)

            for i in range(NT):
                out_read(i, 0)
            dve.wait_ge(ln1_loaded, 32)
            for i in range(NT):
                out_read(i, 1)
                dve.wait_ge(op_read, NT + i + 1)
                norm_a(i)
                norm_b(i, 0, ln1)
                if i >= 1:
                    turn_low(2 * NT + 2 * (i - 1))
                    turn_low(2 * NT + 2 * (i - 1) + 1)
            turn_low(4 * NT - 2)
            turn_low(4 * NT - 1)

            def ffn(g, last):
                for u in range(6):
                    j, k = u // 3, u % 3
                    c0, cn = CH[k]
                    dve.wait_ge(silu_ready, g * 6 + (u + 1))
                    dve.wait_ge(up_done, g * 6 + (u + 1))
                    dve.tensor_tensor(hf[u % 2][:, 0:cn], sl[u % 2][:, 0:cn], ps[2 + u % 2][:, 0:cn],
                                      ALU.mult).then_inc(hid_ready, 1)
                    dve.wait_ge(hid_high, g * 6 + (u + 1))
                    dve.tensor_tensor(hid_l[j][:, c0:c0 + cn], hf[u % 2][:, 0:cn],
                                      hid_h[j][:, c0:c0 + cn].bitcast(F32), ALU.subtract).then_inc(hid_low, 1)
                for i in range(NT):
                    w = tokens(i)[1]
                    for half in range(2):
                        n = 2 * i + half
                        dve.wait_ge(down_done, g * (2 * NT) + (n + 1))
                        r = rows[0:w, i, half * 512:half * 512 + 512]
                        dve.scalar_tensor_tensor(out=r, in0=r, scalar=res[0:w, bass.ds(g, 1)], in1=ps[4 + n % 4][0:w, :],
                                                 op0=ALU.mult, op1=ALU.add).then_inc(down_read, 1)
                    if last:
                        dve.wait_ge(down_read, g * (2 * NT) + (n + 1))
                        norm_a(i)
                        norm_b(i, NT, ln2)

            with dve.Fori(0, NG - 1) as g:
                ffn(g, False)
            dve.wait_ge(ln2_loaded, 32)
            ffn(NG - 1, True)

        @block.tensor
        def _(pe):
            def turn(n, rows_t, w):
                g = n % 2
                if n >= 4:
                    pe.wait_ge(turned_low, n - 3)
                for c in range(4):
                    f = (4 * g + c) * P
                    ins = pe.transpose(ps[3 + n % 4][:, c * P:c * P + w], rows_t[0:w, f:f + P], ident[0:w, 0:w])
                ins.then_inc(turned, 1)

            def split_product(out, terms):
                last = len(terms) - 1
                for c, (sh, sl_, mh, ml) in enumerate(terms):
                    pe.matmul(out, sh, mh, start=(c == 0), stop=False)
                    pe.matmul(out, sh, ml, start=False, stop=False)
                    ins = pe.matmul(out, sl_, mh, start=False, stop=(c == last))
                return ins

            def project(n, slot, k, width=P):
                c0, cn = CH[k]
                if k == 0:
                    pe.wait_ge(w_low, n + 1)
                if not isinstance(n, int) or n >= 1:
                    if isinstance(n, int) and n > N_GR:
                        m = 3 * (n - 1 - N_GR) + k
                        if m < 12:
                            pe.wait_ge(gx_ready, m + 1)
                        else:
                            pe.wait_ge(sg_ready, m - 12 + 1)
                    else:
                        pe.wait_ge(in_read, n * 3 + (k - 2))
                split_product(ps[k][0:width, 0:cn],
                              [(wh[slot % 2][:, c, 0:width], wl[slot % 2][:, c, 0:width],
                                act_h[:, c, c0:c0 + cn], act_l[:, c, c0:c0 + cn]) for c in range(KC)]
                              ).then_inc(in_done, 1)

            pe.wait_ge(consts_made, 1)
            for i in range(NT):
                w = tokens(i)[1]
                pe.wait_ge(x_loaded[i], 16)
                for g in range(2):
                    turn(2 * i + g, x_in[:, i, :], w)
            pe.wait_ge(state_loaded, 32)
            pe.wait_ge(params_loaded, 16 * 8)
            for c in range(4):
                pe.transpose(ps[7][:, c * 32:c * 32 + 32], st_rows[0:32, c * P:(c + 1) * P], ident[0:32, 0:32])
            ins = pe.transpose(ps[7][:, P:P + 35], par_rows[:, :], ident[0:35, 0:35])
            ins.then_inc(states_turned, 1)
            pe.wait_ge(turned_low, 2 * NT)
            for k in range(3):
                project(N_Z, N_Z, k, RANK)
            pe.wait_ge(in_read, 3)
            
            pe.wait_ge(states_read, 1)
            for u in range(6):
                p, k = u // 3, u % 3
                c0, cn = CH[k]
                if u == 5:
                    pe.wait_ge(zg_read, 1)
                pe.matmul(ps[3 + u % 5][:, 0:cn], wgate[:, p, :], z[:, c0:c0 + cn], start=True, stop=True
                          ).then_inc(zg_done, 1)
            with pe.Fori(0, 2) as i:
                for j in range(2):
                    for k in range(3):
                        project(i * 2 + (N_XR + j), N_XR + j, k)

            pe.wait_ge(zg_read, 6)

            def gates(ch, k):
                c0, cn = CH[k]
                if k == 0:
                    pe.wait_ge(conv_ready, ch + 1)
                else:
                    pe.wait_ge(gates_read, ch * 3 + k)
                pe.matmul(ps[3][:, 0:cn], gw[:, 0, :], xc[:, c0:c0 + cn], start=True, stop=True)
                pe.matmul(ps[4][:, 0:cn], gw[:, 1, :], xc[:, c0:c0 + cn], start=True, stop=True).then_inc(gates_done, 1)

            with pe.Fori(0, 4) as i:
                n = i * 2 + N_QKV
                project(n, N_QKV, 0)
                project(n, N_QKV, 1)
                gates(i, 0)
                project(n, N_QKV, 2)
                gates(i, 1)
                project(n + 1, N_QKV + 1, 0)
                gates(i, 2)
                project(n + 1, N_QKV + 1, 1)
                project(n + 1, N_QKV + 1, 2)

            def scores(s):
                t0, w = tokens(s)
                b = s % 2
                pe.wait_ge(prep_ready, s + 1)
                if s:
                    pe.wait_ge(sc_ready, s)
                    pe.wait_ge(tok_ready, s)
                p3 = ps[3][:, :].rearrange("p (h c) -> p h c", h=4)
                for p in range(2):
                    heads = slice(2 * p, 2 * p + 2)
                    if s < STEPS:
                        pe.matmul(p3[0:64, heads, 0:64], ke[b][:, p, 0:64], qe[b][:, p, :, 0:64], start=True, stop=True)
                        pe.matmul(p3[0:64, heads, 64:128], ka[b][:, p, :], qe[b][:, p, :, 64:128], start=True, stop=True)
                        pe.matmul(p3[64:128, heads, 64:128], ke[b][:, p, 64:128], qe[b][:, p, :, 64:128],
                                  start=True, stop=True)
                    else:
                        pe.matmul(p3[0:w, heads, 0:w], ke[b][:, p, 0:w], qe[b][:, p, :, 0:w], start=True, stop=True)
                for p in range(2):
                    pe.transpose(ps[4][0:w, p * P:(p + 1) * P], k2[b][:, p, 0:w], ident[:, :])
                for h in range(4):
                    ins = pe.transpose(ps[5][0:w, h * DV:(h + 1) * DV], v[:, h, t0:t0 + w], ident[:, :])
                ins.then_inc(a_done, 1)

            def attend(s):
                w = tokens(s)[1]
                b = s % 2
                pe.wait_ge(sc_ready, s + 1)
                pe.wait_ge(tok_ready, s + 1)
                if s:
                    pe.wait_ge(o_ready, s)
                    pe.wait_ge(kv_read, s)
                if s == STEPS:
                    pe.wait_ge(gla_state_loaded, 32)
                for h in range(4):
                    p, q = h // 2, h % 2
                    o = ps[6][:, h * P:h * P + w]
                    pe.matmul(o, vt[b][0:w, h * DV:(h + 1) * DV], sc[b][0:w, h, 0:w], start=True, stop=False)
                    if s < STEPS:
                        pe.matmul(ps[6][:, h * P:h * P + 64], s_p[:, p, :], qe[b][:, p, q, 0:64], start=False, stop=False)
                        ins = pe.matmul(ps[6][:, h * P + 64:h * P + 128], s_p[:, p, :], qi[b][:, p, q, :],
                                        start=False, stop=True)
                    else:
                        for e in range(NB):
                            ins = pe.matmul(ps[6][:, h * P + e * LS:h * P + (e + 1) * LS], s_s[:, p, e, :],
                                            qe[b][:, p, q, e * LS:(e + 1) * LS], start=False, stop=(e == NB - 1))
                if s < STEPS:
                    for h in range(4):
                        p, q = h // 2, h % 2
                        ins = pe.matmul(ps[7][64 * q:64 * q + 64, p * DV:(p + 1) * DV],
                                        k2t[b][:, h * DK:(h + 1) * DK], vt[b][:, h * DV:(h + 1) * DV],
                                        start=True, stop=True)
                ins.then_inc(b_done, 1)

            def sample_kv():
                for h in range(4):
                    p, q = h // 2, h % 2
                    pe.wait_ge(vb_ready, h + 1)
                    if h == 2:
                        pe.wait_ge(kv_read, STEPS + 1)
                    for e, bank in enumerate((3, 7)):
                        ins = pe.matmul(ps[bank][64 * q:64 * q + 64, :], k2t[STEPS % 2][0:TS, h * DK:(h + 1) * DK],
                                        vb[0:TS, 4 * e:4 * e + 4, :], start=True, stop=True)
                    ins.then_inc(kv_done, 1)

            for m in range(12):
                project(N_GR + m // 3, N_GR + m // 3, m % 3)
                if m <= STEPS:
                    scores(m)
                if 1 <= m <= STEPS + 1:
                    attend(m - 1)
                if m == 10:
                    sample_kv()
            pe.wait_ge(h_ready, 4)
            for c in range(4):
                ins = pe.transpose(ps[4][0:36, c * P:(c + 1) * P], st_out[:, c, :], ident[:, :])
            ins.then_inc(states_back, 1)

            def mean_square(h):
                pe.wait_ge(sq_ready, h + 1)
                if h:
                    pe.wait_ge(rs_ready, h)
                for k, (c0, cn) in enumerate(CH):
                    pe.matmul(ps[3 + k][:, 0:cn], ones[:, :], sq[:, c0:c0 + cn], start=True, stop=True
                              ).then_inc(ms_done, 1)

            for h in range(4):
                for k in range(3):
                    project(N_G + h, N_G + h, k)
                    if k == 0 and h == 0:
                        pe.wait_ge(states_rows, 1)
                        mean_square(0)
                    if k == 2 and h < 3:
                        mean_square(h + 1)

            for half in range(2):
                pe.wait_ge(w_low, N_WO + 4 * half + 4)
                for i in range(NT):
                    t0, w = tokens(i)
                    n = half * NT + i
                    if n == 0:
                        pe.wait_ge(sg_ready, 12)
                    if half == 0:
                        pe.wait_ge(y_low, i + 1)
                        pe.wait_ge(y_low2, i + 1)
                    if n == 8:
                        pe.wait_ge(op_read, 1)
                    elif n >= NT:
                        pe.wait_ge(op_read, NT if n < NT + 4 else n - 3)
                    split_product(ps[out_bank(n)][0:w, :],
                                  [(act_h[:, c, t0:t0 + w], act_l[:, c, t0:t0 + w], wo_h[half][:, c, :], wo_l[half][:, c, :])
                                   for c in range(KC)]).then_inc(op_done, 1)
                    if half and i >= 2:
                        pe.wait_ge(ln_done, i - 1)
                        for g in range(2):
                            turn(2 * NT + 2 * (i - 2) + g, rows[:, i - 2, :], tokens(i - 2)[1])
            for i in (NT - 2, NT - 1):
                pe.wait_ge(ln_done, i + 1)
                for g in range(2):
                    turn(2 * NT + 2 * i + g, rows[:, i, :], tokens(i)[1])
            pe.wait_ge(turned_low, 4 * NT)
            pe.wait_ge(op_read, 2 * NT)

            def ffn(g, first=False):
                for u in range(6):
                    j, k = u // 3, u % 3
                    c0, cn = CH[k]
                    for m, done in enumerate((gate_done, up_done)):
                        if k == 0:
                            pe.wait_ge(w_low, g * 6 + (N_FFN + 3 * j + m + 1))
                        if not (first and u < 2):
                            pe.wait_ge(silu_ready if m == 0 else hid_ready, g * 6 + (u - 1))
                        split_product(ps[2 * m + u % 2][:, 0:cn],
                                      [(gu_h[m][j][:, c, :], gu_l[m][j][:, c, :], act_h[:, c, c0:c0 + cn],
                                        act_l[:, c, c0:c0 + cn]) for c in range(KC)]).then_inc(done, 1)
                pe.wait_ge(w_low, g * 6 + (N_FFN + 6))
                for i in range(NT):
                    t0, w = tokens(i)
                    pe.wait_ge(hid_low, g * 6 + (4 + chunk_of(i)))
                    for half in range(2):
                        n = 2 * i + half
                        cols = slice(half * 512, half * 512 + 512)
                        if not (first and n < 4):
                            pe.wait_ge(down_read, g * (2 * NT) + (n - 3))
                        split_product(ps[4 + n % 4][0:w, :],
                                      [(hid_h[j][:, t0:t0 + w], hid_l[j][:, t0:t0 + w], wd_h[j][:, cols], wd_l[j][:, cols])
                                       for j in range(2)]).then_inc(down_done, 1)

            ffn(0, True)
            with pe.Fori(1, NG) as g:
                ffn(g)


_INS = ["x_prompt", "x_sample", "state_gla", "state_rglru", "state_conv", "w_in", "gla_w_gate", "gla_b_gate",
        "gla_norm_g", "rg_conv_w", "rg_conv_b", "rg_w_a", "rg_b_a", "rg_w_x", "rg_b_x", "rg_lambda", "w_out",
        "ln1_g", "ln1_b", "ffn_w_gate", "ffn_w_up", "ffn_w_down", "ln2_g", "ln2_b"]
_OUTS = [(1, 1024, 1024), (8, 8, 1024), (1, 1, 4, 64, 128), (1, 1, 512), (1, 1, 3, 512),
         (1, 8, 4, 64, 128), (1, 8, 512), (1, 8, 3, 512)]


def kernel(**inputs):
    import numpy as _np
    import concourse.bacc as _bacc
    from concourse.bass_utils import run_bass_kernel_spmd as _run

    nc = _bacc.Bacc("TRN2", target_bir_lowering=False, num_devices=1)
    arrays, args = {}, []
    for name in _INS:
        a = _np.ascontiguousarray(inputs[name])
        arrays[f"in_{name}"] = a
        args.append(nc.dram_tensor(f"in_{name}", a.shape, mybir.dt.from_np(a.dtype), kind="ExternalInput").ap())
    for i, shape in enumerate(_OUTS):
        args.append(nc.dram_tensor(f"out_{i}", shape, F32, kind="ExternalOutput").ap())
    build(nc, *args)
    r = _run(nc, [arrays], core_ids=[0])
    return tuple(r.results[0][f"out_{i}"] for i in range(len(_OUTS)))
```

```python
from contextlib import ExitStack

import concourse.bass as bass
from concourse import mybir

F32 = mybir.dt.float32
F32R = mybir.dt.float32r
ACT = mybir.ActivationFunctionType
ALU = mybir.AluOpType

P = 128
D = 1024
KC = D // P
TP = 1024
NB, LS = 8, 8
TS = NB * LS
T = TP + TS
NT = -(-T // P)
CH = [(0, 3 * P), (3 * P, 3 * P), (6 * P, T - 6 * P)]
CW = CH[0][1]
F = 2816
NF = F // P
NG = NF // 2
DK, DV, CHUNK = 64, 128, 64
STEPS = TP // P
RANK = 16
COL_Q, COL_G, COL_Z, COL_XR, COL_GR = 0, 1024, 1536, 1552, 2064
ALPHA = 2.0 ** 0.25
LN_EPS, RMS_EPS = 1e-5, 1e-6

N_Z, N_XR, N_QKV, N_GR, N_G, N_WO, N_FFN = 0, 1, 5, 13, 17, 21, 29


def tokens(i):
    return i * P, min(P, T - i * P)


def chunk_of(i):
    return i // 3


def out_bank(n):
    return n % 8 if n < NT else (7, 0, 1, 2)[(n - NT) % 4]


def units(last):
    return [(j, k) for k in range(3) for j in range(2)] if last else [(j, k) for j in range(2) for k in range(3)]


LAST_DOWN = {2: (0, 1, 2), 4: (3, 4, 5), 5: (6, 7, 8)}


WO_EARLY = 4
Z_AFTER = (3, 6, NT - 1)


class Steps:

    def __init__(self, eng, sem):
        self.eng, self.sem, self.base, self.k = eng, sem, 0, 0

    def __call__(self, ins):
        ins.then_inc(self.sem, 1)
        self.k += 1
        self.eng.wait_ge(self.sem, self.base + self.k)

    def enter(self, i, per):
        self.saved, self.per = self.base + self.k, per
        self.base, self.k = i * per + self.saved, 0

    def leave(self, n):
        assert self.k == self.per, (self.k, self.per)
        self.base, self.k = self.saved + n * self.per, 0


def build(nc, x_prompt, x_sample, state_gla, state_rglru, state_conv, w_in, gla_w_gate, gla_b_gate,
          gla_norm_g, rg_conv_w, rg_conv_b, rg_w_a, rg_b_a, rg_w_x, rg_b_x, rg_lambda, w_out,
          ln1_g, ln1_b, ffn_w_gate, ffn_w_up, ffn_w_down, ln2_g, ln2_b,
          y_prompt, y_sample, gla_p, rg_p, conv_p, gla_s, rg_s, conv_s):
    ctx = ExitStack()
    with ctx:
        def at(name, shape, offset, dt=F32):
            return nc.alloc_sbuf_tensor_at(name, shape, dt, offset=BASE + offset)

        def sem(name):
            return ctx.enter_context(nc.semaphore(name))

        BASE = 16512
        TB = T * 4
        R_HIGH, R_LOW = 0, 8 * TB
        R_OHS = 16 * TB
        R_X = R_OHS + NT * 4096
        R_G = R_X + 32768
        R_RING = R_G + 45056
        R_RAW = R_RING + 4 * TB
        R_CONST = R_RAW + 8192

        act_h = at("act_h", [P, KC, T], R_HIGH, F32R)
        act_l = at("act_l", [P, KC, T], R_LOW, F32R)
        qk = at("qk", [P, 4, T], R_OHS)
        xr = at("xr", [P, 4, T], R_OHS + 4 * TB)
        rows = at("rows", [P, NT, D], R_OHS)
        v = at("v", [P, 4, T], R_X)
        soft = at("soft", [P, 2, T], R_X)
        z = at("z", [RANK, T], R_X + 2 * TB)
        cum = at("cum", [P, 2, T], R_X + 4 * TB)
        m01 = at("m01", [P, T], R_X + 6 * TB)
        gw = at("gw", [P, 2, P], R_X + 7 * TB)
        x_in = at("x_in", [P, NT, D], R_G)
        xc, t1, t2, tn = (at(n, [P, T], R_G + j * TB) for j, n in enumerate(("xc", "t1", "t2", "tn")))
        gw4 = at("gw4", [P, 4, 2, P], R_G + 4 * TB)
        g_at = [R_G]

        def gla(name, shape, bufs=1):
            size = 4
            for s in shape[1:]:
                size *= s
            out = []
            for b in range(bufs):
                out.append(at(f"{name}{b}", shape, g_at[0]))
                g_at[0] += -(-size // 32) * 32
            return out

        ke = gla("ke", [P, 2, P], 2)
        ka = gla("ka", [P, 2, CHUNK], 2)
        k2 = gla("k2", [P, 2, P], 2)
        k2t = gla("k2t", [P, 2 * P], 2)
        vt = gla("vt", [P, 4 * DV], 2)
        gx = gla("gx", [P, CW], 2)
        gt = gla("gt", [P, CW], 2)
        g_at[0] = R_G + 4 * TB
        eb, enb, een = gla("eb", [P, 2, P])[0], gla("enb", [P, 2, P])[0], gla("een", [P, 2, P])[0]
        g_at[0] = R_G + 4 * TB + 4096
        qe = gla("qe", [P, 2, 2, P], 2)
        qi = gla("qi", [P, 2, 2, CHUNK], 2)
        sc = gla("sc", [P, 4, P], 2)
        s_p = gla("s_p", [P, 2, DV])[0]
        s_s = gla("s_s", [P, 2, NB, DV])[0]
        vb = [*gla("vb", [P, NB, DV]),
              at("vb1", [P, NB, DV], R_X + 6 * TB)]
        assert g_at[0] <= R_RING, (g_at[0], R_RING)
        sq = at("sq", [P, T], R_X + 8192)
        sg = [at(f"sg{b}", [P, CW], R_X + 8192 + TB + b * CW * 4) for b in range(2)]
        rs = at("rs", [P, T], R_X + 24576)
        wh = [at(f"wh{b}", [P, KC, P], R_RING + b * 8192, F32R) for b in range(2)]
        wl = [at(f"wl{b}", [P, KC, P], R_RING + b * 8192 + 4096, F32R) for b in range(2)]
        raw = [at(f"raw{b}", [P, 1024], R_RAW + b * 4096) for b in range(2)]
        wo_h = [at(f"wo_h{b}", [P, KC, 512], r, F32R) for b, r in enumerate((R_G, R_X))]
        wo_l = [at(f"wo_l{b}", [P, KC, 512], r + 16384, F32R) for b, r in enumerate((R_G, R_X))]
        ln1 = at("ln1", [P, 2, D], R_G + 32768)
        gu_h = [[at(f"gu_h{m}{b}", [P, KC, P], R_G + m * 16384 + b * 8192, F32R) for b in range(2)] for m in range(2)]
        gu_l = [[at(f"gu_l{m}{b}", [P, KC, P], R_G + m * 16384 + b * 8192 + 4096, F32R) for b in range(2)]
                for m in range(2)]
        wd_h = [at(f"wd_h{b}", [P, D], R_X + b * 8192, F32R) for b in range(2)]
        wd_l = [at(f"wd_l{b}", [P, D], R_X + b * 8192 + 4096, F32R) for b in range(2)]
        ln2 = at("ln2", [P, 2, D], R_X + 16384)
        sl = [at(f"sl{b}", [P, CW], R_X + 24576 + b * CW * 4) for b in range(2)]
        hf = [at(f"hf{b}", [P, CW], R_X + 24576 + (2 + b) * CW * 4) for b in range(2)]
        hid_h = [at(f"hid_h{b}", [P, T], R_RING + b * TB, F32R) for b in range(2)]
        hid_l = [at(f"hid_l{b}", [P, T], R_RING + (2 + b) * TB, F32R) for b in range(2)]
        c_at = [R_CONST]

        def const(name, shape):
            size = 4
            for s in shape[1:]:
                size *= s
            out = at(name, shape, c_at[0])
            c_at[0] += -(-size // 32) * 32
            return out

        ident = const("ident", [P, P])
        causal = const("causal", [P, P])
        smask = const("smask", [TS, TS])
        ones = const("ones", [P, P])
        bmask = const("bmask", [TS, NB])
        par = const("par", [P, 35])
        cw = par[:, 0:16].rearrange("p (j c) -> p j c", j=4)
        cb, ba, bx, lam = (par[:, 16 + 4 * j:20 + 4 * j] for j in range(4))
        bg, gn = par[:, 32:34], par[:, 34:35]
        pk = const("pk", [P, 4, 4])
        hba, hbx, kp, kn = (pk[:, :, j] for j in range(4))
        cur = const("cur", [P, 4])
        e0, e1, e2, e3 = (const(n, [P, 4]) for n in ("e0", "e1", "e2", "e3"))
        eps = const("eps", [P, 1])
        res = const("res", [P, NG])
        dec = [const(f"dec{b}", [P, 2, NB]) for b in range(2)]
        dec2 = const("dec2", [P, 2])
        stats = [const(f"stats{b}", [P, 2, 6]) for b in range(2)]
        mv = [const(f"mv{b}", [P, 4]) for b in range(2)]
        wgate = at("wgate", [RANK, 2, P], R_X + 7 * TB + 1024)
        assert c_at[0] <= 229344 - BASE, c_at[0] - (229344 - BASE)
        st_in = at("st_in", [P, 4, 32], R_OHS + 8 * TB)
        st_out = at("st_out", [P, 4, 36], R_OHS + 8 * TB + 512)
        st_rows = at("st_rows", [36, 512], R_X)

        par_rows = at("par_rows", [35, P], R_X + 2048)
        ps = [ctx.enter_context(nc.psum_tensor(f"ps{b}", [P, 512], F32)) for b in range(8)]

        x_loaded = [sem(f"x_loaded{i}") for i in range(NT)]
        raw_loaded = [sem("raw_loaded0"), sem("raw_loaded1")]
        params_loaded, gw_loaded, state_loaded = sem("params_loaded"), sem("gw_loaded"), sem("state_loaded")
        gla_state_loaded, ln1_loaded, ln2_loaded = sem("gla_state_loaded"), sem("ln1_loaded"), sem("ln2_loaded")
        out_stored, states_stored = sem("out_stored"), sem("states_stored")
        ident_made, consts_made, gw_zeroed = sem("ident_made"), sem("consts_made"), sem("gw_zeroed")
        turned, turned_high, turned_low = sem("turned"), sem("turned_high"), sem("turned_low")
        w_high, w_low = sem("w_high"), sem("w_low")
        in_done, in_read = sem("in_done"), sem("in_read")
        zg_done, zg_read, soft_ready, cum_ready = sem("zg_done"), sem("zg_read"), sem("soft_ready"), sem("cum_ready")
        states_turned, states_read = sem("states_turned"), sem("states_read")
        states_back, states_rows = sem("states_back"), sem("states_rows")
        dve_step, act_step, pool_step = sem("dve_step"), sem("act_step"), sem("pool_step")
        lam_abs, lam_ready = sem("lam_abs"), sem("lam_ready")
        conv_ready, gates_done, gates_read = sem("conv_ready"), sem("gates_done"), sem("gates_read")
        decay_ready, room_ready, root_ready, h_ready = sem("decay_ready"), sem("room_ready"), sem("root_ready"), sem("h_ready")
        d_ready, exp_ready, prep_ready = sem("d_ready"), sem("exp_ready"), sem("prep_ready")
        a_done, b_done, tok_ready, sc_ready, o_ready = (sem(n) for n in ("a_done", "b_done", "tok_ready", "sc_ready", "o_ready"))
        vb_ready, kv_done, kv_read = sem("vb_ready"), sem("kv_done"), sem("kv_read")
        gx_ready, poly_ready, tanh_ready, gelu_done = (sem(n) for n in ("gx_ready", "poly_ready", "tanh_ready", "gelu_done"))
        sq_ready, ms_done, rs_ready, o_normed, sg_ready, yg_ready = (
            sem(n) for n in ("sq_ready", "ms_done", "rs_ready", "o_normed", "sg_ready", "yg_ready"))
        y_high, yr_high, y_low, y_low2 = sem("y_high"), sem("yr_high"), sem("y_low"), sem("y_low2")
        op_done, op_read = sem("op_done"), sem("op_read")
        var_ready, std_ready, ln_z, ln_scaled, ln_done = (
            sem(n) for n in ("var_ready", "std_ready", "ln_z", "ln_scaled", "ln_done"))
        gate_done, up_done, silu_ready, hid_ready, hid_high, hid_low = (
            sem(n) for n in ("gate_done", "up_done", "silu_ready", "hid_ready", "hid_high", "hid_low"))
        down_done, down_read = sem("down_done"), sem("down_read")

        w_in_v = w_in.rearrange("l (c p) n -> p (l c) n", p=P)
        w_out_v = w_out.rearrange("l (c p) n -> p (l c) n", p=P)
        w_gu_v = [w.rearrange("l (c p) n -> p (l c) n", p=P) for w in (ffn_w_gate, ffn_w_up)]
        w_dn_v = ffn_w_down.rearrange("l f n -> (l f) n")
        xp_v = x_prompt.rearrange("b t d -> (b t) d")
        xs_v = x_sample.rearrange("b t d -> (b t) d")
        yp_v = y_prompt.rearrange("b t d -> (b t) d")
        ys_v = y_sample.rearrange("b t d -> (b t) d")

        def raw3(n, c=KC):
            return raw[n % 2][:, :].rearrange("p (c n) -> p c n", c=c)

        block = ctx.enter_context(nc.Block())

        @block.sync
        def _(sp):
            def x_rows(i):
                return xp_v[i * P:(i + 1) * P, :] if i < NT - 1 else xs_v

            def piece(n, slot, src, dst=None):
                if not isinstance(n, int) or n >= 2:
                    sp.wait_ge(w_low, n - 1)
                sp.dma_start(raw3(slot) if dst is None else dst, src).then_inc(raw_loaded[slot % 2], 16)

            def w_in_tile(col):
                return w_in_v[:, :, bass.ds(col, P)]

            sp.dma_start(x_in[:, 0, :], x_rows(0)).then_inc(x_loaded[0], 16)
            piece(0, 0, w_in_v[:, :, COL_Z:COL_Z + RANK], raw[0][:, 0:KC * RANK].rearrange("p (c n) -> p c n", c=KC))
            for i in range(1, 4):
                sp.dma_start(x_in[:, i, :], x_rows(i)).then_inc(x_loaded[i], 16)
            piece(1, 1, w_in_tile(COL_XR))
            for i in range(4, NT):
                w = tokens(i)[1]
                sp.dma_start(x_in[0:w, i, :], x_rows(i)).then_inc(x_loaded[i], 16)
            for n in range(2, 5):
                piece(n, n, w_in_tile(COL_XR + (n - 1) * P))
            sp.wait_ge(gw_zeroed, 1)
            for c in range(4):
                for m, w in enumerate((rg_w_a, rg_w_x)):
                    for q in range(2):
                        sp.dma_start(gw4[q * 64:q * 64 + 64, c, m, q * 64:q * 64 + 64],
                                     w[0, 2 * c + q]).then_inc(gw_loaded, 16)
            for p in range(2):
                sp.dma_start(s_s[:, p, :, :], state_gla[0, :, 2 * p:2 * p + 2].rearrange("b q d v -> (q d) b v")
                             ).then_inc(gla_state_loaded, 16)
            with sp.Fori(0, 4) as i:
                for j in range(2):
                    piece(i * 2 + (N_QKV + j), N_QKV + j, w_in_tile(i * 256 + (COL_Q + j * P)))
            for j in range(4):
                piece(N_GR + j, N_GR + j, w_in_tile(COL_GR + j * P))
            for j in range(2):
                piece(N_G + j, N_G + j, w_in_tile(COL_G + j * P))
            sp.wait_ge(states_rows, 1)
            sp.dma_start(conv_p[0, 0], st_rows[0:3, :]).then_inc(states_stored, 16)
            sp.dma_start(conv_s.rearrange("l b w c -> (l b w) c"), st_rows[3:27, :]).then_inc(states_stored, 16)
            sp.dma_start(rg_p[0], st_rows[27:28, :]).then_inc(states_stored, 16)
            sp.dma_start(rg_s[0], st_rows[28:36, :]).then_inc(states_stored, 16)
            for j in range(2, 4):
                piece(N_G + j, N_G + j, w_in_tile(COL_G + j * P))
            sp.wait_ge(kv_read, STEPS + 2)
            sp.dma_start(gla_p[0, 0].rearrange("(p q) d v -> (q d) p v", q=2), s_p[:, :, :]).then_inc(states_stored, 16)
            for p in range(2):
                sp.dma_start(gla_s[0, :, 2 * p:2 * p + 2].rearrange("b q d v -> (q d) b v"),
                             s_s[:, p, :, :]).then_inc(states_stored, 16)
            for m in range(8):
                q = m % 4
                piece(N_WO + m, N_WO + m, w_out_v[:, 2 * q:2 * q + 2, (m // 4) * 512:(m // 4) * 512 + 512],
                      raw3(N_WO + m, 2))
            sp.wait_ge(y_low, NT)
            sp.wait_ge(y_low2, NT)
            for i in range(NT):
                w = tokens(i)[1]
                sp.dma_start(rows[0:w, i, :], x_rows(i)).then_inc(x_loaded[i], 16)
            for j, w in enumerate((ln1_g, ln1_b)):
                sp.dma_start(ln1[:, j, :], w[0:1, :].broadcast_to([P, D])).then_inc(ln1_loaded, 16)

            def ffn_pieces(g):
                for j in range(2):
                    for m in range(2):
                        k = 3 * j + m
                        piece(g * 6 + (N_FFN + k), N_FFN + k, w_gu_v[m][:, :, bass.ds(g * 256 + j * P, P)])
                    k = 3 * j + 2
                    piece(g * 6 + (N_FFN + k), N_FFN + k, w_dn_v[bass.ds(g * 256 + j * P, P), :],
                          raw[(N_FFN + k) % 2][:, :])

            ffn_pieces(0)
            for j, w in enumerate((ln2_g, ln2_b)):
                sp.dma_start(ln2[:, j, :], w[0:1, :].broadcast_to([P, D])).then_inc(ln2_loaded, 16)
            with sp.Fori(1, NG) as g:
                ffn_pieces(g)
            for i in range(NT):
                sp.wait_ge(ln_done, NT + i + 1)
                w = tokens(i)[1]
                dst = yp_v[i * P:(i + 1) * P, :] if i < NT - 1 else ys_v
                sp.dma_start(dst, rows[0:w, i, :]).then_inc(out_stored, 16)
            sp.wait_ge(out_stored, 16 * NT)
            sp.wait_ge(states_stored, 16 * 7)

        @block.gpsimd
        def _(pool):
            step = Steps(pool, pool_step)
            step(pool.memset(ident[:, :], 1.0))
            pool.affine_select(out=ident[:, :], in_=ident[:, :], compare_op=ALU.is_equal, fill=0.0, base=0,
                               pattern=[[-1, P]], channel_multiplier=1).then_inc(ident_made, 1)
            def low(n, slot, dst, src):
                pool.wait_ge(w_high, n + 1)
                pool.tensor_tensor(dst[0], src, dst[1].bitcast(F32), ALU.subtract).then_inc(w_low, 1)

            def ring_low(n, slot):
                low(n, slot, (wl[slot % 2][:, :, :], wh[slot % 2][:, :, :]), raw3(slot))

            pool.dma_start(par_rows[0:16, :], rg_conv_w.rearrange("l j (c p) -> (l j c) p", p=P)).then_inc(params_loaded, 16)
            for r, src in ((16, rg_conv_b), (20, rg_b_a), (24, rg_b_x), (28, rg_lambda), (32, gla_b_gate), (34, gla_norm_g)):
                n = src.shape[1] // P
                pool.dma_start(par_rows[r:r + n, :], src.rearrange("l (c p) -> (l c) p", p=P)).then_inc(params_loaded, 16)
            pool.dma_start(wgate[:, :, :], gla_w_gate[0].rearrange("r (a n) -> r a n", a=2)).then_inc(params_loaded, 16)
            low(0, 0, (wl[0][:, :, 0:RANK], wh[0][:, :, 0:RANK]),
                raw[0][:, 0:KC * RANK].rearrange("p (c n) -> p c n", c=KC))
            pool.dma_start(st_rows[0:24, :], state_conv[0].rearrange("b w c -> (b w) c")).then_inc(state_loaded, 16)
            pool.dma_start(st_rows[24:32, :], state_rglru[0]).then_inc(state_loaded, 16)
            step(pool.memset(causal[:, :], 1.0))
            step(pool.affine_select(out=causal[:, :], in_=causal[:, :], compare_op=ALU.is_ge, fill=0.0, base=0,
                                    pattern=[[1, P]], channel_multiplier=-1))
            step(pool.affine_select(out=smask[:, :].rearrange("p (b c) -> p b c", b=NB),
                                    in_=causal[0:TS, 0:TS].rearrange("p (b c) -> p b c", b=NB),
                                    compare_op=ALU.is_ge, fill=0.0, base=0,
                                    pattern=[[-LS, NB], [0, LS]], channel_multiplier=1))
            step(pool.memset(bmask[:, :], 1.0))
            step(pool.affine_select(out=bmask[:, :], in_=bmask[:, :], compare_op=ALU.is_ge, fill=0.0, base=0,
                                    pattern=[[-LS, NB]], channel_multiplier=1))
            step(pool.affine_select(out=bmask[:, :], in_=bmask[:, :], compare_op=ALU.is_ge, fill=0.0, base=LS - 1,
                                    pattern=[[LS, NB]], channel_multiplier=-1))
            pool.memset(ones[:, :], 1.0 / DV)
            pool.memset(eps[:, :], RMS_EPS)
            step(pool.memset(m01[:, :], 1.0))
            pool.memset(m01[:, 0:TP:CHUNK], 0.0)
            pool.memset(m01[:, TP:T:LS], 0.0)
            step(pool.memset(res[:, :], 1.0))
            step(pool.memset(res[:, 0:1], ALPHA))
            pool.memset(dec2[:, :], 0.0).then_inc(consts_made, 1)

            with pool.Fori(0, 6) as i:
                for j in range(2):
                    ring_low(i * 2 + (N_XR + j), N_XR + j)

            def gelu_poly(m):
                w = CH[m % 3][1]
                pool.wait_ge(gx_ready, m + 1)
                if m >= 2:
                    pool.wait_ge(gelu_done, m - 1)
                a, b = gx[m % 2][:, 0:w], gt[m % 2][:, 0:w]
                step(pool.tensor_tensor(b, a, a, ALU.mult))
                step(pool.tensor_scalar(b, b, 0.044715, 1.0, ALU.mult, ALU.add))
                pool.tensor_tensor(b, b, a, ALU.mult).then_inc(poly_ready, 1)

            ring_low(N_GR, N_GR)
            for m in range(12):
                if m % 3 == 0:
                    ring_low(N_GR + m // 3 + 1, N_GR + m // 3 + 1)
                gelu_poly(m)
            for j in range(1, 4):
                ring_low(N_G + j, N_G + j)
            def wo_low(m):
                q, b = m % 4, m // 4
                low(N_WO + m, N_WO + m, (wo_l[b][:, 2 * q:2 * q + 2, :], wo_h[b][:, 2 * q:2 * q + 2, :]),
                    raw3(N_WO + m, 2))

            for m in range(WO_EARLY):
                wo_low(m)
            for i in range(NT):
                t0, w = tokens(i)
                pool.wait_ge(yr_high, i + 1)
                pool.tensor_tensor(act_l[:, 4:8, t0:t0 + w], xr[:, :, t0:t0 + w],
                                   act_h[:, 4:8, t0:t0 + w].bitcast(F32), ALU.subtract).then_inc(y_low2, 1)
            for m in range(WO_EARLY, 8):
                wo_low(m)

            def affine(i, ln, base):
                w = tokens(i)[1]
                pool.wait_ge(ln_scaled, base + i + 1)
                pool.tensor_tensor(rows[0:w, i, :], rows[0:w, i, :], ln[0:w, 1, :], ALU.add).then_inc(ln_done, 1)

            def ffn_low(g, k):
                j, m = k // 3, k % 3
                if m < 2:
                    low(g * 6 + (N_FFN + k), N_FFN + k, (gu_l[m][j][:, :, :], gu_h[m][j][:, :, :]), raw3(N_FFN + k))
                else:
                    low(g * 6 + (N_FFN + k), N_FFN + k, (wd_l[j][:, :], wd_h[j][:, :]), raw[(N_FFN + k) % 2][:, :])

            pool.wait_ge(ln1_loaded, 32)
            for i in range(NT):
                affine(i, ln1, 0)
                if i == 5:
                    ffn_low(0, 0)
                    ffn_low(0, 1)
                if i == NT - 2:
                    ffn_low(0, 2)
            for k in range(3, 6):
                ffn_low(0, k)

            with pool.Fori(1, NG) as g:
                for k in range(6):
                    ffn_low(g, k)
            pool.wait_ge(ln2_loaded, 32)
            for i in range(NT):
                affine(i, ln2, NT)

        @block.scalar
        def _(act):
            step = Steps(act, act_step)

            def turn_high(n):
                i, g = n // 2, n % 2
                t0, w = tokens(i % NT)
                act.wait_ge(turned, n + 1)
                act.activation(act_h[:, 4 * g:4 * g + 4, t0:t0 + w],
                               ps[3 + n % 4][:, :].rearrange("p (c t) -> p c t", c=4)[:, :, 0:w],
                               ACT.Copy).then_inc(turned_high, 1)

            def high(n, slot, dst, src, uses):
                act.wait_ge(raw_loaded[slot % 2], uses)
                act.activation(dst, src, ACT.Copy).then_inc(w_high, 1)

            def loads(n, slot):
                return (n - slot % 2) * 8 + 16

            def ring_high(n, slot, wait=True):
                if wait:
                    act.wait_ge(in_done, n * 3 - 3)
                high(n, slot, wh[slot % 2][:, :, :], raw3(slot), loads(n, slot))

            def read(n, k, out, fn=ACT.Copy, also=None):
                c0, cn = CH[k]
                act.wait_ge(in_done, n * 3 + (k + 1))
                ins = act.activation(out, ps[k][:, 0:cn], fn)
                ins.then_inc(in_read, 1)
                return ins

            high(0, 0, wh[0][:, :, 0:RANK], raw[0][:, 0:KC * RANK].rearrange("p (c n) -> p c n", c=KC), 16)
            for n in range(2 * NT):
                turn_high(n)
                if n == 7:
                    high(1, 1, wh[1][:, :, :], raw3(1), 16)
            for k, (c0, cn) in enumerate(CH):
                act.wait_ge(in_done, k + 1)
                act.activation(z[:, c0:c0 + cn], ps[k][0:RANK, 0:cn], ACT.Copy).then_inc(in_read, 1)
            ring_high(2, 2)
            act.wait_ge(states_read, 1)
            act.activation(e0[:, :], lam[:, :], ACT.Abs).then_inc(lam_abs, 1)
            for u in range(6):
                p, k = u // 3, u % 3
                c0, cn = CH[k]
                act.wait_ge(zg_done, u + 1)
                act.activation(cum[:, p, c0:c0 + cn], ps[3 + u % 5][:, 0:cn], ACT.Identity,
                               bias=bg[:, p:p + 1]).then_inc(zg_read, 1)
            act.wait_ge(zg_read, 6)
            step(act.activation(soft[:, :, :], cum[:, :, :], ACT.Abs))
            act.wait_ge(lam_abs, 1)
            act.activation(e0[:, :], e0[:, :], ACT.Exp, scale=-1.0).then_inc(lam_ready, 1)
            step(act.activation(soft[:, :, :], soft[:, :, :], ACT.Exp, scale=-1.0))
            act.activation(soft[:, :, :], soft[:, :, :], ACT.Ln, bias=1.0).then_inc(soft_ready, 1)
            with act.Fori(0, 2) as i:
                for j in range(2):
                    for k, (c0, cn) in enumerate(CH):
                        read(i * 2 + (N_XR + j), k, xr[:, bass.ds(i * 2 + j, 1), c0:c0 + cn])
                    ring_high(i * 2 + (N_XR + j + 2), N_XR + j + 2)

            def rg_tanh(i, k):
                c0, cn = CH[k]
                if k == 0:
                    act.wait_ge(h_ready, i + 1)
                act.wait_ge(gates_done, i * 3 + (k + 1))
                act.activation(t1[:, c0:c0 + cn], ps[3][:, 0:cn], ACT.Tanh, bias=cur[:, 0:1], scale=0.5)
                act.activation(t2[:, c0:c0 + cn], ps[4][:, 0:cn], ACT.Tanh, bias=cur[:, 1:2],
                               scale=0.5).then_inc(gates_read, 1)

            def qkv_body(i, n0, dst):
                ch = i + (n0 - N_QKV) // 2
                n = i * 2 + n0

                def tile(j, k):
                    c0, cn = CH[k]
                    read(n + j, k, dst[:, bass.ds(i * 2 + j, 1), c0:c0 + cn])

                tile(0, 0)
                rg_tanh(ch, 0)
                tile(0, 1)
                rg_tanh(ch, 1)
                tile(0, 2)
                rg_tanh(ch, 2)
                act.wait_ge(gates_read, ch * 3 + 3)
                step(act.activation(tn[:, :], t1[:, :], ACT.Tanh, bias=cur[:, 2:3], scale=cur[:, 2:3]))
                act.activation(t1[:, :], t1[:, :], ACT.Exp, bias=cur[:, 3:4],
                               scale=cur[:, 3:4]).then_inc(decay_ready, 1)
                ring_high(n + 2, n0 + 2)
                tile(1, 0)
                act.wait_ge(room_ready, ch + 1)
                act.activation(tn[:, :], tn[:, :], ACT.Sqrt, scale=-1.0).then_inc(root_ready, 1)
                tile(1, 1)
                tile(1, 2)
                ring_high(n + 3, n0 + 3)

            for n0, dst in ((N_QKV, qk), (N_QKV + 4, v)):
                with act.Fori(0, 2) as i:
                    step.enter(i, 1)
                    qkv_body(i, n0, dst)
                    step.leave(2)

            def exps(s):
                w = tokens(s)[1]
                t0 = tokens(s)[0]
                act.wait_ge(d_ready, s + 1)
                act.activation(een[:, :, 0:w], een[:, :, 0:w], ACT.Exp, scale=1 / 16)
                act.activation(enb[:, :, 0:w], cum[:, :, t0:t0 + w], ACT.Exp, scale=-1 / 16)
                act.activation(eb[:, :, 0:w], cum[:, :, t0:t0 + w], ACT.Exp, scale=1 / 16).then_inc(exp_ready, 1)

            def to_tokens(s):
                w = tokens(s)[1]
                act.wait_ge(a_done, s + 1)
                act.activation(k2t[s % 2][0:w, :], ps[4][0:w, 0:2 * P], ACT.Copy)
                act.activation(vt[s % 2][0:w, :], ps[5][0:w, :], ACT.Copy).then_inc(tok_ready, 1)

            def gelu_tanh(m):
                w = CH[m % 3][1]
                act.wait_ge(poly_ready, m + 1)
                act.activation(gt[m % 2][:, 0:w], gt[m % 2][:, 0:w], ACT.Tanh,
                               scale=0.7978845608028654).then_inc(tanh_ready, 1)

            exps(0)
            for m in range(12):
                n, k = N_GR + m // 3, m % 3
                if m + 1 <= STEPS:
                    exps(m + 1)
                if m >= 2:
                    act.wait_ge(gelu_done, m - 1)
                act.wait_ge(in_done, n * 3 + k + 1)
                act.activation(gx[m % 2][:, 0:CH[k][1]], ps[k][:, 0:CH[k][1]], ACT.Copy).then_inc(gx_ready, 1)
                if k == 2:
                    ring_high(n + 2, n + 2)
                if m <= STEPS:
                    to_tokens(m)
                if m >= 1:
                    gelu_tanh(m - 1)
                if m == STEPS + 1:
                    act.wait_ge(states_back, 1)
                    act.activation(st_rows[:, :], ps[4][0:36, :], ACT.Copy).then_inc(states_rows, 1)
                if m == STEPS + 2:
                    act.wait_ge(o_ready, STEPS + 1)
                    act.activation(sq[:, :], qk[:, 0, :], ACT.Square).then_inc(sq_ready, 1)
            gelu_tanh(11)

            def wo_high(m):
                q, b = m % 4, m // 4
                n = N_WO + m
                high(n, n, wo_h[b][:, 2 * q:2 * q + 2, :], raw3(n, 2), loads(n, n))

            for h in range(4):
                n = N_G + h
                if h:
                    act.wait_ge(o_normed, h)
                for k, (c0, cn) in enumerate(CH):
                    act.wait_ge(ms_done, 3 * h + k + 1)
                    ins = act.activation(rs[:, c0:c0 + cn], ps[3 + k][:, 0:cn], ACT.Ln, bias=eps[:, 0:1])
                step(ins)
                act.activation(rs[:, :], rs[:, :], ACT.Exp, scale=-0.5).then_inc(rs_ready, 1)
                if h < 3:
                    act.activation(sq[:, :], qk[:, h + 1, :], ACT.Square).then_inc(sq_ready, 1)
                if h == 2:
                    act.wait_ge(states_stored, 16 * 7)
                if h >= 2:
                    for m in range(2 * (h - 2), 2 * (h - 2) + 2):
                        wo_high(m)
                for k, (c0, cn) in enumerate(CH):
                    u = 3 * h + k
                    if u >= 2:
                        act.wait_ge(yg_ready, u - 1)
                    act.wait_ge(in_done, n * 3 + k + 1)
                    act.activation(sg[u % 2][:, 0:cn], ps[k][:, 0:cn], ACT.Silu).then_inc(sg_ready, 1)
                    if h == 3:
                        new = range(3 * k, 3 * k + 3)
                        for i in new:
                            t0, w = tokens(i)
                            act.activation(act_h[:, 4:8, t0:t0 + w], xr[:, :, t0:t0 + w], ACT.Copy).then_inc(yr_high, 1)
                        act.wait_ge(yg_ready, u + 1)
                        for i in new:
                            t0, w = tokens(i)
                            act.activation(act_h[:, 0:4, t0:t0 + w], qk[:, :, t0:t0 + w], ACT.Copy).then_inc(y_high, 1)
                if h < 2:
                    ring_high(n + 2, n + 2)
            for m in range(WO_EARLY, 8):
                wo_high(m)

            def ln_scale(i, base):
                w = tokens(i)[1]
                act.wait_ge(var_ready, base + i + 1)
                act.activation(mv[i % 2][0:w, 1:2], mv[i % 2][0:w, 1:2], ACT.Sqrt).then_inc(std_ready, 1)
                act.wait_ge(std_ready, base + i + 1)
                act.wait_ge(ln_z, base + i + 1)
                act.activation(rows[0:w, i, :], rows[0:w, i, :], ACT.Copy, scale=mv[i % 2][0:w, 1:2]).then_inc(ln_scaled, 1)

            def ffn_high(g, k):
                j, m = k // 3, k % 3
                n = g * 6 + (N_FFN + k)
                if m < 2:
                    high(n, N_FFN + k, gu_h[m][j][:, :, :], raw3(N_FFN + k), loads(n, N_FFN + k))
                else:
                    high(n, N_FFN + k, wd_h[j][:, :], raw[(N_FFN + k) % 2][:, :], loads(n, N_FFN + k))

            act.wait_ge(op_done, NT)
            for i in range(NT):
                if i == NT - 1:
                    act.wait_ge(op_done, 2 * NT)
                    ffn_high(0, 2)
                    ffn_high(0, 3)
                ln_scale(i, 0)
                if i == 5:
                    ffn_high(0, 0)
                    ffn_high(0, 1)
                if i >= 1:
                    for n in (2 * (i - 1), 2 * (i - 1) + 1):
                        turn_high(2 * NT + n)

            def silu(g, u, k):
                cn = CH[k][1]
                act.wait_ge(gate_done, g * 6 + (u + 1))
                act.activation(sl[u % 2][:, 0:cn], ps[u % 2][:, 0:cn], ACT.Silu).then_inc(silu_ready, 1)

            def hidden_high(g, u, j, k):
                c0, cn = CH[k]
                act.wait_ge(hid_ready, g * 6 + (u + 1))
                act.activation(hid_h[j][:, c0:c0 + cn], hf[u % 2][:, 0:cn], ACT.Copy).then_inc(hid_high, 1)

            def ffn(g, first=False, last=False):
                for u, (j, k) in enumerate(units(last)):
                    silu(g, u, k)
                    if first and u == 1:
                        turn_high(4 * NT - 2)
                        turn_high(4 * NT - 1)
                    hidden_high(g, u, j, k)
                    if first and u == 0:
                        ffn_high(0, 4)
                    if first and u == 2:
                        ffn_high(0, 5)
                    if not last and u == 3:
                        act.wait_ge(up_done, g * 6 + 3)
                        ffn_high(g + 1, 0)
                        ffn_high(g + 1, 1)
                    if last and u == 5:
                        ln_scale(5, NT)
                    if last and u in LAST_DOWN:
                        for i in LAST_DOWN[u]:
                            if i != 5:
                                ln_scale(i, NT)
                if not last:
                    act.wait_ge(down_done, g * (2 * NT) + 2 * NT)
                    ffn_high(g + 1, 2)
                    act.wait_ge(up_done, g * 6 + 6)
                    for k in range(3, 6):
                        ffn_high(g + 1, k)

            ffn(0, first=True)
            with act.Fori(1, NG - 1) as g:
                ffn(g)
            ffn(NG - 1, last=True)

        @block.vector
        def _(dve):
            step = Steps(dve, dve_step)

            def turn_low(n):
                i, g = n // 2, n % 2
                t0, w = tokens(i % NT)
                dve.wait_ge(turned_high, n + 1)
                dve.tensor_tensor(act_l[:, 4 * g:4 * g + 4, t0:t0 + w],
                                  ps[3 + n % 4][:, :].rearrange("p (c t) -> p c t", c=4)[:, :, 0:w],
                                  act_h[:, 4 * g:4 * g + 4, t0:t0 + w].bitcast(F32),
                                  ALU.subtract).then_inc(turned_low, 1)

            for n in range(2 * NT):
                turn_low(n)
            dve.memset(gw4[:, :, :, :], 0.0).then_inc(gw_zeroed, 1)
            for b in range(2):
                dve.memset(qe[b][:, :, :, :], 0.0)
                dve.memset(qi[b][:, :, :, :], 0.0)
                dve.memset(sc[b][:, :, :], 0.0)
            step(dve.memset(s_p[:, :, :], 0.0))
            dve.wait_ge(states_turned, 1)
            dve.tensor_copy(par[:, :], ps[7][:, P:P + 35])
            dve.tensor_copy(st_in[:, :, :], ps[7][:, 0:128].rearrange("p (c n) -> p c n", c=4)).then_inc(states_read, 1)
            dve.wait_ge(lam_ready, 1)
            step(dve.tensor_scalar(e1[:, :], e0[:, :], 2.0, None, ALU.add))
            step(dve.reciprocal(e1[:, :], e1[:, :]))
            step(dve.tensor_tensor(e1[:, :], e0[:, :], e1[:, :], ALU.mult))
            step(dve.tensor_tensor(e2[:, :], e1[:, :], e1[:, :], ALU.mult))
            step(dve.tensor_scalar(e3[:, :], e2[:, :], 1 / 17, None, ALU.mult))
            for q in range(15, 1, -2):
                step(dve.scalar_tensor_tensor(out=e3[:, :], in0=e3[:, :], scalar=1.0 / q, in1=e2[:, :],
                                              op0=ALU.add, op1=ALU.mult))
            step(dve.scalar_tensor_tensor(out=e3[:, :], in0=e3[:, :], scalar=1.0, in1=e1[:, :],
                                          op0=ALU.add, op1=ALU.mult))
            step(dve.tensor_scalar(e2[:, :], lam[:, :], -1.0, 0.0, ALU.mult, ALU.max))
            step(dve.scalar_tensor_tensor(out=e3[:, :], in0=e3[:, :], scalar=2.0, in1=e2[:, :],
                                          op0=ALU.mult, op1=ALU.add))
            dve.tensor_scalar(kp, e3[:, :], 2.0, None, ALU.mult)
            dve.tensor_scalar(kn, e3[:, :], -4.0, None, ALU.mult).then_inc(h_ready, 1)
            dve.tensor_scalar(hba, ba[:, :], 0.5, None, ALU.mult)
            step(dve.tensor_scalar(hbx, bx[:, :], 0.5, None, ALU.mult))
            dve.wait_ge(soft_ready, 1)
            dve.wait_ge(consts_made, 1)
            step(dve.scalar_tensor_tensor(out=cum[:, :, :], in0=cum[:, :, :], scalar=0.0, in1=soft[:, :, :],
                                          op0=ALU.min, op1=ALU.subtract))
            for p in range(2):
                ins = dve.tensor_tensor_scan(cum[:, p, :], m01[:, :], cum[:, p, :], 0.0, ALU.mult, ALU.add)
            ins.then_inc(cum_ready, 1)

            dve.wait_ge(in_read, 3 * N_QKV)
            dve.wait_ge(gw_loaded, 16 * 16)

            def sample(tile, a, b):
                return tile.rearrange("p (b t) -> p b t", b=NB)[:, :, a:b]

            def rg_conv(ch, k):
                one = bass.ds(ch, 1)
                x_t = xr[:, one, :].rearrange("p o t -> p (o t)")
                c0, c1 = CH[k][0], CH[k][0] + CH[k][1]
                if k == 0:
                    dve.tensor_copy(gw[:, :, :], gw4[:, one, :, :].rearrange("p o m n -> p (o m) n"))
                    dve.tensor_copy(cur[:, :], pk[:, one, :].rearrange("p o k -> p (o k)"))
                step(dve.tensor_scalar(xc[:, c0:c1], x_t[:, c0:c1], cw[:, 3, one], cb[:, one], ALU.mult, ALU.add))
                for d in range(1, 4):
                    tap = cw[:, 3 - d, one]
                    a, b = max(c0, d), min(c1, TP)
                    ins = dve.scalar_tensor_tensor(out=xc[:, a:b], in0=x_t[:, a - d:b - d], scalar=tap, in1=xc[:, a:b],
                                                   op0=ALU.mult, op1=ALU.add)
                    if c1 > TP:
                        s_x = x_t[:, TP:T]
                        s_c = xc[:, TP:T]
                        dve.scalar_tensor_tensor(out=sample(s_c, d, LS), in0=sample(s_x, 0, LS - d), scalar=tap,
                                                 in1=sample(s_c, d, LS), op0=ALU.mult, op1=ALU.add)
                        hist = st_in[:, one, 0:24].rearrange("p o (b w) -> p (o b) w", w=3)[:, :, 3 - d:3]
                        ins = dve.scalar_tensor_tensor(out=sample(s_c, 0, d), in0=hist, scalar=tap,
                                                       in1=sample(s_c, 0, d), op0=ALU.mult, op1=ALU.add)
                    if d < 3:
                        step(ins)
                ins.then_inc(conv_ready, 1)

            def rg_decay(ch):
                dve.wait_ge(decay_ready, ch + 1)
                step(dve.scalar_tensor_tensor(out=tn[:, :], in0=t1[:, :], scalar=1.0, in1=tn[:, :],
                                              op0=ALU.add, op1=ALU.mult))
                dve.tensor_scalar(t1[:, :], tn[:, :], -1.0, 1.0, ALU.mult, ALU.add)
                step(dve.scalar_tensor_tensor(out=tn[:, :], in0=tn[:, :], scalar=2.0, in1=tn[:, :],
                                              op0=ALU.subtract, op1=ALU.mult))
                dve.tensor_scalar(tn[:, :], tn[:, :], 0.0, None, ALU.min).then_inc(room_ready, 1)
                step(dve.scalar_tensor_tensor(out=t2[:, :], in0=t2[:, :], scalar=1.0, in1=xc[:, :],
                                              op0=ALU.add, op1=ALU.mult))

            def rg_scan(ch):
                one = bass.ds(ch, 1)
                x_t = xr[:, one, :].rearrange("p o t -> p (o t)")
                dve.tensor_copy(st_out[:, one, 0:3], xr[:, one, TP - 3:TP])
                dve.tensor_copy(st_out[:, one, 3:27].rearrange("p o (b w) -> p (o b) w", w=3), sample(x_t[:, TP:T], LS - 3, LS))
                dve.wait_ge(root_ready, ch + 1)
                step(dve.scalar_tensor_tensor(out=t2[:, :], in0=t2[:, :], scalar=0.5, in1=tn[:, :],
                                              op0=ALU.mult, op1=ALU.mult))
                first_a, first_u = sample(t1[:, TP:T], 0, 1), sample(t2[:, TP:T], 0, 1)
                h0 = st_in[:, one, 24:32].rearrange("p o (b w) -> p (o b) w", w=1)
                tmp = tn[:, 0:NB].rearrange("p (b w) -> p b w", w=1)
                step(dve.tensor_tensor(tmp, first_a, h0, ALU.mult))
                dve.tensor_tensor(first_u, first_u, tmp, ALU.add)
                step(dve.memset(first_a, 0.0))
                step(dve.tensor_tensor_scan(x_t, t1[:, :], t2[:, :], 0.0, ALU.mult, ALU.add))
                dve.tensor_copy(st_out[:, one, 27:28], xr[:, one, TP - 1:TP])
                dve.tensor_copy(st_out[:, one, 28:36].rearrange("p o (b w) -> p (o b) w", w=1),
                                sample(x_t[:, TP:T], LS - 1, LS)).then_inc(h_ready, 1)

            for k in range(3):
                rg_conv(0, k)
            with dve.Fori(0, 3) as i:
                step.enter(i, 16)
                rg_decay(i)
                rg_conv(i + 1, 0)
                rg_scan(i)
                rg_conv(i + 1, 1)
                rg_conv(i + 1, 2)
                step.leave(3)
            rg_decay(3)
            rg_scan(3)

            dve.wait_ge(h_ready, 5)

            def spread(s):
                t0, w = tokens(s)
                c = CHUNK if s < STEPS else LS
                b = cum[:, :, t0:t0 + w].rearrange("p a (n c) -> p a n c", c=c)
                dve.tensor_tensor(een[:, :, 0:w].rearrange("p a (n c) -> p a n c", c=c),
                                  b[:, :, :, c - 1:c].broadcast_to([P, 2, w // c, c]), b,
                                  ALU.subtract).then_inc(d_ready, 1)

            def prep(s):
                t0, w = tokens(s)
                b = s % 2
                c = CHUNK if s < STEPS else LS
                if s >= 2:
                    dve.wait_ge(b_done, s - 1)
                dve.wait_ge(exp_ready, s + 1)
                for q in range(2):
                    r = slice(64 * q, 64 * q + 64)
                    dve.scalar_tensor_tensor(out=qe[b][r, :, q, 0:w], in0=qk[r, 0:2, t0:t0 + w], scalar=DK ** -0.5,
                                             in1=eb[r, :, 0:w], op0=ALU.mult, op1=ALU.mult)
                dve.tensor_tensor(ke[b][:, :, 0:w], qk[:, 2:4, t0:t0 + w], enb[:, :, 0:w], ALU.mult)
                dve.tensor_copy(dec[b][:, :, 0:w // c], eb[:, :, c - 1:w:c])
                if s < STEPS:
                    dve.tensor_tensor(ka[b][:, :, :], qk[:, 2:4, t0:t0 + 64], een[:, :, 0:64], ALU.mult)
                    step(dve.tensor_tensor(k2[b][:, :, 64:128], qk[:, 2:4, t0 + 64:t0 + 128], een[:, :, 64:128], ALU.mult))
                    for q in range(2):
                        r = slice(64 * q, 64 * q + 64)
                        dve.tensor_tensor(qi[b][r, :, q, :], qe[b][r, :, q, 64:128],
                                          dec[b][r, :, 0:1].broadcast_to([64, 2, 64]), ALU.mult)
                    dve.tensor_tensor(k2[b][:, :, 0:64], ka[b][:, :, :],
                                      dec[b][:, :, 1:2].broadcast_to([P, 2, 64]), ALU.mult).then_inc(prep_ready, 1)
                else:
                    dve.tensor_tensor(k2[b][:, :, 0:w], qk[:, 2:4, t0:t0 + w], een[:, :, 0:w],
                                      ALU.mult).then_inc(prep_ready, 1)

            def mask(s):
                b = s % 2
                dve.wait_ge(a_done, s + 1)
                if s < STEPS:
                    p3 = ps[3][:, :].rearrange("p (h c) -> p h c", h=4)
                    dve.tensor_tensor(sc[b][0:64, :, :], p3[0:64, :, :],
                                      causal[0:64, :].rearrange("p (o c) -> p o c", o=1).broadcast_to([64, 4, P]), ALU.mult)
                    dve.tensor_tensor(sc[b][64:128, :, 64:128], p3[64:128, :, 64:128],
                                      causal[64:128, 64:128].rearrange("p (o c) -> p o c", o=1).broadcast_to([64, 4, 64]),
                                      ALU.mult).then_inc(sc_ready, 1)
                else:
                    dve.tensor_tensor(sc[b][0:TS, :, 0:TS], ps[3][0:TS, :].rearrange("p (h c) -> p h c", h=4)[:, :, 0:TS],
                                      smask[:, :].rearrange("p (o c) -> p o c", o=1).broadcast_to([TS, 4, TS]),
                                      ALU.mult).then_inc(sc_ready, 1)

            def take(s):
                t0, w = tokens(s)
                b = s % 2
                if s < STEPS:
                    step(dve.tensor_tensor(dec2[:, :], dec[b][:, :, 0], dec[b][:, :, 1], ALU.mult))
                dve.wait_ge(b_done, s + 1)
                dve.tensor_copy(qk[:, :, t0:t0 + w], ps[6][:, :].rearrange("p (h c) -> p h c", h=4)[:, :, 0:w]
                                ).then_inc(o_ready, 1)
                if s < STEPS:
                    for p in range(2):
                        ins = dve.scalar_tensor_tensor(out=s_p[:, p, :], in0=s_p[:, p, :], scalar=dec2[:, p:p + 1],
                                                       in1=ps[7][:, p * DV:p * DV + DV], op0=ALU.mult, op1=ALU.add)
                    ins.then_inc(kv_read, 1)

            def gelu(m):
                c, (c0, cn) = m // 3, CH[m % 3]
                a, b = gx[m % 2][:, 0:cn], gt[m % 2][:, 0:cn]
                dve.wait_ge(tanh_ready, m + 1)
                step(dve.scalar_tensor_tensor(out=b, in0=b, scalar=1.0, in1=a, op0=ALU.add, op1=ALU.mult))
                dve.scalar_tensor_tensor(out=xr[:, c, c0:c0 + cn], in0=b, scalar=0.5, in1=xr[:, c, c0:c0 + cn],
                                         op0=ALU.mult, op1=ALU.mult).then_inc(gelu_done, 1)

            def spread_v(h):
                if h == 0:
                    dve.wait_ge(tok_ready, STEPS + 1)
                elif h >= 2:
                    dve.wait_ge(kv_done, h - 1)
                dve.tensor_tensor(vb[h % 2][0:TS, :, :],
                                  vt[STEPS % 2][0:TS, h * DV:(h + 1) * DV].rearrange("p (o v) -> p o v", o=1).broadcast_to([TS, NB, DV]),
                                  bmask[:, :].rearrange("p (b o) -> p b o", o=1).broadcast_to([TS, NB, DV]),
                                  ALU.mult).then_inc(vb_ready, 1)

            spread(0)
            prep(0)
            def sample_state(p):
                dve.wait_ge(kv_done, 2 * p + 2)
                for e in range(NB):
                    ins = dve.scalar_tensor_tensor(
                        out=s_s[:, p, e, :], in0=s_s[:, p, e, :], scalar=dec[STEPS % 2][:, p, e:e + 1],
                        in1=ps[3 if e < 4 else 7][:, (e % 4) * DV:(e % 4 + 1) * DV], op0=ALU.mult, op1=ALU.add)
                ins.then_inc(kv_read, 1)

            for m in range(12):
                if m >= 2:
                    gelu(m - 2)
                if m + 1 <= STEPS:
                    if m:
                        dve.wait_ge(prep_ready, m + 1)
                    spread(m + 1)
                if m <= STEPS:
                    mask(m)
                if 1 <= m <= STEPS + 1:
                    take(m - 1)
                if m + 1 <= STEPS:
                    prep(m + 1)
                if m == STEPS:
                    spread_v(0)
                    spread_v(1)
                if m == STEPS + 1:
                    sample_state(0)
                    spread_v(2)
                    spread_v(3)
                if m == STEPS + 2:
                    sample_state(1)
            gelu(10)
            gelu(11)

            for h in range(4):
                dve.wait_ge(rs_ready, h + 1)
                dve.scalar_tensor_tensor(out=qk[:, h, :], in0=qk[:, h, :], scalar=gn[:, 0:1], in1=rs[:, :],
                                         op0=ALU.mult, op1=ALU.mult).then_inc(o_normed, 1)
                dve.wait_ge(o_normed, h + 1)
                for k, (c0, cn) in enumerate(CH):
                    u = 3 * h + k
                    dve.wait_ge(sg_ready, u + 1)
                    dve.tensor_tensor(qk[:, h, c0:c0 + cn], qk[:, h, c0:c0 + cn], sg[u % 2][:, 0:cn],
                                      ALU.mult).then_inc(yg_ready, 1)
                    if h == 3:
                        for i in range(3 * k, 3 * k + 3):
                            t0, w = tokens(i)
                            dve.wait_ge(y_high, i + 1)
                            dve.tensor_tensor(act_l[:, 0:4, t0:t0 + w], qk[:, :, t0:t0 + w],
                                              act_h[:, 0:4, t0:t0 + w].bitcast(F32), ALU.subtract).then_inc(y_low, 1)

            def out_read(i, half):
                w = tokens(i)[1]
                n = half * NT + i
                dve.wait_ge(x_loaded[i], 32)
                dve.wait_ge(op_done, n + 1)
                r = rows[0:w, i, half * 512:half * 512 + 512]
                ins = dve.scalar_tensor_tensor(out=r, in0=r, scalar=ALPHA, in1=ps[out_bank(n)][0:w, :],
                                               op0=ALU.mult, op1=ALU.add)
                ins.then_inc(op_read, 1)

            def norm_a(i, base):
                w = tokens(i)[1]
                if base + i >= 2:
                    dve.wait_ge(ln_scaled, base + i - 1)
                st, m = stats[i % 2], mv[i % 2]
                for half in range(2):
                    ins = dve.bn_stats(st[0:w, half, :], rows[0:w, i, half * 512:half * 512 + 512])
                step(ins)
                step(dve.bn_aggr(m[0:w, 0:2], st[0:w, :, :]))
                step(dve.tensor_scalar(m[0:w, 1:2], m[0:w, 1:2], LN_EPS, None, ALU.add))
                dve.reciprocal(m[0:w, 1:2], m[0:w, 1:2]).then_inc(var_ready, 1)

            def norm_b(i, ln):
                w = tokens(i)[1]
                r = rows[0:w, i, :]
                dve.scalar_tensor_tensor(out=r, in0=r, scalar=mv[i % 2][0:w, 0:1], in1=ln[0:w, 0, :],
                                         op0=ALU.subtract, op1=ALU.mult).then_inc(ln_z, 1)

            for i in range(NT):
                out_read(i, 0)
            dve.wait_ge(ln1_loaded, 32)
            for i in range(NT):
                out_read(i, 1)
                dve.wait_ge(op_read, NT + i + 1)
                norm_a(i, 0)
                norm_b(i, ln1)
                if i >= 1:
                    turn_low(2 * NT + 2 * (i - 1))
                    turn_low(2 * NT + 2 * (i - 1) + 1)
            def down_rows(g, i):
                w = tokens(i)[1]
                for half in range(2):
                    n = 2 * i + half
                    dve.wait_ge(down_done, g * (2 * NT) + (n + 1))
                    r = rows[0:w, i, half * 512:half * 512 + 512]
                    dve.scalar_tensor_tensor(out=r, in0=r, scalar=res[0:w, bass.ds(g, 1)], in1=ps[4 + n % 4][0:w, :],
                                             op0=ALU.mult, op1=ALU.add).then_inc(down_read, 1)

            def last_norm(i):
                dve.wait_ge(down_read, (NG - 1) * (2 * NT) + 2 * i + 2)
                norm_a(i, NT)
                norm_b(i, ln2)

            def ffn(g, first=False, last=False):
                for u, (j, k) in enumerate(units(last)):
                    c0, cn = CH[k]
                    dve.wait_ge(silu_ready, g * 6 + (u + 1))
                    dve.wait_ge(up_done, g * 6 + (u + 1))
                    dve.tensor_tensor(hf[u % 2][:, 0:cn], sl[u % 2][:, 0:cn], ps[2 + u % 2][:, 0:cn],
                                      ALU.mult).then_inc(hid_ready, 1)
                    dve.wait_ge(hid_high, g * 6 + (u + 1))
                    dve.tensor_tensor(hid_l[j][:, c0:c0 + cn], hf[u % 2][:, 0:cn],
                                      hid_h[j][:, c0:c0 + cn].bitcast(F32), ALU.subtract).then_inc(hid_low, 1)
                    if first and u == 0:
                        turn_low(4 * NT - 2)
                        turn_low(4 * NT - 1)
                    if last and u == 5:
                        last_norm(5)
                    if last and u in LAST_DOWN:
                        for i in LAST_DOWN[u]:
                            down_rows(g, i)
                            if i != 5:
                                last_norm(i)
                if not last:
                    for i in range(NT):
                        down_rows(g, i)

            ffn(0, first=True)
            with dve.Fori(1, NG - 1) as g:
                ffn(g)
            dve.wait_ge(ln2_loaded, 32)
            ffn(NG - 1, last=True)

        @block.tensor
        def _(pe):
            def turn(n, rows_t, w):
                g = n % 2
                if n >= 4:
                    pe.wait_ge(turned_low, n - 3)
                for c in range(4):
                    f = (4 * g + c) * P
                    ins = pe.transpose(ps[3 + n % 4][:, c * P:c * P + w], rows_t[0:w, f:f + P], ident[0:w, 0:w])
                ins.then_inc(turned, 1)

            def split_product(out, terms):
                last = len(terms) - 1
                for c, (sh, sl_, mh, ml) in enumerate(terms):
                    pe.matmul(out, sh, mh, start=(c == 0), stop=False)
                    pe.matmul(out, sh, ml, start=False, stop=False)
                    ins = pe.matmul(out, sl_, mh, start=False, stop=(c == last))
                return ins

            def project(n, slot, k, width=P):
                c0, cn = CH[k]
                if k == 0:
                    pe.wait_ge(w_low, n + 1)
                if not isinstance(n, int) or n >= 1:
                    if isinstance(n, int) and n > N_GR:
                        m = 3 * (n - 1 - N_GR) + k
                        if m < 12:
                            pe.wait_ge(gx_ready, m + 1)
                        else:
                            pe.wait_ge(sg_ready, m - 12 + 1)
                    else:
                        pe.wait_ge(in_read, n * 3 + (k - 2))
                split_product(ps[k][0:width, 0:cn],
                              [(wh[slot % 2][:, c, 0:width], wl[slot % 2][:, c, 0:width],
                                act_h[:, c, c0:c0 + cn], act_l[:, c, c0:c0 + cn]) for c in range(KC)]
                              ).then_inc(in_done, 1)

            pe.wait_ge(ident_made, 1)
            for i in range(NT):
                w = tokens(i)[1]
                pe.wait_ge(x_loaded[i], 16)
                for g in range(2):
                    turn(2 * i + g, x_in[:, i, :], w)
                if i in Z_AFTER:
                    k = Z_AFTER.index(i)
                    pe.wait_ge(turned_low, 2 * (3 * k + 3))
                    project(N_Z, N_Z, k, RANK)
            pe.wait_ge(state_loaded, 32)
            pe.wait_ge(params_loaded, 16 * 8)
            for c in range(4):
                pe.transpose(ps[7][:, c * 32:c * 32 + 32], st_rows[0:32, c * P:(c + 1) * P], ident[0:32, 0:32])
            ins = pe.transpose(ps[7][:, P:P + 35], par_rows[:, :], ident[0:35, 0:35])
            ins.then_inc(states_turned, 1)
            pe.wait_ge(in_read, 3)
            pe.wait_ge(states_read, 1)
            for u in range(6):
                p, k = u // 3, u % 3
                c0, cn = CH[k]
                if u == 5:
                    pe.wait_ge(zg_read, 1)
                pe.matmul(ps[3 + u % 5][:, 0:cn], wgate[:, p, :], z[:, c0:c0 + cn], start=True, stop=True
                          ).then_inc(zg_done, 1)
            with pe.Fori(0, 2) as i:
                for j in range(2):
                    for k in range(3):
                        project(i * 2 + (N_XR + j), N_XR + j, k)

            pe.wait_ge(zg_read, 6)

            def gates(ch, k):
                c0, cn = CH[k]
                pe.wait_ge(conv_ready, ch * 3 + (k + 1))
                if k:
                    pe.wait_ge(gates_read, ch * 3 + k)
                pe.matmul(ps[3][:, 0:cn], gw[:, 0, :], xc[:, c0:c0 + cn], start=True, stop=True)
                pe.matmul(ps[4][:, 0:cn], gw[:, 1, :], xc[:, c0:c0 + cn], start=True, stop=True).then_inc(gates_done, 1)

            with pe.Fori(0, 4) as i:
                n = i * 2 + N_QKV
                for k in range(3):
                    project(n, N_QKV, k)
                    gates(i, k)
                for k in range(3):
                    project(n + 1, N_QKV + 1, k)

            def scores(s):
                t0, w = tokens(s)
                b = s % 2
                pe.wait_ge(prep_ready, s + 1)
                if s:
                    pe.wait_ge(sc_ready, s)
                    pe.wait_ge(tok_ready, s)
                p3 = ps[3][:, :].rearrange("p (h c) -> p h c", h=4)
                for p in range(2):
                    heads = slice(2 * p, 2 * p + 2)
                    if s < STEPS:
                        pe.matmul(p3[0:64, heads, 0:64], ke[b][:, p, 0:64], qe[b][:, p, :, 0:64], start=True, stop=True)
                        pe.matmul(p3[0:64, heads, 64:128], ka[b][:, p, :], qe[b][:, p, :, 64:128], start=True, stop=True)
                        pe.matmul(p3[64:128, heads, 64:128], ke[b][:, p, 64:128], qe[b][:, p, :, 64:128],
                                  start=True, stop=True)
                    else:
                        pe.matmul(p3[0:w, heads, 0:w], ke[b][:, p, 0:w], qe[b][:, p, :, 0:w], start=True, stop=True)
                for p in range(2):
                    pe.transpose(ps[4][0:w, p * P:(p + 1) * P], k2[b][:, p, 0:w], ident[:, :])
                for h in range(4):
                    ins = pe.transpose(ps[5][0:w, h * DV:(h + 1) * DV], v[:, h, t0:t0 + w], ident[:, :])
                ins.then_inc(a_done, 1)

            def attend(s):
                w = tokens(s)[1]
                b = s % 2
                pe.wait_ge(sc_ready, s + 1)
                pe.wait_ge(tok_ready, s + 1)
                if s:
                    pe.wait_ge(o_ready, s)
                    pe.wait_ge(kv_read, s)
                if s == STEPS:
                    pe.wait_ge(gla_state_loaded, 32)
                for h in range(4):
                    pe.matmul(ps[6][:, h * P:h * P + w], vt[b][0:w, h * DV:(h + 1) * DV], sc[b][0:w, h, 0:w],
                              start=(h == 0), stop=False)
                o = ps[6][:, :].rearrange("p (h c) -> p h c", h=4)
                for p in range(2):
                    heads = slice(2 * p, 2 * p + 2)
                    if s < STEPS:
                        pe.matmul(o[:, heads, 0:64], s_p[:, p, :], qe[b][:, p, :, 0:64], start=False, stop=False)
                        ins = pe.matmul(o[:, heads, 64:128], s_p[:, p, :], qi[b][:, p, :, :], start=False, stop=(p == 1))
                    else:
                        for e in range(NB):
                            t = slice(e * LS, (e + 1) * LS)
                            ins = pe.matmul(o[:, heads, t], s_s[:, p, e, :], qe[b][:, p, :, t], start=False,
                                            stop=(p == 1 and e == NB - 1))
                if s < STEPS:
                    for h in range(4):
                        p, q = h // 2, h % 2
                        ins = pe.matmul(ps[7][64 * q:64 * q + 64, p * DV:(p + 1) * DV],
                                        k2t[b][:, h * DK:(h + 1) * DK], vt[b][:, h * DV:(h + 1) * DV],
                                        start=True, stop=True)
                ins.then_inc(b_done, 1)

            def sample_kv(h):
                p, q = h // 2, h % 2
                pe.wait_ge(vb_ready, h + 1)
                if h == 2:
                    pe.wait_ge(kv_read, STEPS + 1)
                for e, bank in enumerate((3, 7)):
                    ins = pe.matmul(ps[bank][64 * q:64 * q + 64, :], k2t[STEPS % 2][0:TS, h * DK:(h + 1) * DK],
                                    vb[h % 2][0:TS, 4 * e:4 * e + 4, :], start=True, stop=True)
                ins.then_inc(kv_done, 1)

            for m in range(12):
                project(N_GR + m // 3, N_GR + m // 3, m % 3)
                if m <= STEPS:
                    scores(m)
                if 1 <= m <= STEPS + 1:
                    attend(m - 1)
                if m == STEPS + 1:
                    for c in range(4):
                        ins = pe.transpose(ps[4][0:36, c * P:(c + 1) * P], st_out[:, c, :], ident[:, :])
                    ins.then_inc(states_back, 1)
                if m > STEPS and m < STEPS + 3:
                    sample_kv(2 * (m - STEPS - 1))
                    sample_kv(2 * (m - STEPS - 1) + 1)

            def mean_square(h):
                pe.wait_ge(sq_ready, h + 1)
                if h:
                    pe.wait_ge(rs_ready, h)
                for k, (c0, cn) in enumerate(CH):
                    pe.matmul(ps[3 + k][:, 0:cn], ones[:, :], sq[:, c0:c0 + cn], start=True, stop=True
                              ).then_inc(ms_done, 1)

            for h in range(4):
                for k in range(3):
                    project(N_G + h, N_G + h, k)
                    if k == 0 and h == 0:
                        pe.wait_ge(states_rows, 1)
                        pe.wait_ge(kv_read, STEPS + 2)
                        mean_square(0)
                    if k == 2 and h < 3:
                        mean_square(h + 1)

            for half in range(2):
                pe.wait_ge(w_low, N_WO + 4 * half + 4)
                for i in range(NT):
                    t0, w = tokens(i)
                    n = half * NT + i
                    if n < 3:
                        pe.wait_ge(sg_ready, 10 + n)
                    if half == 0:
                        pe.wait_ge(y_low, i + 1)
                        pe.wait_ge(y_low2, i + 1)
                    if n == 8:
                        pe.wait_ge(op_read, 1)
                    elif n >= NT:
                        pe.wait_ge(op_read, NT if n < NT + 4 else n - 3)
                    split_product(ps[out_bank(n)][0:w, :],
                                  [(act_h[:, c, t0:t0 + w], act_l[:, c, t0:t0 + w], wo_h[half][:, c, :], wo_l[half][:, c, :])
                                   for c in range(KC)]).then_inc(op_done, 1)
                    if half and i >= 2:
                        pe.wait_ge(ln_done, i - 1)
                        for g in range(2):
                            turn(2 * NT + 2 * (i - 2) + g, rows[:, i - 2, :], tokens(i - 2)[1])
            def down(g, i, first, hidden):
                t0, w = tokens(i)
                if i == 0:
                    pe.wait_ge(w_low, g * 6 + (N_FFN + 6))
                pe.wait_ge(hid_low, hidden)
                for half in range(2):
                    n = 2 * i + half
                    cols = slice(half * 512, half * 512 + 512)
                    if not (first and n < 4):
                        pe.wait_ge(down_read, g * (2 * NT) + (n - 3))
                    split_product(ps[4 + n % 4][0:w, :],
                                  [(hid_h[j][:, t0:t0 + w], hid_l[j][:, t0:t0 + w], wd_h[j][:, cols], wd_l[j][:, cols])
                                   for j in range(2)]).then_inc(down_done, 1)

            def ffn(g, first=False, last=False):
                for u, (j, k) in enumerate(units(last)):
                    c0, cn = CH[k]
                    if first and u in (1, 2):
                        i = NT - 3 + u
                        pe.wait_ge(ln_done, i + 1)
                        for q in range(2):
                            turn(2 * NT + 2 * i + q, rows[:, i, :], tokens(i)[1])
                    if first and u < 3:
                        pe.wait_ge(turned_low, 2 * NT + 2 * (3 * u + 3))
                    for m, done in enumerate((gate_done, up_done)):
                        if k == 0:
                            pe.wait_ge(w_low, g * 6 + (N_FFN + 3 * j + m + 1))
                        if first and u == 0:
                            pe.wait_ge(op_read, 2 * NT - 3 + 2 * m)
                        if first and u == 1:
                            pe.wait_ge(op_read, 2 * NT - 2)
                            if m == 1:
                                pe.wait_ge(turned_low, 4 * NT - 3)
                        if not (first and u < 2):
                            pe.wait_ge(silu_ready if m == 0 else hid_ready, g * 6 + (u - 1))
                        split_product(ps[2 * m + u % 2][:, 0:cn],
                                      [(gu_h[m][j][:, c, :], gu_l[m][j][:, c, :], act_h[:, c, c0:c0 + cn],
                                        act_l[:, c, c0:c0 + cn]) for c in range(KC)]).then_inc(done, 1)
                    if last and u in LAST_DOWN:
                        for i in LAST_DOWN[u]:
                            down(g, i, False, g * 6 + 2 * (chunk_of(i) + 1))
                if not last:
                    for i in range(NT):
                        down(g, i, first, g * 6 + (4 + chunk_of(i)))

            ffn(0, first=True)
            with pe.Fori(1, NG - 1) as g:
                ffn(g)
            ffn(NG - 1, last=True)


_INS = ["x_prompt", "x_sample", "state_gla", "state_rglru", "state_conv", "w_in", "gla_w_gate", "gla_b_gate",
        "gla_norm_g", "rg_conv_w", "rg_conv_b", "rg_w_a", "rg_b_a", "rg_w_x", "rg_b_x", "rg_lambda", "w_out",
        "ln1_g", "ln1_b", "ffn_w_gate", "ffn_w_up", "ffn_w_down", "ln2_g", "ln2_b"]
_OUTS = [(1, 1024, 1024), (8, 8, 1024), (1, 1, 4, 64, 128), (1, 1, 512), (1, 1, 3, 512),
         (1, 8, 4, 64, 128), (1, 8, 512), (1, 8, 3, 512)]


def kernel(**inputs):
    import numpy as _np
    import concourse.bacc as _bacc
    from concourse.bass_utils import run_bass_kernel_spmd as _run

    nc = _bacc.Bacc("TRN2", target_bir_lowering=False, num_devices=1)
    arrays, args = {}, []
    for name in _INS:
        a = _np.ascontiguousarray(inputs[name])
        arrays[f"in_{name}"] = a
        args.append(nc.dram_tensor(f"in_{name}", a.shape, mybir.dt.from_np(a.dtype), kind="ExternalInput").ap())
    for i, shape in enumerate(_OUTS):
        args.append(nc.dram_tensor(f"out_{i}", shape, F32, kind="ExternalOutput").ap())
    build(nc, *args)
    r = _run(nc, [arrays], core_ids=[0])
    return tuple(r.results[0][f"out_{i}"] for i in range(len(_OUTS)))
```

```python
from contextlib import ExitStack

import concourse.bass as bass
from concourse import mybir

F32 = mybir.dt.float32
F32R = mybir.dt.float32r
ACT = mybir.ActivationFunctionType
ALU = mybir.AluOpType

P = 128
D = 1024
KC = D // P
TP = 1024
NB, LS = 8, 8
TS = NB * LS
T = TP + TS
NT = -(-T // P)
CH = [(0, 3 * P), (3 * P, 3 * P), (6 * P, T - 6 * P)]
CW = CH[0][1]
F = 2816
NF = F // P
NG = NF // 2
DK, DV, CHUNK = 64, 128, 64
STEPS = TP // P
RANK = 16
ZP = 32 + RANK
COL_Q, COL_G, COL_Z, COL_XR, COL_GR = 0, 1024, 1536, 1552, 2064
ALPHA = 2.0 ** 0.25
LN_EPS, RMS_EPS = 1e-5, 1e-6

N_XR, N_QKV, N_GR, N_G, N_WO, N_FFN = 1, 5, 13, 17, 21, 29


def tokens(i):
    return i * P, min(P, T - i * P)


def chunk_of(i):
    return i // 3


def out_bank(n):
    return n % 8 if n < NT else (7, 0, 1, 2)[(n - NT) % 4]


def units(last):
    return [(j, k) for k in range(3) for j in range(2)] if last else [(j, k) for j in range(2) for k in range(3)]


def turns_after(i):
    return range(2 * i - 2, 2 * i) if 0 < i < NT - 2 else range(2 * NT - 6, 2 * NT - 2) if i == NT - 1 else ()


DOWN = (0, 1, 2, 3, 4, 5, 8, 6, 7)
LN2 = (0, 1, 2, 3, 4, 5, 6, 8, 7)
LAST_DOWN = {2: (0, 1, 2), 4: (3, 4, 5), 5: (8, 6, 7)}
LAST_NORM = {2: (0, 1, 2), 4: (3, 4), 5: (5, 6, 8, 7)}
WO_EARLY = 4
Z_AFTER = (3, 6, NT - 1)


class Steps:

    def __init__(self, eng, sem):
        self.eng, self.sem, self.base, self.k = eng, sem, 0, 0

    def __call__(self, ins):
        ins.then_inc(self.sem, 1)
        self.k += 1
        self.eng.wait_ge(self.sem, self.base + self.k)

    def enter(self, i, per):
        self.saved, self.per = self.base + self.k, per
        self.base, self.k = i * per + self.saved, 0

    def leave(self, n):
        assert self.k == self.per, (self.k, self.per)
        self.base, self.k = self.saved + n * self.per, 0


def build(nc, x_prompt, x_sample, state_gla, state_rglru, state_conv, w_in, gla_w_gate, gla_b_gate,
          gla_norm_g, rg_conv_w, rg_conv_b, rg_w_a, rg_b_a, rg_w_x, rg_b_x, rg_lambda, w_out,
          ln1_g, ln1_b, ffn_w_gate, ffn_w_up, ffn_w_down, ln2_g, ln2_b,
          y_prompt, y_sample, gla_p, rg_p, conv_p, gla_s, rg_s, conv_s):
    ctx = ExitStack()
    with ctx:
        def at(name, shape, offset, dt=F32):
            return nc.alloc_sbuf_tensor_at(name, shape, dt, offset=BASE + offset)

        def sem(name):
            return ctx.enter_context(nc.semaphore(name))

        BASE = 16512
        TB = T * 4
        R_HIGH, R_LOW = 0, 8 * TB
        R_OHS = 16 * TB
        R_X = R_OHS + NT * 4096
        R_G = R_X + 32768
        R_RING = R_G + 45056
        R_RAW = R_RING + 4 * TB
        R_CONST = R_RAW + 8192

        act_h = at("act_h", [P, KC, T], R_HIGH, F32R)
        act_l = at("act_l", [P, KC, T], R_LOW, F32R)
        qk = at("qk", [P, 4, T], R_OHS)
        xr = at("xr", [P, 4, T], R_OHS + 4 * TB)
        rows = at("rows", [P, NT, D], R_OHS)
        v = at("v", [P, 4, T], R_X)
        soft = at("soft", [P, 2, T], R_X)
        z = at("z", [ZP, T], R_X + 2 * TB)
        cum = at("cum", [P, 2, T], R_X + 4 * TB)
        m01 = at("m01", [P, T], R_X + 6 * TB)
        gw = at("gw", [P, 2, P], R_X + 7 * TB)
        x_in = at("x_in", [P, NT, D], R_G)
        xc, t1, t2, tn = (at(n, [P, T], R_G + j * TB) for j, n in enumerate(("xc", "t1", "t2", "tn")))
        gw4 = at("gw4", [P, 4, 2, P], R_G + 4 * TB)
        g_at = [R_G]

        def gla(name, shape, bufs=1):
            size = 4
            for s in shape[1:]:
                size *= s
            out = []
            for b in range(bufs):
                out.append(at(f"{name}{b}", shape, g_at[0]))
                g_at[0] += -(-size // 32) * 32
            return out

        ke = gla("ke", [P, 2, P], 2)
        ka = gla("ka", [P, 2, CHUNK], 2)
        k2 = gla("k2", [P, 2, P], 2)
        k2t = gla("k2t", [P, 2 * P], 2)
        vt = gla("vt", [P, 4 * DV], 2)
        gx = gla("gx", [P, CW], 2)
        gt = gla("gt", [P, CW], 2)
        g_at[0] = R_G + 4 * TB
        eb, enb, een = gla("eb", [P, 2, P])[0], gla("enb", [P, 2, P])[0], gla("een", [P, 2, P])[0]
        g_at[0] = R_G + 4 * TB + 4096
        qe = gla("qe", [P, 2, 2, P], 2)
        qi = gla("qi", [P, 2, 2, CHUNK], 2)
        sc = gla("sc", [P, 4, P], 2)
        s_p = gla("s_p", [P, 2, DV])[0]
        s_s = gla("s_s", [P, 2, NB, DV])[0]
        vb = [*gla("vb", [P, NB, DV]),
              at("vb1", [P, NB, DV], R_X + 6 * TB)]
        assert g_at[0] <= R_RING, (g_at[0], R_RING)
        sq = at("sq", [P, T], R_X + 8192)
        sg = [at(f"sg{b}", [P, CW], R_X + 8192 + TB + b * CW * 4) for b in range(2)]
        rs = at("rs", [P, T], R_X + 24576)
        wh = [at(f"wh{b}", [P, KC, P], R_RING + b * 8192, F32R) for b in range(2)]
        wl = [at(f"wl{b}", [P, KC, P], R_RING + b * 8192 + 4096, F32R) for b in range(2)]
        raw = [at(f"raw{b}", [P, 1024], R_RAW + b * 4096) for b in range(2)]
        wo_h = [at(f"wo_h{b}", [P, KC, 512], r, F32R) for b, r in enumerate((R_G, R_X))]
        wo_l = [at(f"wo_l{b}", [P, KC, 512], r + 16384, F32R) for b, r in enumerate((R_G, R_X))]
        ln1 = at("ln1", [P, 2, D], R_G + 32768)
        gu_h = [[at(f"gu_h{m}{b}", [P, KC, P], R_G + m * 16384 + b * 8192, F32R) for b in range(2)] for m in range(2)]
        gu_l = [[at(f"gu_l{m}{b}", [P, KC, P], R_G + m * 16384 + b * 8192 + 4096, F32R) for b in range(2)]
                for m in range(2)]
        wd_h = [at(f"wd_h{b}", [P, D], R_X + b * 8192, F32R) for b in range(2)]
        wd_l = [at(f"wd_l{b}", [P, D], R_X + b * 8192 + 4096, F32R) for b in range(2)]
        ln2 = at("ln2", [P, 2, D], R_X + 16384)
        sl = [at(f"sl{b}", [P, CW], R_X + 24576 + b * CW * 4) for b in range(2)]
        hf = [at(f"hf{b}", [P, CW], R_X + 24576 + (2 + b) * CW * 4) for b in range(2)]
        hid = [at(f"hid{b}", [P, 2 * T], R_RING + 2 * b * TB, F32R) for b in range(2)]
        c_at = [R_CONST]

        def const(name, shape):
            size = 4
            for s in shape[1:]:
                size *= s
            out = at(name, shape, c_at[0])
            c_at[0] += -(-size // 32) * 32
            return out

        ident = const("ident", [P, P])
        causal = const("causal", [P, P])
        smask = const("smask", [TS, TS])
        ones = const("ones", [P, P])
        fold = const("fold", [P, TS])
        bmask = const("bmask", [TS, NB])
        par = const("par", [P, 35])
        cw = par[:, 0:16].rearrange("p (j c) -> p j c", j=4)
        cb, ba, bx, lam = (par[:, 16 + 4 * j:20 + 4 * j] for j in range(4))
        bg, gn = par[:, 32:34], par[:, 34:35]
        pk = const("pk", [P, 4, 4])
        hba, hbx, kp, kn = (pk[:, :, j] for j in range(4))
        cur = const("cur", [P, 4])
        e0, e1, e2, e3 = (const(n, [P, 4]) for n in ("e0", "e1", "e2", "e3"))
        eps = const("eps", [P, 1])
        res = const("res", [P, NG])
        dec = [const(f"dec{b}", [P, 2, NB]) for b in range(2)]
        dec2 = const("dec2", [P, 2])
        stats = [const(f"stats{b}", [P, 2, 6]) for b in range(2)]
        mv = [const(f"mv{b}", [P, 4]) for b in range(2)]
        wgate = at("wgate", [ZP, 2, P], R_X + 7 * TB + 1024)
        assert c_at[0] <= 229344 - BASE, c_at[0] - (229344 - BASE)
        st_in = at("st_in", [P, 4, 32], R_OHS + 8 * TB)
        st_out = at("st_out", [P, 4, 36], R_OHS + 8 * TB + 512)
        st_rows = at("st_rows", [36, 512], R_X)

        par_rows = at("par_rows", [35, P], R_X + 2048)
        ps = [ctx.enter_context(nc.psum_tensor(f"ps{b}", [P, 512], F32)) for b in range(8)]

        x_loaded = [sem(f"x_loaded{i}") for i in range(NT)]
        raw_loaded = [sem("raw_loaded0"), sem("raw_loaded1")]
        params_loaded, gw_loaded, state_loaded = sem("params_loaded"), sem("gw_loaded"), sem("state_loaded")
        gla_state_loaded, ln1_loaded, ln2_loaded = sem("gla_state_loaded"), sem("ln1_loaded"), sem("ln2_loaded")
        out_stored, states_stored = sem("out_stored"), sem("states_stored")
        ident_made, consts_made, gw_zeroed = sem("ident_made"), sem("consts_made"), sem("gw_zeroed")
        turned, turned_high, turned_low = sem("turned"), sem("turned_high"), sem("turned_low")
        w_high, w_low = sem("w_high"), sem("w_low")
        in_done, in_read = sem("in_done"), sem("in_read")
        zg_done, zg_read, soft_ready, cum_ready = sem("zg_done"), sem("zg_read"), sem("soft_ready"), sem("cum_ready")
        states_turned, states_read = sem("states_turned"), sem("states_read")
        states_back, states_rows = sem("states_back"), sem("states_rows")
        dve_step, act_step, pool_step = sem("dve_step"), sem("act_step"), sem("pool_step")
        lam_abs, lam_ready = sem("lam_abs"), sem("lam_ready")
        conv_ready, gates_done, gates_read = sem("conv_ready"), sem("gates_done"), sem("gates_read")
        decay_ready, room_ready, root_ready, h_ready = sem("decay_ready"), sem("room_ready"), sem("root_ready"), sem("h_ready")
        d_ready, exp_ready, prep_ready = sem("d_ready"), sem("exp_ready"), sem("prep_ready")
        a_done, b_done, tok_ready, sc_ready, o_ready = (
            sem(n) for n in ("a_done", "b_done", "tok_ready", "sc_ready", "o_ready"))
        vb_ready, kv_done, kv_read = sem("vb_ready"), sem("kv_done"), sem("kv_read")
        gx_ready, poly_ready, tanh_ready, gelu_done = (sem(n) for n in ("gx_ready", "poly_ready", "tanh_ready", "gelu_done"))
        sq_ready, ms_done, rs_ready, o_normed, sg_ready, yg_ready = (
            sem(n) for n in ("sq_ready", "ms_done", "rs_ready", "o_normed", "sg_ready", "yg_ready"))
        y_high, yr_high, y_low, y_low2 = sem("y_high"), sem("yr_high"), sem("y_low"), sem("y_low2")
        op_done, op_read = sem("op_done"), sem("op_read")
        var_ready, std_ready, ln_z, ln_scaled, ln_done = (
            sem(n) for n in ("var_ready", "std_ready", "ln_z", "ln_scaled", "ln_done"))
        ln_done_v, fold_done = sem("ln_done_v"), sem("fold_done")
        gate_done, up_done, silu_ready, hid_ready, hid_high, hid_low = (
            sem(n) for n in ("gate_done", "up_done", "silu_ready", "hid_ready", "hid_high", "hid_low"))
        down_done, down_read = sem("down_done"), sem("down_read")

        w_in_v = w_in.rearrange("l (c p) n -> p (l c) n", p=P)
        w_out_v = w_out.rearrange("l (c p) n -> p (l c) n", p=P)
        w_gu_v = [w.rearrange("l (c p) n -> p (l c) n", p=P) for w in (ffn_w_gate, ffn_w_up)]
        w_dn_v = ffn_w_down.rearrange("l f n -> (l f) n")
        xp_v = x_prompt.rearrange("b t d -> (b t) d")
        xs_v = x_sample.rearrange("b t d -> (b t) d")
        yp_v = y_prompt.rearrange("b t d -> (b t) d")
        ys_v = y_sample.rearrange("b t d -> (b t) d")

        def raw3(n, c=KC):
            return raw[n % 2][:, :].rearrange("p (c n) -> p c n", c=c)

        block = ctx.enter_context(nc.Block())

        @block.sync
        def _(sp):
            def x_rows(i):
                return xp_v[i * P:(i + 1) * P, :] if i < NT - 1 else xs_v

            def piece(n, slot, src, dst=None, reused=True):
                if reused:
                    sp.wait_ge(w_low, n - 1)
                sp.dma_start(raw3(slot) if dst is None else dst, src).then_inc(raw_loaded[slot % 2], 16)

            def w_in_tile(col):
                return w_in_v[:, :, bass.ds(col, P)]

            sp.dma_start(x_in[:, 0, :], x_rows(0)).then_inc(x_loaded[0], 16)
            piece(0, 0, w_in_v[:, :, COL_Z:COL_Z + RANK], raw[0][:, 0:KC * RANK].rearrange("p (c n) -> p c n", c=KC),
                  reused=False)
            for i in range(1, 4):
                sp.dma_start(x_in[:, i, :], x_rows(i)).then_inc(x_loaded[i], 16)
            piece(1, 1, w_in_tile(COL_XR), reused=False)
            for i in range(4, NT):
                w = tokens(i)[1]
                sp.dma_start(x_in[0:w, i, :], x_rows(i)).then_inc(x_loaded[i], 16)
            for n in range(2, 5):
                piece(n, n, w_in_tile(COL_XR + (n - 1) * P))
            sp.wait_ge(gw_zeroed, 1)
            for c in range(4):
                for m, w in enumerate((rg_w_a, rg_w_x)):
                    for q in range(2):
                        sp.dma_start(gw4[q * 64:q * 64 + 64, c, m, q * 64:q * 64 + 64],
                                     w[0, 2 * c + q]).then_inc(gw_loaded, 16)
            for p in range(2):
                sp.dma_start(s_s[:, p, :, :], state_gla[0, :, 2 * p:2 * p + 2].rearrange("b q d v -> (q d) b v")
                             ).then_inc(gla_state_loaded, 16)
            with sp.Fori(0, 4) as i:
                for j in range(2):
                    piece(i * 2 + (N_QKV + j), N_QKV + j, w_in_tile(i * 256 + (COL_Q + j * P)))
            for j in range(4):
                piece(N_GR + j, N_GR + j, w_in_tile(COL_GR + j * P))
            for j in range(2):
                piece(N_G + j, N_G + j, w_in_tile(COL_G + j * P))
            sp.wait_ge(states_rows, 1)
            sp.dma_start(conv_p[0, 0], st_rows[0:3, :]).then_inc(states_stored, 16)
            sp.dma_start(conv_s.rearrange("l b w c -> (l b w) c"), st_rows[3:27, :]).then_inc(states_stored, 16)
            sp.dma_start(rg_p[0], st_rows[27:28, :]).then_inc(states_stored, 16)
            sp.dma_start(rg_s[0], st_rows[28:36, :]).then_inc(states_stored, 16)
            for j in range(2, 4):
                piece(N_G + j, N_G + j, w_in_tile(COL_G + j * P))
            sp.wait_ge(kv_read, STEPS + 2)
            sp.dma_start(gla_p[0, 0].rearrange("(p q) d v -> (q d) p v", q=2), s_p[:, :, :]).then_inc(states_stored, 16)
            for p in range(2):
                sp.dma_start(gla_s[0, :, 2 * p:2 * p + 2].rearrange("b q d v -> (q d) b v"),
                             s_s[:, p, :, :]).then_inc(states_stored, 16)
            for m in range(8):
                q = m % 4
                piece(N_WO + m, N_WO + m, w_out_v[:, 2 * q:2 * q + 2, (m // 4) * 512:(m // 4) * 512 + 512],
                      raw3(N_WO + m, 2))
            sp.wait_ge(y_low, NT)
            sp.wait_ge(y_low2, NT)
            for i in range(NT):
                w = tokens(i)[1]
                sp.dma_start(rows[0:w, i, :], x_rows(i)).then_inc(x_loaded[i], 16)
            for j, w in enumerate((ln1_g, ln1_b)):
                sp.dma_start(ln1[:, j, :], w[0:1, :].broadcast_to([P, D])).then_inc(ln1_loaded, 16)

            def ffn_pieces(g):
                for j in range(2):
                    for m in range(2):
                        k = 3 * j + m
                        piece(g * 6 + (N_FFN + k), N_FFN + k, w_gu_v[m][:, :, bass.ds(g * 256 + j * P, P)])
                    k = 3 * j + 2
                    piece(g * 6 + (N_FFN + k), N_FFN + k, w_dn_v[bass.ds(g * 256 + j * P, P), :],
                          raw[(N_FFN + k) % 2][:, :])

            ffn_pieces(0)
            for j, w in enumerate((ln2_g, ln2_b)):
                sp.dma_start(ln2[:, j, :], w[0:1, :].broadcast_to([P, D])).then_inc(ln2_loaded, 16)
            with sp.Fori(1, NG) as g:
                ffn_pieces(g)
            for r, i in enumerate(LN2[:-1]):
                sp.wait_ge(ln_done, NT + r + 1)
                w = tokens(i)[1]
                dst = yp_v[i * P:(i + 1) * P, :] if i < NT - 1 else ys_v
                sp.dma_start(dst, rows[0:w, i, :]).then_inc(out_stored, 16)
            i = LN2[-1]
            for half, done, count in ((0, ln_done, 2 * NT), (1, ln_done_v, 1)):
                cols = slice(half * 512, half * 512 + 512)
                sp.wait_ge(done, count)
                sp.dma_start(yp_v[i * P:(i + 1) * P, cols], rows[:, i, cols]).then_inc(out_stored, 16)
            sp.wait_ge(out_stored, 16 * (NT + 1))
            sp.wait_ge(states_stored, 16 * 7)

        @block.gpsimd
        def _(pool):
            step = Steps(pool, pool_step)
            step(pool.memset(ident[:, :], 1.0))
            step(pool.memset(wgate[:, :, :], 0.0))
            step(pool.memset(wh[0][:, :, RANK:32].bitcast(F32), 0.0))
            pool.affine_select(out=ident[:, :], in_=ident[:, :], compare_op=ALU.is_equal, fill=0.0, base=0,
                               pattern=[[-1, P]], channel_multiplier=1).then_inc(ident_made, 1)
            def low(n, slot, dst, src):
                pool.wait_ge(w_high, n + 1)
                pool.tensor_tensor(dst[0], src, dst[1].bitcast(F32), ALU.subtract).then_inc(w_low, 1)

            def ring_low(n, slot):
                low(n, slot, (wl[slot % 2][:, :, :], wh[slot % 2][:, :, :]), raw3(slot))

            pool.dma_start(par_rows[0:16, :], rg_conv_w.rearrange("l j (c p) -> (l j c) p", p=P)).then_inc(params_loaded, 16)
            for r, src in ((16, rg_conv_b), (20, rg_b_a), (24, rg_b_x), (28, rg_lambda), (32, gla_b_gate), (34, gla_norm_g)):
                n = src.shape[1] // P
                pool.dma_start(par_rows[r:r + n, :], src.rearrange("l (c p) -> (l c) p", p=P)).then_inc(params_loaded, 16)
            for r in (0, 32):
                pool.dma_start(wgate[r:r + RANK, :, :], gla_w_gate[0].rearrange("r (a n) -> r a n", a=2)
                               ).then_inc(params_loaded, 16)
            low(0, 0, (wh[0][:, :, 32:32 + RANK], wh[0][:, :, 0:RANK]),
                raw[0][:, 0:KC * RANK].rearrange("p (c n) -> p c n", c=KC))
            pool.dma_start(st_rows[0:24, :], state_conv[0].rearrange("b w c -> (b w) c")).then_inc(state_loaded, 16)
            pool.dma_start(st_rows[24:32, :], state_rglru[0]).then_inc(state_loaded, 16)
            step(pool.memset(causal[:, :], 1.0))
            step(pool.affine_select(out=causal[:, :], in_=causal[:, :], compare_op=ALU.is_ge, fill=0.0, base=0,
                                    pattern=[[1, P]], channel_multiplier=-1))
            step(pool.affine_select(out=smask[:, :].rearrange("p (b c) -> p b c", b=NB),
                                    in_=causal[0:TS, 0:TS].rearrange("p (b c) -> p b c", b=NB),
                                    compare_op=ALU.is_ge, fill=0.0, base=0,
                                    pattern=[[-LS, NB], [0, LS]], channel_multiplier=1))
            pool.tensor_tensor(fold[:, :], ident[:, 0:TS], ident[:, TS:P], ALU.add)
            step(pool.memset(bmask[:, :], 1.0))
            step(pool.affine_select(out=bmask[:, :], in_=bmask[:, :], compare_op=ALU.is_ge, fill=0.0, base=0,
                                    pattern=[[-LS, NB]], channel_multiplier=1))
            step(pool.affine_select(out=bmask[:, :], in_=bmask[:, :], compare_op=ALU.is_ge, fill=0.0, base=LS - 1,
                                    pattern=[[LS, NB]], channel_multiplier=-1))
            pool.memset(ones[:, :], 1.0 / DV)
            pool.memset(eps[:, :], RMS_EPS)
            step(pool.memset(m01[:, :], 1.0))
            pool.memset(m01[:, 0:TP:CHUNK], 0.0)
            pool.memset(m01[:, TP:T:LS], 0.0)
            step(pool.memset(res[:, :], 1.0))
            step(pool.memset(res[:, 0:1], ALPHA))
            pool.memset(dec2[:, :], 0.0).then_inc(consts_made, 1)

            with pool.Fori(0, 6) as i:
                for j in range(2):
                    ring_low(i * 2 + (N_XR + j), N_XR + j)

            def gelu_poly(m):
                w = CH[m % 3][1]
                pool.wait_ge(gx_ready, m + 1)
                if m >= 2:
                    pool.wait_ge(gelu_done, m - 1)
                a, b = gx[m % 2][:, 0:w], gt[m % 2][:, 0:w]
                step(pool.tensor_tensor(b, a, a, ALU.mult))
                step(pool.tensor_scalar(b, b, 0.044715, 1.0, ALU.mult, ALU.add))
                pool.tensor_tensor(b, b, a, ALU.mult).then_inc(poly_ready, 1)

            ring_low(N_GR, N_GR)
            for m in range(12):
                if m % 3 == 0:
                    ring_low(N_GR + m // 3 + 1, N_GR + m // 3 + 1)
                gelu_poly(m)
            for j in range(1, 4):
                ring_low(N_G + j, N_G + j)
            def wo_low(m):
                q, b = m % 4, m // 4
                low(N_WO + m, N_WO + m, (wo_l[b][:, 2 * q:2 * q + 2, :], wo_h[b][:, 2 * q:2 * q + 2, :]),
                    raw3(N_WO + m, 2))

            for m in range(WO_EARLY):
                wo_low(m)
            for i in range(NT):
                t0, w = tokens(i)
                pool.wait_ge(yr_high, i + 1)
                pool.tensor_tensor(act_l[:, 4:8, t0:t0 + w], xr[:, :, t0:t0 + w],
                                   act_h[:, 4:8, t0:t0 + w].bitcast(F32), ALU.subtract).then_inc(y_low2, 1)
            for m in range(WO_EARLY, 8):
                wo_low(m)

            def affine(r, i, ln, base, cols=slice(0, D)):
                w = tokens(i)[1]
                pool.wait_ge(ln_scaled, base + r + 1)
                pool.tensor_tensor(rows[0:w, i, cols], rows[0:w, i, cols], ln[0:w, 1, cols], ALU.add).then_inc(ln_done, 1)

            def ffn_low(g, k):
                j, m = k // 3, k % 3
                if m < 2:
                    low(g * 6 + (N_FFN + k), N_FFN + k, (gu_l[m][j][:, :, :], gu_h[m][j][:, :, :]), raw3(N_FFN + k))
                else:
                    low(g * 6 + (N_FFN + k), N_FFN + k, (wd_l[j][:, :], wd_h[j][:, :]), raw[(N_FFN + k) % 2][:, :])

            pool.wait_ge(ln1_loaded, 32)
            for i in range(NT):
                affine(i, i, ln1, 0)
                if i == 5:
                    ffn_low(0, 0)
                    ffn_low(0, 1)
                if i == NT - 2:
                    ffn_low(0, 2)
            for k in range(3, 6):
                ffn_low(0, k)

            with pool.Fori(1, NG) as g:
                for k in range(6):
                    ffn_low(g, k)
            pool.wait_ge(ln2_loaded, 32)
            for r, i in enumerate(LN2):
                affine(r, i, ln2, NT, slice(0, D) if r < NT - 1 else slice(0, 512))

        @block.scalar
        def _(act):
            step = Steps(act, act_step)

            def turn_high(n):
                i, g = n // 2, n % 2
                t0, w = tokens(i % NT)
                act.wait_ge(turned, n + 1)
                act.activation(act_h[:, 4 * g:4 * g + 4, t0:t0 + w],
                               ps[3 + n % 4][:, :].rearrange("p (c t) -> p c t", c=4)[:, :, 0:w],
                               ACT.Copy).then_inc(turned_high, 1)

            def high(n, slot, dst, src, uses):
                act.wait_ge(raw_loaded[slot % 2], uses)
                act.activation(dst, src, ACT.Copy).then_inc(w_high, 1)

            def loads(n, slot):
                return (n - slot % 2) * 8 + 16

            def ring_high(n, slot):
                act.wait_ge(in_done, n * 3 - 3)
                high(n, slot, wh[slot % 2][:, :, :], raw3(slot), loads(n, slot))

            def read(n, k, out):
                act.wait_ge(in_done, n * 3 + (k + 1))
                act.activation(out, ps[k][:, 0:CH[k][1]], ACT.Copy).then_inc(in_read, 1)

            high(0, 0, wh[0][:, :, 0:RANK], raw[0][:, 0:KC * RANK].rearrange("p (c n) -> p c n", c=KC), 16)
            for n in range(2 * NT):
                turn_high(n)
                if n == 7:
                    high(1, 1, wh[1][:, :, :], raw3(1), 16)
            for k, (c0, cn) in enumerate(CH):
                act.wait_ge(in_done, k + 1)
                act.activation(z[:, c0:c0 + cn], ps[k][0:ZP, 0:cn], ACT.Copy).then_inc(in_read, 1)
            ring_high(2, 2)
            act.wait_ge(states_read, 1)
            act.activation(e0[:, :], lam[:, :], ACT.Abs).then_inc(lam_abs, 1)
            for u in range(6):
                p, k = u // 3, u % 3
                c0, cn = CH[k]
                act.wait_ge(zg_done, u + 1)
                act.activation(cum[:, p, c0:c0 + cn], ps[3 + u % 5][:, 0:cn], ACT.Identity,
                               bias=bg[:, p:p + 1]).then_inc(zg_read, 1)
            act.wait_ge(zg_read, 6)
            step(act.activation(soft[:, :, :], cum[:, :, :], ACT.Abs))
            act.wait_ge(lam_abs, 1)
            act.activation(e0[:, :], e0[:, :], ACT.Exp, scale=-1.0).then_inc(lam_ready, 1)
            step(act.activation(soft[:, :, :], soft[:, :, :], ACT.Exp, scale=-1.0))
            act.activation(soft[:, :, :], soft[:, :, :], ACT.Ln, bias=1.0).then_inc(soft_ready, 1)
            with act.Fori(0, 2) as i:
                for j in range(2):
                    for k, (c0, cn) in enumerate(CH):
                        read(i * 2 + (N_XR + j), k, xr[:, bass.ds(i * 2 + j, 1), c0:c0 + cn])
                    ring_high(i * 2 + (N_XR + j + 2), N_XR + j + 2)

            def rg_tanh(i, k):
                c0, cn = CH[k]
                if k == 0:
                    act.wait_ge(h_ready, i + 1)
                act.wait_ge(gates_done, i * 3 + (k + 1))
                act.activation(t1[:, c0:c0 + cn], ps[3][:, 0:cn], ACT.Tanh, bias=cur[:, 0:1], scale=0.5)
                act.activation(t2[:, c0:c0 + cn], ps[4][:, 0:cn], ACT.Tanh, bias=cur[:, 1:2],
                               scale=0.5).then_inc(gates_read, 1)

            def qkv_body(i, n0, dst):
                ch = i + (n0 - N_QKV) // 2
                n = i * 2 + n0

                def tile(j, k):
                    c0, cn = CH[k]
                    read(n + j, k, dst[:, bass.ds(i * 2 + j, 1), c0:c0 + cn])

                tile(0, 0)
                rg_tanh(ch, 0)
                tile(0, 1)
                rg_tanh(ch, 1)
                tile(0, 2)
                rg_tanh(ch, 2)
                act.wait_ge(gates_read, ch * 3 + 3)
                step(act.activation(tn[:, :], t1[:, :], ACT.Tanh, bias=cur[:, 2:3], scale=cur[:, 2:3]))
                act.activation(t1[:, :], t1[:, :], ACT.Exp, bias=cur[:, 3:4],
                               scale=cur[:, 3:4]).then_inc(decay_ready, 1)
                ring_high(n + 2, n0 + 2)
                tile(1, 0)
                act.wait_ge(room_ready, ch + 1)
                act.activation(tn[:, :], tn[:, :], ACT.Sqrt, scale=-1.0).then_inc(root_ready, 1)
                tile(1, 1)
                tile(1, 2)
                ring_high(n + 3, n0 + 3)

            for n0, dst in ((N_QKV, qk), (N_QKV + 4, v)):
                with act.Fori(0, 2) as i:
                    step.enter(i, 1)
                    qkv_body(i, n0, dst)
                    step.leave(2)

            def exps(s):
                w = tokens(s)[1]
                t0 = tokens(s)[0]
                act.wait_ge(d_ready, s + 1)
                act.activation(een[:, :, 0:w], een[:, :, 0:w], ACT.Exp, scale=1 / 16)
                act.activation(enb[:, :, 0:w], cum[:, :, t0:t0 + w], ACT.Exp, scale=-1 / 16)
                act.activation(eb[:, :, 0:w], cum[:, :, t0:t0 + w], ACT.Exp, scale=1 / 16).then_inc(exp_ready, 1)

            def to_tokens(s):
                w = tokens(s)[1]
                act.wait_ge(a_done, s + 1)
                act.activation(k2t[s % 2][0:w, :], ps[4][0:w, 0:2 * P], ACT.Copy)
                act.activation(vt[s % 2][0:w, :], ps[5][0:w, :], ACT.Copy).then_inc(tok_ready, 1)

            def gelu_tanh(m):
                w = CH[m % 3][1]
                act.wait_ge(poly_ready, m + 1)
                act.activation(gt[m % 2][:, 0:w], gt[m % 2][:, 0:w], ACT.Tanh,
                               scale=0.7978845608028654).then_inc(tanh_ready, 1)

            exps(0)
            for m in range(12):
                n, k = N_GR + m // 3, m % 3
                if m + 1 <= STEPS:
                    exps(m + 1)
                if m >= 2:
                    act.wait_ge(gelu_done, m - 1)
                act.wait_ge(in_done, n * 3 + k + 1)
                act.activation(gx[m % 2][:, 0:CH[k][1]], ps[k][:, 0:CH[k][1]], ACT.Copy).then_inc(gx_ready, 1)
                if k == 2:
                    ring_high(n + 2, n + 2)
                if m <= STEPS:
                    to_tokens(m)
                if m >= 1:
                    gelu_tanh(m - 1)
                if m == STEPS + 1:
                    act.wait_ge(states_back, 1)
                    act.activation(st_rows[:, :], ps[4][0:36, :], ACT.Copy).then_inc(states_rows, 1)
                if m == STEPS + 2:
                    act.wait_ge(o_ready, STEPS + 1)
                    act.activation(sq[:, :], qk[:, 0, :], ACT.Square).then_inc(sq_ready, 1)
            gelu_tanh(11)

            def wo_high(m):
                q, b = m % 4, m // 4
                n = N_WO + m
                high(n, n, wo_h[b][:, 2 * q:2 * q + 2, :], raw3(n, 2), loads(n, n))

            for h in range(4):
                n = N_G + h
                if h:
                    act.wait_ge(o_normed, h)
                for k, (c0, cn) in enumerate(CH):
                    act.wait_ge(ms_done, 3 * h + k + 1)
                    ins = act.activation(rs[:, c0:c0 + cn], ps[3 + k][:, 0:cn], ACT.Ln, bias=eps[:, 0:1])
                step(ins)
                act.activation(rs[:, :], rs[:, :], ACT.Exp, scale=-0.5).then_inc(rs_ready, 1)
                if h < 3:
                    act.activation(sq[:, :], qk[:, h + 1, :], ACT.Square).then_inc(sq_ready, 1)
                if h == 2:
                    act.wait_ge(states_stored, 16 * 7)
                if h >= 2:
                    for m in range(2 * (h - 2), 2 * (h - 2) + 2):
                        wo_high(m)
                for k, (c0, cn) in enumerate(CH):
                    u = 3 * h + k
                    if u >= 2:
                        act.wait_ge(yg_ready, u - 1)
                    act.wait_ge(in_done, n * 3 + k + 1)
                    act.activation(sg[u % 2][:, 0:cn], ps[k][:, 0:cn], ACT.Silu).then_inc(sg_ready, 1)
                    if h == 3:
                        new = range(3 * k, 3 * k + 3)
                        for i in new:
                            t0, w = tokens(i)
                            act.activation(act_h[:, 4:8, t0:t0 + w], xr[:, :, t0:t0 + w], ACT.Copy).then_inc(yr_high, 1)
                        act.wait_ge(yg_ready, u + 1)
                        for i in new:
                            t0, w = tokens(i)
                            act.activation(act_h[:, 0:4, t0:t0 + w], qk[:, :, t0:t0 + w], ACT.Copy).then_inc(y_high, 1)
                if h < 2:
                    ring_high(n + 2, n + 2)
            for m in range(WO_EARLY, 8):
                wo_high(m)

            def ln_scale(r, i, base):
                w = tokens(i)[1]
                m = mv[r % 2]
                act.wait_ge(var_ready, base + r + 1)
                act.activation(m[0:w, 1:2], m[0:w, 1:2], ACT.Sqrt).then_inc(std_ready, 1)
                act.wait_ge(std_ready, base + r + 1)
                act.wait_ge(ln_z, base + r + 1)
                for cols in (slice(0, D),) if base + r < 2 * NT - 1 else (slice(0, 512), slice(512, D)):
                    act.activation(rows[0:w, i, cols], rows[0:w, i, cols], ACT.Copy,
                                   scale=m[0:w, 1:2]).then_inc(ln_scaled, 1)

            def ffn_high(g, k):
                j, m = k // 3, k % 3
                n = g * 6 + (N_FFN + k)
                if m < 2:
                    high(n, N_FFN + k, gu_h[m][j][:, :, :], raw3(N_FFN + k), loads(n, N_FFN + k))
                else:
                    high(n, N_FFN + k, wd_h[j][:, :], raw[(N_FFN + k) % 2][:, :], loads(n, N_FFN + k))

            act.wait_ge(op_done, NT)
            for i in range(NT):
                if i == NT - 1:
                    act.wait_ge(op_done, 2 * NT)
                    ffn_high(0, 2)
                    ffn_high(0, 3)
                ln_scale(i, i, 0)
                if i == 5:
                    ffn_high(0, 0)
                    ffn_high(0, 1)
                for n in turns_after(i):
                    turn_high(2 * NT + n)

            def silu(g, u, k):
                cn = CH[k][1]
                act.wait_ge(gate_done, g * 6 + (u + 1))
                act.activation(sl[u % 2][:, 0:cn], ps[u % 2][:, 0:cn], ACT.Silu).then_inc(silu_ready, 1)

            def hidden_high(g, u, j, k):
                c0, cn = CH[k]
                act.wait_ge(hid_ready, g * 6 + (u + 1))
                act.activation(hid[j][:, c0:c0 + cn], hf[u % 2][:, 0:cn], ACT.Copy).then_inc(hid_high, 1)

            def ffn(g, first=False, last=False):
                for u, (j, k) in enumerate(units(last)):
                    silu(g, u, k)
                    if first and u == 1:
                        turn_high(4 * NT - 2)
                        turn_high(4 * NT - 1)
                    hidden_high(g, u, j, k)
                    if first and u == 0:
                        ffn_high(0, 4)
                    if first and u == 2:
                        ffn_high(0, 5)
                    if not last and u == 3:
                        act.wait_ge(up_done, g * 6 + 3)
                        ffn_high(g + 1, 0)
                        ffn_high(g + 1, 1)
                    if last and u in LAST_NORM:
                        for i in LAST_NORM[u]:
                            ln_scale(LN2.index(i), i, NT)
                if not last:
                    act.wait_ge(down_done, g * (2 * NT) + 2 * NT)
                    ffn_high(g + 1, 2)
                    act.wait_ge(up_done, g * 6 + 6)
                    for k in range(3, 6):
                        ffn_high(g + 1, k)

            ffn(0, first=True)
            with act.Fori(1, NG - 1) as g:
                ffn(g)
            ffn(NG - 1, last=True)

        @block.vector
        def _(dve):
            step = Steps(dve, dve_step)

            def turn_low(n):
                i, g = n // 2, n % 2
                t0, w = tokens(i % NT)
                dve.wait_ge(turned_high, n + 1)
                dve.tensor_tensor(act_l[:, 4 * g:4 * g + 4, t0:t0 + w],
                                  ps[3 + n % 4][:, :].rearrange("p (c t) -> p c t", c=4)[:, :, 0:w],
                                  act_h[:, 4 * g:4 * g + 4, t0:t0 + w].bitcast(F32),
                                  ALU.subtract).then_inc(turned_low, 1)

            for n in range(2 * NT):
                turn_low(n)
            dve.memset(gw4[:, :, :, :], 0.0).then_inc(gw_zeroed, 1)
            for b in range(2):
                dve.memset(qe[b][:, :, :, :], 0.0)
                dve.memset(qi[b][:, :, :, :], 0.0)
                dve.memset(sc[b][:, :, :], 0.0)
            step(dve.memset(s_p[:, :, :], 0.0))
            dve.wait_ge(states_turned, 1)
            dve.tensor_copy(par[:, :], ps[7][:, P:P + 35])
            dve.tensor_copy(st_in[:, :, :], ps[7][:, 0:128].rearrange("p (c n) -> p c n", c=4)).then_inc(states_read, 1)
            dve.wait_ge(lam_ready, 1)
            step(dve.tensor_scalar(e1[:, :], e0[:, :], 2.0, None, ALU.add))
            step(dve.reciprocal(e1[:, :], e1[:, :]))
            step(dve.tensor_tensor(e1[:, :], e0[:, :], e1[:, :], ALU.mult))
            step(dve.tensor_tensor(e2[:, :], e1[:, :], e1[:, :], ALU.mult))
            step(dve.tensor_scalar(e3[:, :], e2[:, :], 1 / 17, None, ALU.mult))
            for q in range(15, 1, -2):
                step(dve.scalar_tensor_tensor(out=e3[:, :], in0=e3[:, :], scalar=1.0 / q, in1=e2[:, :],
                                              op0=ALU.add, op1=ALU.mult))
            step(dve.scalar_tensor_tensor(out=e3[:, :], in0=e3[:, :], scalar=1.0, in1=e1[:, :],
                                          op0=ALU.add, op1=ALU.mult))
            step(dve.tensor_scalar(e2[:, :], lam[:, :], -1.0, 0.0, ALU.mult, ALU.max))
            step(dve.scalar_tensor_tensor(out=e3[:, :], in0=e3[:, :], scalar=2.0, in1=e2[:, :],
                                          op0=ALU.mult, op1=ALU.add))
            dve.tensor_scalar(kp, e3[:, :], 2.0, None, ALU.mult)
            dve.tensor_scalar(kn, e3[:, :], -4.0, None, ALU.mult).then_inc(h_ready, 1)
            dve.tensor_scalar(hba, ba[:, :], 0.5, None, ALU.mult)
            step(dve.tensor_scalar(hbx, bx[:, :], 0.5, None, ALU.mult))
            dve.wait_ge(soft_ready, 1)
            dve.wait_ge(consts_made, 1)
            step(dve.scalar_tensor_tensor(out=cum[:, :, :], in0=cum[:, :, :], scalar=0.0, in1=soft[:, :, :],
                                          op0=ALU.min, op1=ALU.subtract))
            for p in range(2):
                ins = dve.tensor_tensor_scan(cum[:, p, :], m01[:, :], cum[:, p, :], 0.0, ALU.mult, ALU.add)
            ins.then_inc(cum_ready, 1)

            dve.wait_ge(in_read, 3 * N_QKV)
            dve.wait_ge(gw_loaded, 16 * 16)

            def sample(tile, a, b):
                return tile.rearrange("p (b t) -> p b t", b=NB)[:, :, a:b]

            def rg_conv(ch, k):
                one = bass.ds(ch, 1)
                x_t = xr[:, one, :].rearrange("p o t -> p (o t)")
                c0, c1 = CH[k][0], CH[k][0] + CH[k][1]
                if k == 0:
                    dve.tensor_copy(gw[:, :, :], gw4[:, one, :, :].rearrange("p o m n -> p (o m) n"))
                    dve.tensor_copy(cur[:, :], pk[:, one, :].rearrange("p o k -> p (o k)"))
                step(dve.tensor_scalar(xc[:, c0:c1], x_t[:, c0:c1], cw[:, 3, one], cb[:, one], ALU.mult, ALU.add))
                for d in range(1, 4):
                    tap = cw[:, 3 - d, one]
                    a, b = max(c0, d), min(c1, TP)
                    ins = dve.scalar_tensor_tensor(out=xc[:, a:b], in0=x_t[:, a - d:b - d], scalar=tap, in1=xc[:, a:b],
                                                   op0=ALU.mult, op1=ALU.add)
                    if c1 > TP:
                        s_x = x_t[:, TP:T]
                        s_c = xc[:, TP:T]
                        dve.scalar_tensor_tensor(out=sample(s_c, d, LS), in0=sample(s_x, 0, LS - d), scalar=tap,
                                                 in1=sample(s_c, d, LS), op0=ALU.mult, op1=ALU.add)
                        hist = st_in[:, one, 0:24].rearrange("p o (b w) -> p (o b) w", w=3)[:, :, 3 - d:3]
                        ins = dve.scalar_tensor_tensor(out=sample(s_c, 0, d), in0=hist, scalar=tap,
                                                       in1=sample(s_c, 0, d), op0=ALU.mult, op1=ALU.add)
                    if d < 3:
                        step(ins)
                ins.then_inc(conv_ready, 1)

            def rg_decay(ch):
                dve.wait_ge(decay_ready, ch + 1)
                step(dve.scalar_tensor_tensor(out=tn[:, :], in0=t1[:, :], scalar=1.0, in1=tn[:, :],
                                              op0=ALU.add, op1=ALU.mult))
                dve.tensor_scalar(t1[:, :], tn[:, :], -1.0, 1.0, ALU.mult, ALU.add)
                step(dve.scalar_tensor_tensor(out=tn[:, :], in0=tn[:, :], scalar=2.0, in1=tn[:, :],
                                              op0=ALU.subtract, op1=ALU.mult))
                dve.tensor_scalar(tn[:, :], tn[:, :], 0.0, None, ALU.min).then_inc(room_ready, 1)
                step(dve.scalar_tensor_tensor(out=t2[:, :], in0=t2[:, :], scalar=1.0, in1=xc[:, :],
                                              op0=ALU.add, op1=ALU.mult))

            def rg_scan(ch):
                one = bass.ds(ch, 1)
                x_t = xr[:, one, :].rearrange("p o t -> p (o t)")
                dve.tensor_copy(st_out[:, one, 0:3], xr[:, one, TP - 3:TP])
                dve.tensor_copy(st_out[:, one, 3:27].rearrange("p o (b w) -> p (o b) w", w=3),
                                sample(x_t[:, TP:T], LS - 3, LS))
                dve.wait_ge(root_ready, ch + 1)
                step(dve.scalar_tensor_tensor(out=t2[:, :], in0=t2[:, :], scalar=0.5, in1=tn[:, :],
                                              op0=ALU.mult, op1=ALU.mult))
                first_a, first_u = sample(t1[:, TP:T], 0, 1), sample(t2[:, TP:T], 0, 1)
                h0 = st_in[:, one, 24:32].rearrange("p o (b w) -> p (o b) w", w=1)
                tmp = tn[:, 0:NB].rearrange("p (b w) -> p b w", w=1)
                step(dve.tensor_tensor(tmp, first_a, h0, ALU.mult))
                dve.tensor_tensor(first_u, first_u, tmp, ALU.add)
                step(dve.memset(first_a, 0.0))
                step(dve.tensor_tensor_scan(x_t, t1[:, :], t2[:, :], 0.0, ALU.mult, ALU.add))
                dve.tensor_copy(st_out[:, one, 27:28], xr[:, one, TP - 1:TP])
                dve.tensor_copy(st_out[:, one, 28:36].rearrange("p o (b w) -> p (o b) w", w=1),
                                sample(x_t[:, TP:T], LS - 1, LS)).then_inc(h_ready, 1)

            for k in range(3):
                rg_conv(0, k)
            with dve.Fori(0, 3) as i:
                step.enter(i, 16)
                rg_decay(i)
                rg_conv(i + 1, 0)
                rg_scan(i)
                rg_conv(i + 1, 1)
                rg_conv(i + 1, 2)
                step.leave(3)
            rg_decay(3)
            rg_scan(3)

            dve.wait_ge(h_ready, 5)

            def spread(s):
                t0, w = tokens(s)
                c = CHUNK if s < STEPS else LS
                b = cum[:, :, t0:t0 + w].rearrange("p a (n c) -> p a n c", c=c)
                dve.tensor_tensor(een[:, :, 0:w].rearrange("p a (n c) -> p a n c", c=c),
                                  b[:, :, :, c - 1:c].broadcast_to([P, 2, w // c, c]), b,
                                  ALU.subtract).then_inc(d_ready, 1)

            def prep(s):
                t0, w = tokens(s)
                b = s % 2
                c = CHUNK if s < STEPS else LS
                if s >= 2:
                    dve.wait_ge(b_done, s - 1)
                dve.wait_ge(exp_ready, s + 1)
                for q in range(2):
                    r = slice(64 * q, 64 * q + 64)
                    dve.scalar_tensor_tensor(out=qe[b][r, :, q, 0:w], in0=qk[r, 0:2, t0:t0 + w], scalar=DK ** -0.5,
                                             in1=eb[r, :, 0:w], op0=ALU.mult, op1=ALU.mult)
                dve.tensor_tensor(ke[b][:, :, 0:w], qk[:, 2:4, t0:t0 + w], enb[:, :, 0:w], ALU.mult)
                dve.tensor_copy(dec[b][:, :, 0:w // c], eb[:, :, c - 1:w:c])
                if s < STEPS:
                    dve.tensor_tensor(ka[b][:, :, :], qk[:, 2:4, t0:t0 + 64], een[:, :, 0:64], ALU.mult)
                    step(dve.tensor_tensor(k2[b][:, :, 64:128], qk[:, 2:4, t0 + 64:t0 + 128], een[:, :, 64:128], ALU.mult))
                    for q in range(2):
                        r = slice(64 * q, 64 * q + 64)
                        dve.tensor_tensor(qi[b][r, :, q, :], qe[b][r, :, q, 64:128],
                                          dec[b][r, :, 0:1].broadcast_to([64, 2, 64]), ALU.mult)
                    dve.tensor_tensor(k2[b][:, :, 0:64], ka[b][:, :, :],
                                      dec[b][:, :, 1:2].broadcast_to([P, 2, 64]), ALU.mult).then_inc(prep_ready, 1)
                else:
                    dve.tensor_tensor(k2[b][:, :, 0:w], qk[:, 2:4, t0:t0 + w], een[:, :, 0:w],
                                      ALU.mult).then_inc(prep_ready, 1)

            def mask(s):
                b = s % 2
                dve.wait_ge(a_done, s + 1)
                if s < STEPS:
                    p3 = ps[3][:, :].rearrange("p (h c) -> p h c", h=4)
                    dve.tensor_tensor(sc[b][0:64, :, :], p3[0:64, :, :],
                                      causal[0:64, :].rearrange("p (o c) -> p o c", o=1).broadcast_to([64, 4, P]), ALU.mult)
                    dve.tensor_tensor(sc[b][64:128, :, 64:128], p3[64:128, :, 64:128],
                                      causal[64:128, 64:128].rearrange("p (o c) -> p o c", o=1).broadcast_to([64, 4, 64]),
                                      ALU.mult).then_inc(sc_ready, 1)
                else:
                    dve.tensor_tensor(sc[b][0:TS, :, 0:TS], ps[3][0:TS, :].rearrange("p (h c) -> p h c", h=4)[:, :, 0:TS],
                                      smask[:, :].rearrange("p (o c) -> p o c", o=1).broadcast_to([TS, 4, TS]),
                                      ALU.mult).then_inc(sc_ready, 1)

            def take(s):
                t0, w = tokens(s)
                b = s % 2
                if s < STEPS:
                    step(dve.tensor_tensor(dec2[:, :], dec[b][:, :, 0], dec[b][:, :, 1], ALU.mult))
                dve.wait_ge(b_done, s + 1)
                dve.tensor_copy(qk[:, :, t0:t0 + w], ps[6][:, :].rearrange("p (h c) -> p h c", h=4)[:, :, 0:w]
                                ).then_inc(o_ready, 1)
                if s < STEPS:
                    for p in range(2):
                        ins = dve.scalar_tensor_tensor(out=s_p[:, p, :], in0=s_p[:, p, :], scalar=dec2[:, p:p + 1],
                                                       in1=ps[7][:, p * DV:p * DV + DV], op0=ALU.mult, op1=ALU.add)
                    ins.then_inc(kv_read, 1)

            def gelu(m):
                c, (c0, cn) = m // 3, CH[m % 3]
                a, b = gx[m % 2][:, 0:cn], gt[m % 2][:, 0:cn]
                dve.wait_ge(tanh_ready, m + 1)
                step(dve.scalar_tensor_tensor(out=b, in0=b, scalar=1.0, in1=a, op0=ALU.add, op1=ALU.mult))
                dve.scalar_tensor_tensor(out=xr[:, c, c0:c0 + cn], in0=b, scalar=0.5, in1=xr[:, c, c0:c0 + cn],
                                         op0=ALU.mult, op1=ALU.mult).then_inc(gelu_done, 1)

            def spread_v(h):
                if h == 0:
                    dve.wait_ge(tok_ready, STEPS + 1)
                elif h >= 2:
                    dve.wait_ge(kv_done, h - 1)
                dve.tensor_tensor(vb[h % 2][0:TS, :, :],
                                  vt[STEPS % 2][0:TS, h * DV:(h + 1) * DV].rearrange("p (o v) -> p o v", o=1)
                                  .broadcast_to([TS, NB, DV]),
                                  bmask[:, :].rearrange("p (b o) -> p b o", o=1).broadcast_to([TS, NB, DV]),
                                  ALU.mult).then_inc(vb_ready, 1)

            def sample_state(p):
                dve.wait_ge(kv_done, 2 * p + 2)
                for e in range(NB):
                    ins = dve.scalar_tensor_tensor(
                        out=s_s[:, p, e, :], in0=s_s[:, p, e, :], scalar=dec[STEPS % 2][:, p, e:e + 1],
                        in1=ps[3 if e < 4 else 7][:, (e % 4) * DV:(e % 4 + 1) * DV], op0=ALU.mult, op1=ALU.add)
                ins.then_inc(kv_read, 1)

            spread(0)
            prep(0)
            for m in range(12):
                if m >= 2:
                    gelu(m - 2)
                if m + 1 <= STEPS:
                    if m:
                        dve.wait_ge(prep_ready, m + 1)
                    spread(m + 1)
                if m <= STEPS:
                    mask(m)
                if 1 <= m <= STEPS + 1:
                    take(m - 1)
                if m + 1 <= STEPS:
                    prep(m + 1)
                if m == STEPS:
                    spread_v(0)
                    spread_v(1)
                if m == STEPS + 1:
                    sample_state(0)
                    spread_v(2)
                    spread_v(3)
                if m == STEPS + 2:
                    sample_state(1)
            gelu(10)
            gelu(11)

            for h in range(4):
                dve.wait_ge(rs_ready, h + 1)
                dve.scalar_tensor_tensor(out=qk[:, h, :], in0=qk[:, h, :], scalar=gn[:, 0:1], in1=rs[:, :],
                                         op0=ALU.mult, op1=ALU.mult).then_inc(o_normed, 1)
                dve.wait_ge(o_normed, h + 1)
                for k, (c0, cn) in enumerate(CH):
                    u = 3 * h + k
                    dve.wait_ge(sg_ready, u + 1)
                    dve.tensor_tensor(qk[:, h, c0:c0 + cn], qk[:, h, c0:c0 + cn], sg[u % 2][:, 0:cn],
                                      ALU.mult).then_inc(yg_ready, 1)
                    if h == 3:
                        for i in range(3 * k, 3 * k + 3):
                            t0, w = tokens(i)
                            dve.wait_ge(y_high, i + 1)
                            dve.tensor_tensor(act_l[:, 0:4, t0:t0 + w], qk[:, :, t0:t0 + w],
                                              act_h[:, 0:4, t0:t0 + w].bitcast(F32), ALU.subtract).then_inc(y_low, 1)

            def out_read(i, half):
                w = tokens(i)[1]
                n = half * NT + i
                dve.wait_ge(x_loaded[i], 32)
                dve.wait_ge(op_done, n + 1)
                r = rows[0:w, i, half * 512:half * 512 + 512]
                ins = dve.scalar_tensor_tensor(out=r, in0=r, scalar=ALPHA, in1=ps[out_bank(n)][0:w, :],
                                               op0=ALU.mult, op1=ALU.add)
                ins.then_inc(op_read, 1)

            def norm(r, i, base, src, ln):
                w = tokens(i)[1]
                if base + r >= 2:
                    dve.wait_ge(ln_scaled, base + r - 1)
                st, m = stats[r % 2], mv[r % 2]
                for half in range(2):
                    ins = dve.bn_stats(st[0:w, half, :], src[half])
                step(ins)
                step(dve.bn_aggr(m[0:w, 0:2], st[0:w, :, :]))
                step(dve.tensor_scalar(m[0:w, 1:2], m[0:w, 1:2], LN_EPS, None, ALU.add))
                dve.reciprocal(m[0:w, 1:2], m[0:w, 1:2]).then_inc(var_ready, 1)
                if base == 0 or i < NT - 1:
                    pieces = [(rows[0:w, i, :], rows[0:w, i, :], ln[0:w, 0, :])]
                else:
                    pieces = [(rows[0:w, i, 512 * q:512 * q + 512], src[q], ln[0:w, 0, 512 * q:512 * q + 512])
                              for q in range(2)]
                for out, x, g in pieces:
                    ins = dve.scalar_tensor_tensor(out=out, in0=x, scalar=m[0:w, 0:1], in1=g,
                                                   op0=ALU.subtract, op1=ALU.mult)
                ins.then_inc(ln_z, 1)

            def halves(i):
                w = tokens(i)[1]
                return [rows[0:w, i, 512 * q:512 * q + 512] for q in range(2)]

            for i in range(NT):
                out_read(i, 0)
            dve.memset(rows[TS:P, NT - 1, :], 0.0)
            dve.wait_ge(ln1_loaded, 32)
            for i in range(NT):
                out_read(i, 1)
                dve.wait_ge(op_read, NT + i + 1)
                norm(i, i, 0, halves(i), ln1)
                for n in turns_after(i):
                    turn_low(2 * NT + n)
            def down_rows(g, i):
                for half in range(2):
                    n = 2 * DOWN.index(i) + half
                    dve.wait_ge(down_done, g * (2 * NT) + (n + 1))
                    r = rows[:, i, half * 512:half * 512 + 512]
                    dve.scalar_tensor_tensor(out=r, in0=r, scalar=res[:, bass.ds(g, 1)], in1=ps[4 + n % 4][:, :],
                                             op0=ALU.mult, op1=ALU.add).then_inc(down_read, 1)

            def last_norm(i):
                dve.wait_ge(down_read, (NG - 1) * (2 * NT) + 2 * DOWN.index(i) + 2)
                if i == NT - 1:
                    dve.wait_ge(fold_done, 1)
                norm(LN2.index(i), i, NT, [ps[q][0:TS, :] for q in range(2)] if i == NT - 1 else halves(i), ln2)

            def ffn(g, first=False, last=False):
                for u, (j, k) in enumerate(units(last)):
                    c0, cn = CH[k]
                    dve.wait_ge(silu_ready, g * 6 + (u + 1))
                    dve.wait_ge(up_done, g * 6 + (u + 1))
                    dve.tensor_tensor(hf[u % 2][:, 0:cn], sl[u % 2][:, 0:cn], ps[2 + u % 2][:, 0:cn],
                                      ALU.mult).then_inc(hid_ready, 1)
                    dve.wait_ge(hid_high, g * 6 + (u + 1))
                    prompt = min(cn, TP - c0)
                    ins = dve.tensor_tensor(hid[j][:, T + TS + c0:T + TS + c0 + prompt], hf[u % 2][:, 0:prompt],
                                            hid[j][:, c0:c0 + prompt].bitcast(F32), ALU.subtract)
                    if prompt < cn:
                        ins = dve.tensor_tensor(hid[j][:, T:T + TS], hf[u % 2][:, prompt:cn],
                                                hid[j][:, TP:T].bitcast(F32), ALU.subtract)
                    ins.then_inc(hid_low, 1)
                    if first and u == 0:
                        turn_low(4 * NT - 2)
                        turn_low(4 * NT - 1)
                    if last and u == 2:
                        for i in (0, 1, 2):
                            down_rows(g, i)
                            last_norm(i)
                    if last and u == 4:
                        for i in (3, 4):
                            down_rows(g, i)
                            last_norm(i)
                        down_rows(g, 5)
                    if last and u == 5:
                        last_norm(5)
                        down_rows(g, 8)
                        down_rows(g, 6)
                        last_norm(6)
                        last_norm(8)
                        down_rows(g, 7)
                        last_norm(7)
                if not last:
                    for i in DOWN:
                        down_rows(g, i)

            ffn(0, first=True)
            with dve.Fori(1, NG - 1) as g:
                ffn(g)
            dve.wait_ge(ln2_loaded, 32)
            ffn(NG - 1, last=True)
            dve.wait_ge(ln_scaled, 2 * NT + 1)
            half = rows[:, LN2[-1], 512:D]
            dve.tensor_tensor(half, half, ln2[:, 1, 512:D], ALU.add).then_inc(ln_done_v, 1)

        @block.tensor
        def _(pe):
            def turn(n, rows_t, w):
                g = n % 2
                if n >= 4:
                    pe.wait_ge(turned_low, n - 3)
                for c in range(4):
                    f = (4 * g + c) * P
                    ins = pe.transpose(ps[3 + n % 4][:, c * P:c * P + w], rows_t[0:w, f:f + P], ident[0:w, 0:w])
                ins.then_inc(turned, 1)

            def split_product(out, terms):
                last = len(terms) - 1
                for c, (sh, sl_, mh, ml) in enumerate(terms):
                    pe.matmul(out, sh, mh, start=(c == 0), stop=False)
                    pe.matmul(out, sh, ml, start=False, stop=False)
                    ins = pe.matmul(out, sl_, mh, start=False, stop=(c == last))
                return ins

            def project(n, slot, k, bank_read, count):
                c0, cn = CH[k]
                if k == 0:
                    pe.wait_ge(w_low, n + 1)
                pe.wait_ge(bank_read, count)
                split_product(ps[k][:, 0:cn],
                              [(wh[slot % 2][:, c, :], wl[slot % 2][:, c, :],
                                act_h[:, c, c0:c0 + cn], act_l[:, c, c0:c0 + cn]) for c in range(KC)]
                              ).then_inc(in_done, 1)

            pe.wait_ge(ident_made, 1)
            for i in range(NT):
                w = tokens(i)[1]
                pe.wait_ge(x_loaded[i], 16)
                for g in range(2):
                    turn(2 * i + g, x_in[:, i, :], w)
                if i in Z_AFTER:
                    k = Z_AFTER.index(i)
                    pe.wait_ge(turned_low, 2 * (3 * k + 3))
                    c0, cn = CH[k]
                    if k == 0:
                        pe.wait_ge(w_low, 1)
                    for c in range(KC):
                        pe.matmul(ps[k][0:ZP, 0:cn], wh[0][:, c, 0:ZP], act_h[:, c, c0:c0 + cn], start=(c == 0), stop=False)
                        ins = pe.matmul(ps[k][0:ZP, 0:cn], wh[0][:, c, 0:ZP], act_l[:, c, c0:c0 + cn],
                                        start=False, stop=(c == KC - 1))
                    ins.then_inc(in_done, 1)
            pe.wait_ge(state_loaded, 32)
            pe.wait_ge(params_loaded, 16 * 9)
            for c in range(4):
                pe.transpose(ps[7][:, c * 32:c * 32 + 32], st_rows[0:32, c * P:(c + 1) * P], ident[0:32, 0:32])
            ins = pe.transpose(ps[7][:, P:P + 35], par_rows[:, :], ident[0:35, 0:35])
            ins.then_inc(states_turned, 1)
            pe.wait_ge(in_read, 3)
            pe.wait_ge(states_read, 1)
            for u in range(6):
                p, k = u // 3, u % 3
                c0, cn = CH[k]
                if u == 5:
                    pe.wait_ge(zg_read, 1)
                pe.matmul(ps[3 + u % 5][:, 0:cn], wgate[:, p, :], z[:, c0:c0 + cn], start=True, stop=True
                          ).then_inc(zg_done, 1)
            with pe.Fori(0, 2) as i:
                for j in range(2):
                    for k in range(3):
                        n = i * 2 + (N_XR + j)
                        project(n, N_XR + j, k, in_read, n * 3 + (k - 2))

            pe.wait_ge(zg_read, 6)

            def gates(ch, k):
                c0, cn = CH[k]
                pe.wait_ge(conv_ready, ch * 3 + (k + 1))
                if k:
                    pe.wait_ge(gates_read, ch * 3 + k)
                pe.matmul(ps[3][:, 0:cn], gw[:, 0, :], xc[:, c0:c0 + cn], start=True, stop=True)
                pe.matmul(ps[4][:, 0:cn], gw[:, 1, :], xc[:, c0:c0 + cn], start=True, stop=True).then_inc(gates_done, 1)

            with pe.Fori(0, 4) as i:
                n = i * 2 + N_QKV
                for k in range(3):
                    project(n, N_QKV, k, in_read, n * 3 + (k - 2))
                    gates(i, k)
                for k in range(3):
                    project(n + 1, N_QKV + 1, k, in_read, n * 3 + (k + 1))

            def scores(s):
                t0, w = tokens(s)
                b = s % 2
                if s:
                    pe.wait_ge(tok_ready, s)
                for h in range(4):
                    pe.transpose(ps[5][0:w, h * DV:(h + 1) * DV], v[:, h, t0:t0 + w], ident[:, :])
                pe.wait_ge(prep_ready, s + 1)
                if s:
                    pe.wait_ge(sc_ready, s)
                p3 = ps[3][:, :].rearrange("p (h c) -> p h c", h=4)
                for p in range(2):
                    heads = slice(2 * p, 2 * p + 2)
                    if s < STEPS:
                        pe.matmul(p3[0:64, heads, 0:64], ke[b][:, p, 0:64], qe[b][:, p, :, 0:64], start=True, stop=True)
                        pe.matmul(p3[0:64, heads, 64:128], ka[b][:, p, :], qe[b][:, p, :, 64:128], start=True, stop=True)
                        pe.matmul(p3[64:128, heads, 64:128], ke[b][:, p, 64:128], qe[b][:, p, :, 64:128],
                                  start=True, stop=True)
                    else:
                        pe.matmul(p3[0:w, heads, 0:w], ke[b][:, p, 0:w], qe[b][:, p, :, 0:w], start=True, stop=True)
                for p in range(2):
                    ins = pe.transpose(ps[4][0:w, p * P:(p + 1) * P], k2[b][:, p, 0:w], ident[:, :])
                ins.then_inc(a_done, 1)

            def attend(s):
                w = tokens(s)[1]
                b = s % 2
                pe.wait_ge(sc_ready, s + 1)
                pe.wait_ge(tok_ready, s + 1)
                if s:
                    pe.wait_ge(o_ready, s)
                    pe.wait_ge(kv_read, s)
                if s == STEPS:
                    pe.wait_ge(gla_state_loaded, 32)
                for h in range(4):
                    pe.matmul(ps[6][:, h * P:h * P + w], vt[b][0:w, h * DV:(h + 1) * DV], sc[b][0:w, h, 0:w],
                              start=(h == 0), stop=False)
                o = ps[6][:, :].rearrange("p (h c) -> p h c", h=4)
                for p in range(2):
                    heads = slice(2 * p, 2 * p + 2)
                    if s < STEPS:
                        pe.matmul(o[:, heads, 0:64], s_p[:, p, :], qe[b][:, p, :, 0:64], start=False, stop=False)
                        ins = pe.matmul(o[:, heads, 64:128], s_p[:, p, :], qi[b][:, p, :, :], start=False, stop=(p == 1))
                    else:
                        for e in range(NB):
                            t = slice(e * LS, (e + 1) * LS)
                            ins = pe.matmul(o[:, heads, t], s_s[:, p, e, :], qe[b][:, p, :, t], start=False,
                                            stop=(p == 1 and e == NB - 1))
                if s < STEPS:
                    for h in range(4):
                        p, q = h // 2, h % 2
                        ins = pe.matmul(ps[7][64 * q:64 * q + 64, p * DV:(p + 1) * DV],
                                        k2t[b][:, h * DK:(h + 1) * DK], vt[b][:, h * DV:(h + 1) * DV],
                                        start=True, stop=True)
                ins.then_inc(b_done, 1)

            def sample_kv(h):
                p, q = h // 2, h % 2
                pe.wait_ge(vb_ready, h + 1)
                if h == 2:
                    pe.wait_ge(kv_read, STEPS + 1)
                for e, bank in enumerate((3, 7)):
                    ins = pe.matmul(ps[bank][64 * q:64 * q + 64, :], k2t[STEPS % 2][0:TS, h * DK:(h + 1) * DK],
                                    vb[h % 2][0:TS, 4 * e:4 * e + 4, :], start=True, stop=True)
                ins.then_inc(kv_done, 1)

            for m in range(12):
                n = N_GR + m // 3
                if m < 3:
                    project(n, n, m, in_read, n * 3 + (m - 2))
                else:
                    project(n, n, m % 3, gx_ready, m - 2)
                if m <= STEPS:
                    scores(m)
                if 1 <= m <= STEPS + 1:
                    attend(m - 1)
                if m == STEPS + 1:
                    for c in range(4):
                        ins = pe.transpose(ps[4][0:36, c * P:(c + 1) * P], st_out[:, c, :], ident[:, :])
                    ins.then_inc(states_back, 1)
                if m > STEPS and m < STEPS + 3:
                    sample_kv(2 * (m - STEPS - 1))
                    sample_kv(2 * (m - STEPS - 1) + 1)

            def mean_square(h):
                pe.wait_ge(sq_ready, h + 1)
                if h:
                    pe.wait_ge(rs_ready, h)
                for k, (c0, cn) in enumerate(CH):
                    pe.matmul(ps[3 + k][:, 0:cn], ones[:, :], sq[:, c0:c0 + cn], start=True, stop=True
                              ).then_inc(ms_done, 1)

            for h in range(4):
                for k in range(3):
                    if h == 0:
                        project(N_G, N_G, k, gx_ready, 10 + k)
                    else:
                        project(N_G + h, N_G + h, k, sg_ready, 3 * (h - 1) + k + 1)
                    if k == 0 and h == 0:
                        pe.wait_ge(states_rows, 1)
                        pe.wait_ge(kv_read, STEPS + 2)
                        mean_square(0)
                    if k == 2 and h < 3:
                        mean_square(h + 1)

            for half in range(2):
                pe.wait_ge(w_low, N_WO + 4 * half + 4)
                for i in range(NT):
                    t0, w = tokens(i)
                    n = half * NT + i
                    if n < 3:
                        pe.wait_ge(sg_ready, 10 + n)
                    if half == 0:
                        pe.wait_ge(y_low, i + 1)
                        pe.wait_ge(y_low2, i + 1)
                    if n == 8:
                        pe.wait_ge(op_read, 1)
                    elif n >= NT:
                        pe.wait_ge(op_read, NT if n < NT + 4 else n - 3)
                    split_product(ps[out_bank(n)][0:w, :],
                                  [(act_h[:, c, t0:t0 + w], act_l[:, c, t0:t0 + w], wo_h[half][:, c, :], wo_l[half][:, c, :])
                                   for c in range(KC)]).then_inc(op_done, 1)
                    if half and 2 <= i < NT - 1:
                        pe.wait_ge(ln_done, i - 1)
                        for g in range(2):
                            turn(2 * NT + 2 * (i - 2) + g, rows[:, i - 2, :], tokens(i - 2)[1])
            def down(g, i, first, hidden):
                t0 = i * P
                if i == 0:
                    pe.wait_ge(w_low, g * 6 + (N_FFN + 6))
                pe.wait_ge(hid_low, hidden)
                for half in range(2):
                    n = 2 * DOWN.index(i) + half
                    cols = slice(half * 512, half * 512 + 512)
                    if not (first and n < 4):
                        pe.wait_ge(down_read, g * (2 * NT) + (n - 3))
                    out = ps[4 + n % 4][:, :]
                    if i < NT - 1:
                        ins = split_product(out, [(hid[j][:, t0:t0 + P], hid[j][:, T + TS + t0:T + TS + t0 + P],
                                                   wd_h[j][:, cols], wd_l[j][:, cols]) for j in range(2)])
                    else:
                        for j in range(2):
                            pe.matmul(out, hid[j][:, TP:TP + P], wd_h[j][:, cols], start=(j == 0), stop=False)
                            ins = pe.matmul(out, hid[j][:, TP:TP + P], wd_l[j][:, cols], start=False, stop=(j == 1))
                    ins.then_inc(down_done, 1)

            def ffn(g, first=False, last=False):
                for u, (j, k) in enumerate(units(last)):
                    c0, cn = CH[k]
                    if first and u in (1, 2):
                        for i in ((NT - 3, NT - 2), (NT - 1,))[u - 1]:
                            pe.wait_ge(ln_done, i + 1)
                            for q in range(2):
                                turn(2 * NT + 2 * i + q, rows[:, i, :], tokens(i)[1])
                    if first and u < 3:
                        pe.wait_ge(turned_low, 2 * NT + 2 * (3 * u + 3))
                    for m, done in enumerate((gate_done, up_done)):
                        if k == 0:
                            pe.wait_ge(w_low, g * 6 + (N_FFN + 3 * j + m + 1))
                        if first and u == 0:
                            pe.wait_ge(op_read, 2 * NT - 3 + 2 * m)
                        if first and u == 1:
                            pe.wait_ge(op_read, 2 * NT - 2)
                            if m == 1:
                                pe.wait_ge(turned_low, 4 * NT - 3)
                        if not (first and u < 2):
                            pe.wait_ge(silu_ready if m == 0 else hid_ready, g * 6 + (u - 1))
                        split_product(ps[2 * m + u % 2][:, 0:cn],
                                      [(gu_h[m][j][:, c, :], gu_l[m][j][:, c, :], act_h[:, c, c0:c0 + cn],
                                        act_l[:, c, c0:c0 + cn]) for c in range(KC)]).then_inc(done, 1)
                    if last and u in LAST_DOWN:
                        for i in LAST_DOWN[u]:
                            down(g, i, False, g * 6 + 2 * (chunk_of(i) + 1))
                            if i == 6:
                                pe.wait_ge(down_read, g * (2 * NT) + 2 * DOWN.index(NT - 1) + 2)
                                pe.wait_ge(silu_ready, NG * 6)
                                for q in range(2):
                                    ins = pe.matmul(ps[q][0:TS, :], fold[:, :], rows[:, NT - 1, 512 * q:512 * q + 512],
                                                    start=True, stop=True)
                                ins.then_inc(fold_done, 1)
                if not last:
                    for i in DOWN:
                        down(g, i, first, g * 6 + (4 + chunk_of(i)))

            ffn(0, first=True)
            with pe.Fori(1, NG - 1) as g:
                ffn(g)
            ffn(NG - 1, last=True)


_INS = ["x_prompt", "x_sample", "state_gla", "state_rglru", "state_conv", "w_in", "gla_w_gate", "gla_b_gate",
        "gla_norm_g", "rg_conv_w", "rg_conv_b", "rg_w_a", "rg_b_a", "rg_w_x", "rg_b_x", "rg_lambda", "w_out",
        "ln1_g", "ln1_b", "ffn_w_gate", "ffn_w_up", "ffn_w_down", "ln2_g", "ln2_b"]
_OUTS = [(1, 1024, 1024), (8, 8, 1024), (1, 1, 4, 64, 128), (1, 1, 512), (1, 1, 3, 512),
         (1, 8, 4, 64, 128), (1, 8, 512), (1, 8, 3, 512)]


def kernel(**inputs):
    import numpy as _np
    import concourse.bacc as _bacc
    from concourse.bass_utils import run_bass_kernel_spmd as _run

    nc = _bacc.Bacc("TRN2", target_bir_lowering=False, num_devices=1)
    arrays, args = {}, []
    for name in _INS:
        a = _np.ascontiguousarray(inputs[name])
        arrays[f"in_{name}"] = a
        args.append(nc.dram_tensor(f"in_{name}", a.shape, mybir.dt.from_np(a.dtype), kind="ExternalInput").ap())
    for i, shape in enumerate(_OUTS):
        args.append(nc.dram_tensor(f"out_{i}", shape, F32, kind="ExternalOutput").ap())
    build(nc, *args)
    r = _run(nc, [arrays], core_ids=[0])
    return tuple(r.results[0][f"out_{i}"] for i in range(len(_OUTS)))
```
